# Optimizing a Trainium2 kernel written in Bass

```python
import jax, jax.numpy as jnp
from jax import lax
import numpy as np

D_MODEL = 1024
BATCH = 1
SEQ = 256
DEPTH = 1
DEC_BATCH = 1
DEC_SEQ = 256
PAST_LEN = 128

N_MOD = 6
D_SGU = D_MODEL
CHUNK = 128
SGU_HEADS = D_SGU // 128
SGU_HEAD_DIM = D_SGU // SGU_HEADS
D_POOL = D_MODEL
POOL_WINDOWS = (2, 4, 8, 16)
POOL_GROUPS = len(POOL_WINDOWS)
POOL_GROUP_DIM = D_POOL // POOL_GROUPS
N_BRANCH = 2
D_IN = 2 * D_SGU + D_POOL + N_BRANCH * D_MODEL
N_GROUPS = 4
EXPERTS_PER_GROUP = 8
N_EXPERTS = N_GROUPS * EXPERTS_PER_GROUP
TOP_K = 2
D_EXPERT = D_MODEL // 2
EXPERT_BLOCK = 128
ALPHA = (2.0 * DEPTH) ** 0.25
BETA = (8.0 * DEPTH) ** -0.25
LN_EPS = 1e-5

kernel_name = "hybrid_sgu_pool_hmoe_encoder"

def _layer_norm(x):
    xf = x.astype(jnp.float32)
    mu = jnp.mean(xf, axis=-1, keepdims=True)
    var = jnp.mean(jnp.square(xf - mu), axis=-1, keepdims=True)
    return (xf - mu) * lax.rsqrt(var + LN_EPS)

def _ln_affine(x, g, b):
    return (_layer_norm(x) * g + b).astype(x.dtype)

def _spatial_gating(u, v, w_spatial, b_spatial, sgu_g, sgu_b):
    B, S, _ = u.shape
    nc = S // CHUNK
    v = _ln_affine(v, sgu_g, sgu_b).reshape(B, nc, CHUNK, SGU_HEADS, SGU_HEAD_DIM)
    mixed = jnp.einsum("hpq,bnqhc->bnphc", w_spatial, v) + b_spatial.T[None, None, :, :, None]
    u = u.reshape(B, nc, CHUNK, SGU_HEADS, SGU_HEAD_DIM)
    return (u * mixed).reshape(B, S, D_SGU)

def _multiscale_pool(p, w_pool, pool_scale):
    B, S, _ = p.shape
    pf = p.astype(jnp.float32)
    cs = jnp.concatenate([jnp.zeros((B, 1, D_POOL), jnp.float32), jnp.cumsum(pf, axis=1)], axis=1)
    pos = jnp.arange(S, dtype=jnp.int32)
    outs = []
    for gi, w in enumerate(POOL_WINDOWS):
        sl = slice(gi * POOL_GROUP_DIM, (gi + 1) * POOL_GROUP_DIM)
        lo = jnp.maximum(pos - w // 2, 0)
        hi = jnp.minimum(pos + (w - 1 - w // 2), S - 1)
        csg = cs[:, :, sl]
        count = (hi - lo + 1).astype(jnp.float32)[None, :, None]
        mean = (jnp.take(csg, hi + 1, axis=1) - jnp.take(csg, lo, axis=1)) / count
        d = (mean - pf[:, :, sl]).astype(p.dtype)
        outs.append(d @ w_pool[gi])
    return jnp.concatenate(outs, axis=-1) * pool_scale

def _token_mixer(h, w_in, b_in, w_spatial, b_spatial, sgu_g, sgu_b, w_pool, pool_scale,
                 w_branch_a, w_branch_b, w_out):
    z = h @ w_in + b_in
    z_u, z_v, z_pool, z_gate = jnp.split(z, [D_SGU, 2 * D_SGU, 2 * D_SGU + D_POOL], axis=-1)
    a = _spatial_gating(jax.nn.gelu(z_u), jax.nn.gelu(z_v), w_spatial, b_spatial, sgu_g, sgu_b)
    p = _multiscale_pool(z_pool, w_pool, pool_scale)
    g_a, g_b = jnp.split(jax.nn.sigmoid(z_gate), N_BRANCH, axis=-1)
    merged = g_a * (a @ w_branch_a) + g_b * (p @ w_branch_b)
    return merged @ w_out

def _hier_moe(h, w_router_group, b_router_group, w_router_expert, b_router_expert,
              w_exp_gate, w_exp_up, w_exp_down):
    T, D = h.shape
    hf = h.astype(jnp.float32)
    logit_g = hf @ w_router_group.astype(jnp.float32) + b_router_group.astype(jnp.float32)
    prob_g = jax.nn.softmax(logit_g, axis=-1)
    g_sel = jnp.argmax(logit_g, axis=-1).astype(jnp.int32)
    p_sel = jnp.take_along_axis(prob_g, g_sel[:, None], axis=-1)
    logit_e = (hf @ w_router_expert.astype(jnp.float32) + b_router_expert.astype(jnp.float32))
    logit_e = logit_e.reshape(T, N_GROUPS, EXPERTS_PER_GROUP)
    logit_e = jnp.take_along_axis(logit_e, g_sel[:, None, None], axis=1)[:, 0]
    top_logit, top_idx = lax.top_k(logit_e, TOP_K)
    gate = p_sel * jax.nn.softmax(top_logit, axis=-1)
    expert_id = (g_sel[:, None] * EXPERTS_PER_GROUP + top_idx.astype(jnp.int32)).reshape(-1)
    weight = gate.reshape(-1)
    token_id = jnp.repeat(jnp.arange(T, dtype=jnp.int32), TOP_K)

    n_assign = T * TOP_K
    n_blocks = -(-n_assign // EXPERT_BLOCK) + N_EXPERTS
    n_rows = n_blocks * EXPERT_BLOCK
    order = jnp.argsort(expert_id)
    eid_sorted = expert_id[order]
    counts = jnp.zeros((N_EXPERTS,), jnp.int32).at[expert_id].add(1)
    padded = (counts + EXPERT_BLOCK - 1) // EXPERT_BLOCK * EXPERT_BLOCK
    padded_end = jnp.cumsum(padded).astype(jnp.int32)
    padded_start = padded_end - padded
    start = (jnp.cumsum(counts) - counts).astype(jnp.int32)
    dest = padded_start[eid_sorted] + (jnp.arange(n_assign, dtype=jnp.int32) - start[eid_sorted])
    row_token = jnp.full((n_rows,), T, jnp.int32).at[dest].set(token_id[order])
    row_weight = jnp.zeros((n_rows,), jnp.float32).at[dest].set(weight[order])
    block_start = jnp.arange(n_blocks, dtype=jnp.int32) * EXPERT_BLOCK
    block_expert = jnp.minimum(jnp.searchsorted(padded_end, block_start, side="right"),
                               N_EXPERTS - 1).astype(jnp.int32)
    h_pad = jnp.concatenate([h, jnp.zeros((1, D), h.dtype)], axis=0)
    xs = h_pad[row_token].reshape(n_blocks, EXPERT_BLOCK, D)

    def expert_block(args):
        xb, e = args
        return (jax.nn.silu(xb @ w_exp_gate[e]) * (xb @ w_exp_up[e])) @ w_exp_down[e]

    ys = lax.map(expert_block, (xs, block_expert)).reshape(n_rows, D)
    out = jnp.zeros((T + 1, D), h.dtype).at[row_token].add(ys * row_weight[:, None].astype(h.dtype))
    return out[:T]

def _encoder_layer(x, c, w_mod, b_mod, w_in, b_in, w_spatial, b_spatial, sgu_g, sgu_b,
                   w_pool, pool_scale, w_branch_a, w_branch_b, w_out, ln1_g, ln1_b,
                   w_router_group, b_router_group, w_router_expert, b_router_expert,
                   w_exp_gate, w_exp_up, w_exp_down, ln2_g, ln2_b):
    B, S, D = x.shape
    mod = (jax.nn.silu(c) @ w_mod + b_mod).reshape(B, N_MOD, 1, D)
    shift1, scale1, gate1 = mod[:, 0], mod[:, 1], mod[:, 2]
    shift2, scale2, gate2 = mod[:, 3], mod[:, 4], mod[:, 5]
    h = (_layer_norm(x) * (1 + scale1) + shift1).astype(x.dtype)
    t = _token_mixer(h, w_in, b_in, w_spatial, b_spatial, sgu_g, sgu_b, w_pool, pool_scale,
                     w_branch_a, w_branch_b, w_out)
    x = _ln_affine(ALPHA * x + gate1 * t, ln1_g, ln1_b)
    h = (_layer_norm(x) * (1 + scale2) + shift2).astype(x.dtype)
    f = _hier_moe(h.reshape(B * S, D), w_router_group, b_router_group, w_router_expert,
                  b_router_expert, w_exp_gate, w_exp_up, w_exp_down).reshape(B, S, D)
    x = _ln_affine(ALPHA * x + gate2 * f, ln2_g, ln2_b)
    return x

def setup_inputs(seed: int = 0) -> dict:
    key = jax.random.key(seed)
    ks = jax.random.split(key, 32)

    def nrm(k, shape, scale):
        return jax.random.normal(k, shape, jnp.float32) * scale

    L, D = DEPTH, D_MODEL
    return {
        "x_prompt": nrm(ks[0], (BATCH, SEQ, D), 1.0),
        "x_sample": nrm(ks[1], (DEC_BATCH, DEC_SEQ, D), 1.0),
        "c_prompt": nrm(ks[2], (BATCH, D), 1.0),
        "c_sample": nrm(ks[3], (DEC_BATCH, D), 1.0),
        "w_mod": nrm(ks[4], (L, D, N_MOD * D), 0.5 * D ** -0.5),
        "b_mod": nrm(ks[5], (L, N_MOD * D), 0.01),
        "w_in": nrm(ks[6], (L, D, D_IN), D ** -0.5),
        "b_in": nrm(ks[7], (L, D_IN), 0.01),
        "w_spatial": nrm(ks[8], (L, SGU_HEADS, CHUNK, CHUNK), CHUNK ** -0.5),
        "b_spatial": 1.0 + nrm(ks[9], (L, SGU_HEADS, CHUNK), 0.1),
        "sgu_g": 1.0 + nrm(ks[10], (L, D_SGU), 0.05),
        "sgu_b": nrm(ks[11], (L, D_SGU), 0.01),
        "w_pool": nrm(ks[12], (L, POOL_GROUPS, POOL_GROUP_DIM, POOL_GROUP_DIM), POOL_GROUP_DIM ** -0.5),
        "pool_scale": 1.0 + nrm(ks[13], (L, D_POOL), 0.05),
        "w_branch_a": nrm(ks[14], (L, D_SGU, D), D_SGU ** -0.5),
        "w_branch_b": nrm(ks[15], (L, D_POOL, D), D_POOL ** -0.5),
        "w_out": nrm(ks[16], (L, D, D), BETA * D ** -0.5),
        "ln1_g": 1.0 + nrm(ks[17], (L, D), 0.05),
        "ln1_b": nrm(ks[18], (L, D), 0.01),
        "w_router_group": nrm(ks[19], (L, D, N_GROUPS), D ** -0.5),
        "b_router_group": nrm(ks[20], (L, N_GROUPS), 0.01),
        "w_router_expert": nrm(ks[21], (L, D, N_EXPERTS), D ** -0.5),
        "b_router_expert": nrm(ks[22], (L, N_EXPERTS), 0.01),
        "w_exp_gate": nrm(ks[23], (L, N_EXPERTS, D, D_EXPERT), D ** -0.5),
        "w_exp_up": nrm(ks[24], (L, N_EXPERTS, D, D_EXPERT), D ** -0.5),
        "w_exp_down": nrm(ks[25], (L, N_EXPERTS, D_EXPERT, D), BETA * D_EXPERT ** -0.5),
        "ln2_g": 1.0 + nrm(ks[26], (L, D), 0.05),
        "ln2_b": nrm(ks[27], (L, D), 0.01),
    }

def reference(x_prompt, x_sample, c_prompt, c_sample, w_mod, b_mod, w_in, b_in, w_spatial,
              b_spatial, sgu_g, sgu_b, w_pool, pool_scale, w_branch_a, w_branch_b, w_out,
              ln1_g, ln1_b, w_router_group, b_router_group, w_router_expert, b_router_expert,
              w_exp_gate, w_exp_up, w_exp_down, ln2_g, ln2_b):
    layer_params = (w_mod, b_mod, w_in, b_in, w_spatial, b_spatial, sgu_g, sgu_b, w_pool,
                    pool_scale, w_branch_a, w_branch_b, w_out, ln1_g, ln1_b, w_router_group,
                    b_router_group, w_router_expert, b_router_expert, w_exp_gate, w_exp_up,
                    w_exp_down, ln2_g, ln2_b)
    y_prompt, y_sample = x_prompt, x_sample
    for l in range(DEPTH):
        p = [w[l] for w in layer_params]
        y_prompt = _encoder_layer(y_prompt, c_prompt, *p)
        y_sample = _encoder_layer(y_sample, c_sample, *p)
    return (y_prompt, y_sample)


_drawn_inputs = setup_inputs


def setup_inputs(seed=0):
    import zlib

    import numpy as np

    out = dict(_drawn_inputs(seed))
    spreads = {}
    factors = {'b_mod': 8.0,
     'b_in': 8.0,
     'b_spatial': 8.0,
     'sgu_g': 22.994,
     'sgu_b': 64.0,
     'pool_scale': 8.0,
     'ln1_b': 5.219,
     'b_router_group': 57.491,
     'b_router_expert': 51.264,
     'ln2_b': 6.241}
    for name, (base, spread) in spreads.items():
        noise = np.random.default_rng([zlib.crc32(name.encode()), seed]).standard_normal(out[name].shape)
        drawn = base * np.exp(spread * noise) if base else spread * noise
        out[name] = __import__('jax').numpy.asarray(drawn.astype(out[name].dtype))
    for name, factor in factors.items():
        out[name] = (out[name] * factor).astype(out[name].dtype)
    return out
```

```python
import concourse.bass as bass
from concourse import mybir
from contextlib import ExitStack, contextmanager

D = 1024
REQ = 2
SEQ = 256
TOK = REQ * SEQ
KC = D // 128
TILES = TOK // 128
HALF = 64
D_IN = 5 * D
NEXP = 32
NGRP = 4
EPG = NEXP // NGRP
DE = D // 2
FC = DE // 128
CAP = 64
ASSIGN = 2 * TOK
WINDOWS = (2, 4, 8, 16)
ALPHA = 2.0 ** 0.25
EPS = 1e-5
BIG = -3.0e38

C_ID, C_LT, C_ONE, C_SEL, C_EDGE, C_IOTA, C_END = 0, 128, 256, 384, 512, 576, 584

SEG_V, SEG_P, SEG_GB, SEG_WB, SEG_U, SEG_GA, SEG_WA, SEG_WO = range(8)
NBLK = 64


def hybrid_encoder(nc, x_prompt, x_sample, c_prompt, c_sample, w_mod, b_mod, w_in, b_in, w_spatial,
                   b_spatial, sgu_g, sgu_b, w_pool, pool_scale, w_branch_a, w_branch_b, w_out,
                   ln1_g, ln1_b, w_router_group, b_router_group, w_router_expert, b_router_expert,
                   w_exp_gate, w_exp_up, w_exp_down, ln2_g, ln2_b, consts, y_prompt, y_sample):
    f32, f32r, i32, u32 = mybir.dt.float32, mybir.dt.float32r, mybir.dt.int32, mybir.dt.uint32
    ALU, ACT, AX = mybir.AluOpType, mybir.ActivationFunctionType, mybir.AxisListType

    packed_x = nc.dram_tensor("packed_x", (ASSIGN + 8 * CAP, D), f32).ap()
    packed_y = nc.dram_tensor("packed_y", (ASSIGN + 8 * CAP, D), f32).ap()

    ctx = ExitStack()
    with ctx:
        base = (nc.sbuf_base + 63) // 64 * 64

        def at(name, shape, dt, off):
            return nc.alloc_sbuf_tensor_at(name, shape, dt, offset=base + off)

        def sem(name):
            return ctx.enter_context(nc.semaphore(name))

        K = 1024
        SLOT = 48 * K
        R0 = 3 * SLOT
        S0 = R0 + 16 * K
        gate_w = [at(f"gate_w{s}", [128, KC, DE], f32, s * SLOT) for s in range(3)]
        up_w = [at(f"up_w{s}", [128, KC, DE], f32, s * SLOT + 16 * K) for s in range(3)]
        down_w = [at(f"down_w{s}", [128, FC, D], f32, s * SLOT + 32 * K) for s in range(3)]
        a_hi = at("a_hi", [128, KC, TOK], f32r, 0)
        a_lo = at("a_lo", [128, KC, TOK], f32r, 16 * K)
        xin = at("xin", [128, TILES, D], f32, 0)
        ws_raw = at("ws_raw", [128, 8, 128], f32, 16 * K)
        v_nat = at("v_nat", [128, TILES, D], f32, 32 * K)
        g_a = at("g_a", [128, KC, TOK], f32, 32 * K)
        raw = at("raw", [128, 2, KC, 512], f32, SLOT)
        modraw0 = at("modraw0", [128, 4, 4, 512], f32, SLOT)
        m_b = at("m_b", [128, KC, TOK], f32, SLOT + 32 * K)
        modraw = at("modraw", [128, 2, 4, 512], f32, SLOT + 32 * K)
        h_hi = at("h_hi", [128, KC, TOK], f32r, 2 * SLOT)
        h_lo = at("h_lo", [128, KC, TOK], f32r, 2 * SLOT + 16 * K)
        w_hi = [at(f"w_hi{i}", [128, KC, 128], f32r, 2 * SLOT + 32 * K + i * 8 * K) for i in range(2)]
        w_lo = [at(f"w_lo{i}", [128, KC, 128], f32r, 2 * SLOT + 36 * K + i * 8 * K) for i in range(2)]
        ln2_bc = at("ln2_bc", [128, 2, D], f32, 2 * SLOT)
        y_first = [at(f"y_first{i}", [128, D], f32, 2 * SLOT + (8 + 4 * i) * K) for i in range(2)]
        y_second = [at(f"y_second{i}", [128, D], f32, 2 * SLOT + (16 + 4 * i) * K) for i in range(2)]
        n_t = at("n_t", [128, KC, TOK], f32, R0)
        wp_raw = at("wp_raw", [128, 4, 2, 256], f32, R0)
        bs_bc = at("bs_bc", [128, 8, 128], f32, R0 + 8 * K)
        res = at("res", [128, TILES, D], f32, R0)
        cst = at("cst", [128, C_END], f32, S0)
        pcol = at("pcol", [128, 64], f32, S0 + 2432)
        mod_t = at("mod_t", [128, 6, KC, REQ], f32, S0 + 2688)
        scale1p = at("scale1p", [128, KC, REQ], f32, S0 + 3072)
        silu_c = at("silu_c", [128, REQ, KC], f32, S0 + 3136)
        st = at("st", [128, TILES, 2, 6], f32, S0 + 3200)
        mv = at("mv", [128, TILES, 2], f32, S0 + 3392)
        rs = at("rs", [128, 8, TILES], f32, S0 + 3424)
        modrow = at("modrow", [128, 3, 512], f32, S0 + 3584)
        prow = at("prow", [64, 128], f32, S0 + 9728 + 31232)
        route_w = at("route_w", [128, 2, TILES], f32, S0 + 2432)
        pos = at("pos", [128, 2, TILES], u32, S0 + 2464)
        tab = at("tab", [1, 3, NEXP + 1], i32, S0 + 2688)
        T0 = S0 + 9728
        ws_t = at("ws_t", [128, 8, 128], f32, T0)
        wp_hi = at("wp_hi", [128, 2, 256], f32r, T0 + 4096)
        wp_lo = at("wp_lo", [128, 2, 256], f32r, T0 + 6144)
        PADW = SEQ + 16
        zpad = [at(f"zpad{i}", [128, REQ, PADW], f32, T0 + 8192 + 2176 * i) for i in range(2)]
        wsum = [at(f"wsum{i}", [128, REQ, PADW], f32, T0 + 12544 + 2176 * i) for i in range(2)]
        sgu_bc = at("sgu_bc", [128, 2, D], f32, T0 + 8192)
        d32 = [at(f"d32_{i}", [128, TOK], f32, T0 + 16896 + 2048 * i) for i in range(2)]
        d_hi = at("d_hi", [128, 2, TOK], f32r, T0 + 20992)
        d_lo = at("d_lo", [128, 2, TOK], f32r, T0 + 25088)
        g32 = [at(f"g32_{i}", [128, TOK], f32, T0 + 29184 + 2048 * i) for i in range(2)]
        ln1_bc = at("ln1_bc", [128, 2, D], f32, T0)
        h2 = at("h2", [128, TILES, D], f32, T0 + 8192)
        h2_t = at("h2_t", [128, KC, 128], f32, T0 + 24576)
        wr = at("wr", [128, KC, NGRP + NEXP], f32, T0 + 33280)
        Q0 = T0 + 34432
        br_bc = at("br_bc", [128, NGRP + NEXP], f32, Q0)
        lg = at("lg", [128, TILES, NGRP + NEXP], f32, Q0 + 160)
        onehot = at("onehot", [128, 2, TILES, NEXP], f32, Q0 + 736)
        both = at("both", [128, TILES, NEXP], f32, Q0 + 1760)
        seltmp = at("seltmp", [128, TILES, NGRP, EPG], f32, Q0 + 2272)
        q = [at(f"q{i}", [128, TILES, EPG], f32, Q0 + 2784 + 128 * i) for i in range(7)]
        q1 = at("q1", [128, 16, TILES], f32, Q0 + 3680)
        trow = at("trow", [1, 4, NEXP], f32, Q0 + 3936)
        assert Q0 + 3936 + 512 + base < nc.sbuf_usable_end
        xrows = [at(f"xrows{i}", [CAP, D], f32, T0 + 4096 * i) for i in range(3)]
        x_t = [at(f"x_t{i}", [128, KC, CAP], f32, T0 + 12288 + 2048 * i) for i in range(3)]
        sg = at("sg", [CAP, DE], f32, T0 + 18432)
        hid = at("hid", [CAP, DE], f32, T0 + 20480)
        hid_t = at("hid_t", [128, FC, CAP], f32, T0 + 22528)
        yout = at("yout", [128, 512], f32, T0 + 23552)
        xrows_x = at("xrows_x", [CAP, D], f32, T0 + 25600)
        x_t_x = at("x_t_x", [128, KC, CAP], f32, T0 + 29696)
        sg_x = at("sg_x", [CAP, DE], f32, T0 + 31744)
        hid_x = at("hid_x", [CAP, DE], f32, T0 + 33792)
        hid_t_x = at("hid_t_x", [128, FC, CAP], f32, T0 + 35840)
        yout_x = at("yout_x", [128, 512], f32, T0 + 36864)
        zrow = g32[0]

        B = [ctx.enter_context(nc.psum_tensor(f"bank{i}", [128, 512], f32)) for i in range(8)]
        Z = B[0:2]
        TR = B[2:4]
        MX = B[4:6]
        MOD = B[6]
        COL = B[7]

        ident = cst[:, C_ID:C_ID + 128]
        ones = cst[:, C_ONE:C_ONE + 128]

        s_param = sem("s_param")
        s_x = sem("s_x")
        s_ws = sem("s_ws")
        s_bmod = sem("s_bmod")
        s_m0 = [sem(f"s_m0_{i}") for i in range(4)]
        s_m = [sem(f"s_m{i}") for i in range(2)]
        s_w = [sem(f"s_w{i}") for i in range(2)]
        s_bs = sem("s_bs")
        s_wp = sem("s_wp")
        s_sgu = sem("s_sgu")
        s_xres = sem("s_xres")
        s_ln1 = sem("s_ln1")
        s_wr = sem("s_wr")
        s_ln2 = sem("s_ln2")
        s_pad = sem("s_pad")
        s_scat = sem("s_scat")
        s_out = [sem(f"s_out{i}") for i in range(2)]

        pe_pro = sem("pe_pro")
        pe_xt = sem("pe_xt")
        pe_mod = sem("pe_mod")
        pe_modcol = sem("pe_modcol")
        pe_blk = sem("pe_blk")
        pe_tr = sem("pe_tr")
        pe_pool = sem("pe_pool")
        pe_mix = sem("pe_mix")
        pe_rt = sem("pe_rt")
        pe_bc = sem("pe_bc")
        act_pro = sem("act_pro")
        act_nt = sem("act_nt")
        act_hhi = sem("act_hhi")
        act_whi = sem("act_whi")
        act_z = sem("act_z")
        act_dhi = sem("act_dhi")
        act_wphi = sem("act_wphi")
        act_pt = sem("act_pt")
        act_phi = sem("act_phi")
        act_ahi = sem("act_ahi")
        act_mhi = sem("act_mhi")
        act_sq = sem("act_sq")
        act_rt = sem("act_rt")
        dve_c = sem("dve_c")
        dve_pro = sem("dve_pro")
        dve_st = sem("dve_st")
        dve_n = sem("dve_n")
        dve_row = sem("dve_row")
        dve_col = sem("dve_col")
        dve_aff = sem("dve_aff")
        dve_hlo = sem("dve_hlo")
        dve_wlo = sem("dve_wlo")
        dve_z = sem("dve_z")
        dve_tr = sem("dve_tr")
        dve_d = sem("dve_d")
        dve_dlo = sem("dve_dlo")
        dve_wplo = sem("dve_wplo")
        dve_plo = sem("dve_plo")
        dve_vln = sem("dve_vln")
        dve_a = sem("dve_a")
        dve_alo = sem("dve_alo")
        dve_m = sem("dve_m")
        dve_mlo = sem("dve_mlo")
        dve_h2 = sem("dve_h2")
        dve_rt = sem("dve_rt")
        pool_pad = sem("pool_pad")
        pool_c = sem("pool_c")
        pool_win = sem("pool_win")
        e_gu = [sem(f"e_gu{s}") for s in range(3)]
        e_dn = [sem(f"e_dn{s}") for s in range(3)]
        e_x = [sem(f"e_x{s}") for s in range(3)]
        e_st = sem("e_st")
        x_x = sem("x_x")
        m_sem = {n: sem("e_" + n) for n in ("xtr", "xt", "gum", "silu", "hid", "htr", "ht", "ym", "yo")}
        x_sem = {n: sem("x_" + n) for n in ("xtr", "xt", "gum", "silu", "hid", "htr", "ht", "ym", "yo")}
        f_g = [sem(f"f_g{i}") for i in range(2)]
        sp_go = sem("sp_go")
        pe_go = sem("pe_go")
        pool_go = sem("pool_go")
        f_t = sem("f_t")
        f_o = sem("f_o")

        block = ctx.enter_context(nc.Block())

        class Chain:

            def __init__(self, e, s):
                self.e, self.s, self.base, self.n = e, s, 0, 0

            def did(self, ins):
                ins.then_inc(self.s, 1)
                self.n += 1

            def sync(self):
                self.e.wait_ge(self.s, self.base + self.n)

            @contextmanager
            def loop(self, trips, per):
                start = self.base + self.n
                with self.e.Fori(0, trips) as t:
                    self.base, self.n = start + t * per, 0
                    yield t
                    assert self.n == per, (self.n, per)
                self.base, self.n = start + trips * per, 0

        def win_cols(seg, unit):
            first = {SEG_U: 0, SEG_V: D, SEG_P: 2 * D, SEG_GA: 3 * D, SEG_GB: 4 * D}[seg] + 512 * unit
            return w_in[0, :, first:first + 512]

        def unit_source(u):
            seg, half = u // 2, u % 2
            if seg in (SEG_WB, SEG_WA, SEG_WO):
                w = {SEG_WB: w_branch_b, SEG_WA: w_branch_a, SEG_WO: w_out}[seg]
                src = w[0, :, 512 * half:512 * half + 512]
            else:
                src = win_cols(seg, half)
            return src.rearrange("(k p) n -> p k n", p=128)

        def mod_source(m):
            r, kc = m // KC, m % KC
            return w_mod[0, kc * 128:kc * 128 + 128, r * 2048:r * 2048 + 2048].rearrange("p (j n) -> p j n", j=4)

        def gate_src(w, e):
            return w[0, bass.ds(e, 1), :, :].rearrange("a (p k) n -> p (a k) n", p=128)

        @block.sync
        def _(sp):
            def load_unit(u):
                if u >= 2:
                    sp.wait_ge(dve_wlo, 4 * (u - 1))
                sp.dma_start(raw[:, u % 2, :, :], unit_source(u)).then_inc(s_w[u % 2], 16)

            def load_mod(m):
                if m - 10 >= 0:
                    sp.wait_ge(pe_mod, m - 1)
                sp.dma_start(modraw[:, m % 2, :, :], mod_source(m)).then_inc(s_m[m % 2], 16)

            sp.dma_start(cst[:, :], consts).then_inc(s_param, 16)
            sp.dma_start(prow[0:40, :], b_in[0, :].rearrange("(a n) -> a n", n=128)).then_inc(s_param, 16)
            sp.dma_start(prow[40:48, :], pool_scale[0, :].rearrange("(a n) -> a n", n=128)).then_inc(s_param, 16)
            sp.dma_start(prow[48:56, :], c_prompt[0, :].rearrange("(a n) -> a n", n=128)).then_inc(s_param, 16)
            sp.dma_start(prow[56:64, :], c_sample[0, :].rearrange("(a n) -> a n", n=128)).then_inc(s_param, 16)
            for r, x in enumerate((x_prompt, x_sample)):
                sp.dma_start(xin[HALF * r:HALF * r + HALF, :, :],
                             x[0, :, :].rearrange("(i p) d -> p i d", p=HALF)).then_inc(s_x, 16)
            for m in range(KC):
                if m >= 4:
                    sp.wait_ge(pe_mod, m - 3)
                sp.dma_start(modraw0[:, m % 4, :, :], mod_source(m)).then_inc(s_m0[m % 4], 16)
            sp.wait_ge(pe_mod, 6)
            load_unit(0)
            sp.wait_ge(pe_mod, 8)
            load_unit(1)
            for k in range(16):
                if k in (5, 9, 13):
                    load_unit((k - 1) // 4 + 1)
                load_mod(8 + k)
            for u in range(5, 16):
                load_unit(u)

            def load_expert(e, s):
                sp.dma_start(gate_w[s][:, :, :], gate_src(w_exp_gate, e)).then_inc(e_gu[s], 16)
                sp.dma_start(up_w[s][:, :, :], gate_src(w_exp_up, e)).then_inc(e_gu[s], 16)
                sp.dma_start(down_w[s][:, :, :], gate_src(w_exp_down, e)).then_inc(e_dn[s], 16)

            sp.wait_ge(pe_blk, 56)
            sp.wait_ge(dve_m, 8)
            load_expert(0, 0)
            sp.wait_ge(dve_wlo, NBLK)
            load_expert(1, 1)
            sp.wait_ge(pe_blk, NBLK)
            load_expert(2, 2)

            def load_rows(e, s, off):
                sp.dma_start(xrows[s][:, :], packed_x[bass.ds(off, CAP), :]).then_inc(e_x[s], 16)

            def offset(e):
                return sp.value_load(tab[0:1, 0, bass.ds(e, 1)], min_val=0, max_val=ASSIGN)

            def next_expert(e, s):
                done = sp.value_load(tab[0:1, 2, bass.ds(e - 2, 1)], min_val=0, max_val=16)
                sp.wait_ge(m_sem["ym"], e - 2)
                sp.sem_inc(sp_go, 1)
                sp.wait_ge(x_sem["ym"], done + 1)
                sp.sem_inc(sp_go, 1)
                load_expert(e, s)
                load_rows(e, s, offset(e))

            sp.wait_ge(s_scat, 16 * 8)
            sp.wait_ge(s_pad, 16)
            sp.wait_ge(dve_rt, 3)
            for e in range(3):
                load_rows(e, e, offset(e))
            with sp.Fori(0, 9) as t:
                for k in range(3):
                    next_expert(3 + 3 * t + k, k)
            next_expert(30, 0)
            next_expert(31, 1)

        @block.gpsimd
        def _(pool):
            ch = Chain(pool, pool_c)
            pool.dma_start(ws_raw[:, :, :], w_spatial[0, :, :, :].rearrange("h p q -> p h q")).then_inc(s_ws, 16)
            for j in range(4):
                for r in range(REQ):
                    pool.dma_start(modrow[32 * j + r:32 * j + r + 1, :, :],
                                   b_mod[0:1, :].rearrange("a (g j n) -> a g j n", g=3, j=4)[:, :, j, :]).then_inc(s_bmod, 16)
            pool.dma_start(wr[:, :, 0:NGRP], w_router_group[0, :, :].rearrange("(k p) n -> p k n", p=128)).then_inc(s_wr, 16)
            pool.dma_start(wr[:, :, NGRP:], w_router_expert[0, :, :].rearrange("(k p) n -> p k n", p=128)).then_inc(s_wr, 16)
            pool.dma_start(br_bc[:, 0:NGRP], b_router_group[0, :].partition_broadcast(128)).then_inc(s_wr, 16)
            pool.dma_start(br_bc[:, NGRP:], b_router_expert[0, :].partition_broadcast(128)).then_inc(s_wr, 16)
            for i in range(2):
                pool.memset(zpad[i][:, :, :], 0.0).then_inc(pool_pad, 1)
            pool.wait_ge(dve_hlo, KC)
            pool.dma_start(wp_raw[:, :, :, :], w_pool[0, :, :, :].rearrange("g (k p) n -> p g k n", p=128)).then_inc(s_wp, 16)
            pool.dma_start(bs_bc[:, :, :].rearrange("p h q -> p (h q)"),
                           b_spatial[0, :, :].rearrange("h q -> (h q)").partition_broadcast(128)).then_inc(s_bs, 16)
            pool.wait_ge(s_param, 80)
            for n in range(8):
                g = n // 2
                w = WINDOWS[g]
                pool.wait_ge(act_z, 8 + n + 1)
                if n:
                    pool.wait_ge(dve_d, n)
                src = zpad[n % 2]
                for k in range(1, g + 2):
                    length = PADW - 2 ** k + 1
                    dst = wsum[k % 2]
                    if k > 1:
                        ch.sync()
                    ch.did(pool.tensor_tensor(dst[:, :, 0:length], src[:, :, 0:length],
                                              src[:, :, 2 ** (k - 1):2 ** (k - 1) + length], ALU.add))
                    src = dst
                ch.sync()
                edges = []
                for r in range(REQ):
                    edges.append((src[:, r, 8 - w // 2:8], C_EDGE + 16 * g, w // 2))
                    if w > 2:
                        first = 8 - w // 2 + SEQ - w // 2 + 1
                        edges.append((src[:, r, first:first + w // 2 - 1], C_EDGE + 16 * g + 8, w // 2 - 1))
                for part, c, width in edges[:-1]:
                    ch.did(pool.tensor_tensor(part, part, cst[:, c:c + width], ALU.mult))
                ch.sync()
                part, c, width = edges[-1]
                pool.tensor_tensor(part, part, cst[:, c:c + width], ALU.mult).then_inc(pool_win, 1)
            pool.wait_ge(dve_d, 8)
            pool.dma_start(sgu_bc[:, 0, :], sgu_g[0, :].partition_broadcast(128)).then_inc(s_sgu, 16)
            pool.dma_start(sgu_bc[:, 1, :], sgu_b[0, :].partition_broadcast(128)).then_inc(s_sgu, 16)
            pool.wait_ge(dve_a, 8)
            for r, x in enumerate((x_prompt, x_sample)):
                pool.dma_start(res[HALF * r:HALF * r + HALF, :, :],
                               x[0, :, :].rearrange("(i p) d -> p i d", p=HALF)).then_inc(s_xres, 16)
            pool.dma_start(ln1_bc[:, 0, :], ln1_g[0, :].partition_broadcast(128)).then_inc(s_ln1, 16)
            pool.dma_start(ln1_bc[:, 1, :], ln1_b[0, :].partition_broadcast(128)).then_inc(s_ln1, 16)
            pool.wait_ge(dve_tr, 16)
            pool.memset(zrow[:, :], 0.0).then_inc(pool_pad, 1)
            pool.wait_ge(pool_pad, 3)
            pool.dma_start(packed_x[ASSIGN:ASSIGN + CAP, :].rearrange("r (h n) -> (r h) n", h=2), zrow[:, :]).then_inc(s_pad, 16)
            pool.wait_ge(dve_rt, 3)
            pool.wait_ge(dve_h2, TILES)
            for j in range(2):
                for i in range(TILES):
                    pool.indirect_dma_start(packed_x[0:ASSIGN, :], bass.IndirectOffsetOnAxis(pos[:, j, i:i + 1], 0),
                                            h2[:, i, :], None, bounds_check=ASSIGN - 1, oob_is_err=False).then_inc(s_scat, 16)

            def store(y, off, before):
                if not (isinstance(before, int) and before == 0):
                    pool.wait_ge(e_st, 32 * before)
                pool.sem_inc(pool_go, 1)
                pool.dma_start(packed_y[bass.ds(off, CAP), 0:512], y[0:64, :]).then_inc(e_st, 16)
                pool.dma_start(packed_y[bass.ds(off, CAP), 512:1024], y[64:128, :]).then_inc(e_st, 16)

            def expert(e):
                off = pool.value_load(tab[0:1, 0, bass.ds(e, 1)], min_val=0, max_val=ASSIGN)
                more = pool.value_load(tab[0:1, 1, bass.ds(e, 1)], min_val=0, max_val=7)
                first = 0 if isinstance(e, int) else pool.value_load(tab[0:1, 2, bass.ds(e, 1)], min_val=0, max_val=16)
                pool.wait_ge(m_sem["yo"], e + 2)
                store(yout, off, e + first)
                with pool.If(more > 0):
                    with pool.Fori(0, more) as r:
                        here = pool.snap(off + (r + 1) * CAP)
                        pool.wait_ge(x_sem["xtr"], first + r + 1)
                        pool.sem_inc(pool_go, 1)
                        pool.dma_start(xrows_x[:, :], packed_x[bass.ds(here, CAP), :]).then_inc(x_x, 16)
                        pool.wait_ge(x_sem["yo"], first + r + 2)
                        store(yout_x, here, e + 1 + first + r)

            expert(0)
            with pool.Fori(1, NEXP) as e:
                expert(e)
            pool.wait_ge(m_sem["ym"], 30)
            allx = pool.value_load(tab[0:1, 2, NEXP:NEXP + 1], min_val=0, max_val=16)
            pool.wait_ge(x_sem["ym"], allx + 1)
            pool.sem_inc(pool_go, 1)
            pool.dma_start(ln2_bc[:, 0, :], ln2_g[0, :].partition_broadcast(128)).then_inc(s_ln2, 16)
            pool.dma_start(ln2_bc[:, 1, :], ln2_b[0, :].partition_broadcast(128)).then_inc(s_ln2, 16)
            pool.wait_ge(e_st, 32 * (allx + NEXP))
            pool.sem_inc(pool_go, 1)
            for i in range(TILES):
                if i >= 2:
                    pool.wait_ge(f_o, i - 1)
                    pool.wait_ge(s_out[i % 2], 32 * (i // 2))
                for j, y in enumerate((y_first, y_second)):
                    pool.indirect_dma_start(y[i % 2][:, :], None, packed_y[0:ASSIGN, :],
                                            bass.IndirectOffsetOnAxis(pos[:, j, i:i + 1], 0),
                                            bounds_check=ASSIGN - 1, oob_is_err=False).then_inc(f_g[i % 2], 16)

        @block.tensor
        def _(pe):
            def mm(out, lhsT, rhs, start=True, stop=True):
                return pe.matmul(out, lhsT, rhs, start=start, stop=stop, skip_group_check=True)

            pe.wait_ge(s_param, 80)
            pe.transpose(COL[:, 0:64], prow[0:64, :], ident[0:64, 0:64]).then_inc(pe_pro, 1)
            pe.wait_ge(s_ws, 16)
            for hb in range(8):
                x = pe.transpose(MX[hb // 4][:, 128 * (hb % 4):128 * (hb % 4) + 128], ws_raw[:, hb, :], ident)
            x.then_inc(pe_pro, 1)
            for i in range(TILES):
                pe.wait_ge(dve_n, i + 1)
                if i >= 2:
                    pe.wait_ge(act_nt, 2 * (i - 1))
                for kc in range(KC):
                    bank = B[2 * (i % 2) + kc // 4]
                    x = pe.transpose(bank[:, 128 * (kc % 4):128 * (kc % 4) + 128], xin[:, i, 128 * kc:128 * kc + 128], ident)
                x.then_inc(pe_xt, 1)

            def mod_unit(src, kc):
                for j in range(4):
                    x = mm(MOD[32 * j:32 * j + 2, :], silu_c[:, :, kc], src[:, j, :], start=(kc == 0), stop=(kc == KC - 1))
                x.then_inc(pe_mod, 1)

            def mod_cols(g):
                pe.wait_ge(dve_row, g + 1)
                for j in range(4):
                    for k in range(4):
                        c = 4 * j + k
                        x = mm(COL[:, 2 * c:2 * c + 2], modrow[32 * j:32 * j + 2, g, 128 * k:128 * k + 128],
                               ident[32 * j:32 * j + 2, 32 * j:32 * j + 2])
                    x.then_inc(pe_modcol, 1)
                    pe.wait_ge(pe_modcol, 4 * g + j + 1)

            pe.wait_ge(act_pro, 1)
            for m in range(KC):
                pe.wait_ge(s_m0[m % 4], 16 * (m // 4 + 1))
                mod_unit(modraw0[:, m % 4, :, :], m)
            mod_cols(0)

            def blk(b, mov_hi, mov_lo):
                i = b % 2 if isinstance(b, int) else blk.parity
                for kc in range(KC):
                    mm(Z[i][:, :], w_hi[i][:, kc, :], mov_lo[:, kc, :], start=(kc == 0), stop=False)
                    mm(Z[i][:, :], w_hi[i][:, kc, :], mov_hi[:, kc, :], start=False, stop=False)
                for kc in range(KC):
                    x = mm(Z[i][:, :], w_lo[i][:, kc, :], mov_hi[:, kc, :], start=False, stop=(kc == KC - 1))
                x.then_inc(pe_blk, 1)

            def block_at(b, par, mov_hi, mov_lo, freed, count):
                pe.wait_ge(act_whi, b + 1)
                pe.wait_ge(dve_wlo, b + 1)
                if freed is not None:
                    pe.wait_ge(freed, count)
                blk.parity = par
                blk(None, mov_hi, mov_lo)

            pe.wait_ge(act_hhi, KC)
            pe.wait_ge(dve_hlo, KC)
            pe.wait_ge(dve_pro, 2)

            def v_pair(t, first):
                for k in range(2):
                    if first:
                        block_at(k, k, h_hi, h_lo, None, None)
                    else:
                        block_at(2 * t + k, k, h_hi, h_lo, act_z, 2 * t + k - 1)
                    pe.wait_ge(s_m[k], 16 * (t + 1))
                    mod_kc = 2 * t + k
                    yield_mod(mod_kc, k, t)
                for k in range(2):
                    pe.wait_ge(act_z, 2 * t + k + 1)
                    if not first:
                        pe.wait_ge(dve_tr, 2 * t + k - 1)
                    for c in range(TILES):
                        x = pe.transpose(TR[k][:, 128 * c:128 * c + 128], g32[k][:, 128 * c:128 * c + 128], ident)
                    x.then_inc(pe_tr, 1)

            def yield_mod(kc, k, t):
                mod_unit(modraw[:, k, :, :], kc)

            for t in range(4):
                v_pair(t, t == 0)
            def pooled(g):
                pe.wait_ge(act_dhi, 2 * g + 2)
                pe.wait_ge(dve_dlo, 2 * g + 2)
                pe.wait_ge(act_wphi, g + 1)
                pe.wait_ge(dve_wplo, g + 1)
                if g:
                    pe.wait_ge(act_pt, 2 * g)
                for o in range(2):
                    cols = slice(128 * o, 128 * o + 128)
                    for kc in range(2):
                        mm(MX[o][:, :], wp_hi[:, kc, cols], d_lo[:, kc, :], start=(kc == 0), stop=False)
                        mm(MX[o][:, :], wp_hi[:, kc, cols], d_hi[:, kc, :], start=False, stop=False)
                        x = mm(MX[o][:, :], wp_lo[:, kc, cols], d_hi[:, kc, :], start=False, stop=(kc == 1))
                    x.then_inc(pe_pool, 1)

            for n in range(8):
                b = 8 + n
                block_at(b, n % 2, h_hi, h_lo, act_z, b - 1)
                if n >= 2 and n % 2 == 0:
                    pooled(n // 2 - 1)
                pe.wait_ge(s_m[n % 2], 16 * (5 + n // 2))
                if n == 0:
                    pe.wait_ge(dve_row, 2)
                mod_unit(modraw[:, n % 2, :, :], n)
            mod_cols(1)
            with pe.Fori(0, 4) as t:
                for k in range(2):
                    block_at(16 + 2 * t + k, k, h_hi, h_lo, act_z, 16 + 2 * t + k - 1)
            pooled(3)
            pe.wait_ge(act_phi, 8)
            pe.wait_ge(dve_plo, 8)
            for k in range(2):
                block_at(24 + k, k, a_hi, a_lo, act_z, 23 + k)
            with pe.Fori(0, 3) as t:
                for k in range(2):
                    block_at(26 + 2 * t + k, k, a_hi, a_lo, dve_z, 2 * t + k + 1)
            pe.wait_ge(dve_vln, TILES)
            for n in range(8):
                b = 32 + n
                block_at(b, n % 2, h_hi, h_lo, dve_z if n < 2 else act_z, 7 + n if n < 2 else 24 + n - 1)
                if n >= 2:
                    pe.wait_ge(dve_a, n - 1)
                for c in range(TILES):
                    x = mm(MX[n % 2][:, 128 * c:128 * c + 128], v_nat[:, c, 128 * n:128 * n + 128], ws_t[:, n, :])
                x.then_inc(pe_mix, 1)
            with pe.Fori(0, 4) as t:
                for k in range(2):
                    block_at(40 + 2 * t + k, k, h_hi, h_lo, act_z, 31 + 2 * t + k)
            pe.wait_ge(act_ahi, 8)
            pe.wait_ge(dve_alo, 8)
            for k in range(2):
                block_at(48 + k, k, a_hi, a_lo, act_z, 39 + k)
            with pe.Fori(0, 3) as t:
                for k in range(2):
                    block_at(50 + 2 * t + k, k, a_hi, a_lo, dve_z, 8 + 2 * t + k + 1)
            pe.wait_ge(act_mhi, 8)
            pe.wait_ge(dve_mlo, 8)

            def o_pair(t, first):
                for k in range(2):
                    if first:
                        block_at(56 + k, k, h_hi, h_lo, dve_z, 15 + k)
                    else:
                        block_at(56 + 2 * t + k, k, h_hi, h_lo, act_z, 40 + 2 * t + k - 1)
                for k in range(2):
                    pe.wait_ge(act_z, 40 + 2 * t + k + 1)
                    pe.wait_ge(dve_tr, 8 + 2 * t + k - 1)
                    for c in range(TILES):
                        x = pe.transpose(TR[k][:, 128 * c:128 * c + 128], g32[k][:, 128 * c:128 * c + 128], ident)
                    x.then_inc(pe_tr, 1)

            o_pair(0, True)
            with pe.Fori(1, 4) as t:
                o_pair(t, False)

            def broadcast(vec, banks):
                for c in range(2):
                    ch_id = 2 * vec + c
                    g, j = ch_id // 4, ch_id % 4
                    x = mm(banks[c][:, :], cst[32 * j:32 * j + 2, C_SEL:C_SEL + 128], modrow[32 * j:32 * j + 2, g, :])
                x.then_inc(pe_bc, 1)

            pe.wait_ge(dve_row, 3)
            pe.wait_ge(dve_col, 2)
            broadcast(4, (B[4], B[5]))
            broadcast(3, (B[6], B[7]))
            pe.wait_ge(s_wr, 64)
            for i in range(TILES):
                pe.wait_ge(dve_h2, i + 1)
                pe.wait_ge(dve_tr, 16)
                if i:
                    pe.wait_ge(act_rt, 2 * i)
                for kc in range(KC):
                    x = pe.transpose(TR[kc // 4][:, 128 * (kc % 4):128 * (kc % 4) + 128], h2[:, i, 128 * kc:128 * kc + 128], ident)
                x.then_inc(pe_rt, 1)
                pe.wait_ge(act_rt, 2 * (i + 1))
                for kc in range(KC):
                    x = mm(B[0][:, 64 * i:64 * i + NGRP + NEXP], h2_t[:, kc, :], wr[:, kc, :], start=(kc == 0), stop=(kc == KC - 1))
                x.then_inc(pe_rt, 1)
            pe.wait_ge(dve_rt, 1)
            for i in range(TILES):
                for k in range(i + 1):
                    mm(B[1][:, NEXP * i:NEXP * i + NEXP], cst[:, C_LT:C_LT + 128] if k == i else ones, both[:, k, :],
                       start=(k == 0), stop=(k == i))
            for k in range(TILES):
                x = mm(B[1][:, NEXP * TILES:NEXP * TILES + NEXP], ones, both[:, k, :], start=(k == 0), stop=(k == TILES - 1))
            x.then_inc(pe_rt, 1)

            def x_transposes(rows, bank, s):
                pe.sem_inc(pe_go, 1)
                view = rows[:, :].rearrange("c (p k) -> c k p", k=KC)
                for kc in range(KC):
                    x = pe.transpose(bank[:, CAP * kc:CAP * kc + CAP], view[:, kc, :], ident[0:CAP, 0:CAP])
                x.then_inc(s["xtr"], 1)

            def gate_up(xt, s, bank, sm):
                for kc in range(KC):
                    mm(bank[0:CAP, :], xt[:, kc, :], gate_w[s][:, kc, :], start=(kc == 0), stop=(kc == KC - 1))
                    x = mm(bank[CAP:128, :], xt[:, kc, :], up_w[s][:, kc, :], start=(kc == 0), stop=(kc == KC - 1))
                x.then_inc(sm["gum"], 1)

            def h_transposes(hd, bank, sm):
                pe.sem_inc(pe_go, 1)
                view = hd[:, :].rearrange("c (p f) -> c f p", f=FC)
                for fc in range(FC):
                    x = pe.transpose(bank[:, CAP * fc:CAP * fc + CAP], view[:, fc, :], ident[0:CAP, 0:CAP])
                x.then_inc(sm["htr"], 1)

            def down(ht, s, bank, sm):
                for fc in range(FC):
                    mm(bank[0:CAP, :], ht[:, fc, :], down_w[s][:, fc, 0:512], start=(fc == 0), stop=(fc == FC - 1))
                    x = mm(bank[CAP:128, :], ht[:, fc, :], down_w[s][:, fc, 512:1024], start=(fc == 0), stop=(fc == FC - 1))
                x.then_inc(sm["ym"], 1)

            def expert(e, s, turn, last=False):
                pe.wait_ge(e_gu[s], 32 * (turn + 1))
                pe.wait_ge(m_sem["xt"], e + 1)
                gate_up(x_t[s], s, B[0], m_sem)
                if not last:
                    n = (s + 1) % 3
                    pe.wait_ge(e_x[n], 16 * (turn + 1 + (1 if n == 0 else 0)))
                    x_transposes(xrows[n], B[2], m_sem)
                pe.wait_ge(m_sem["hid"], e + 1)
                h_transposes(hid, B[3], m_sem)
                pe.wait_ge(m_sem["ht"], e + 1)
                pe.wait_ge(e_dn[s], 16 * (turn + 1))
                pe.wait_ge(m_sem["yo"], e + 1)
                down(hid_t, s, B[1], m_sem)
                more = pe.value_load(tab[0:1, 1, bass.ds(e, 1)], min_val=0, max_val=7)
                first = pe.value_load(tab[0:1, 2, bass.ds(e, 1)], min_val=0, max_val=16)
                with pe.If(more > 0):
                    with pe.Fori(0, more) as r:
                        turns = pe.snap(first + r)
                        pe.wait_ge(x_x, 16 * (turns + 1))
                        pe.wait_ge(x_sem["yo"], turns + 1)
                        x_transposes(xrows_x, B[6], x_sem)
                        pe.wait_ge(x_sem["xt"], turns + 1)
                        gate_up(x_t_x, s, B[4], x_sem)
                        pe.wait_ge(x_sem["hid"], turns + 1)
                        h_transposes(hid_x, B[7], x_sem)
                        pe.wait_ge(x_sem["ht"], turns + 1)
                        down(hid_t_x, s, B[5], x_sem)

            pe.sem_inc(x_sem["xtr"], 1)
            pe.sem_inc(x_sem["ym"], 1)
            pe.wait_ge(dve_rt, 3)
            pe.wait_ge(e_x[0], 16)
            x_transposes(xrows[0], B[2], m_sem)
            with pe.Fori(0, 10) as t:
                for k in range(3):
                    expert(3 * t + k, k, t)
            expert(30, 0, 10)
            expert(31, 1, 10, last=True)
            broadcast(5, (B[0], B[2]))

        @block.scalar
        def _(act):
            def copy(out, in_, scale=1.0):
                return act.activation(out, in_, ACT.Copy, scale=scale)

            def split_hi(b, par, slot, turn, col, wait_free=True):
                act.wait_ge(s_w[slot], 16 * (turn + 1))
                if wait_free:
                    act.wait_ge(pe_blk, b - 1)
                copy(w_hi[par][:, :, :], raw[:, slot, :, bass.ds(col, 128)]).then_inc(act_whi, 1)

            act.wait_ge(dve_pro, 1)
            act.activation(silu_c[:, :, :].rearrange("p r k -> p (r k)"), COL[:, 48:64], ACT.Silu).then_inc(act_pro, 1)
            act.wait_ge(dve_st, 1)
            act.activation(rs[:, 1, :], rs[:, 0, :], ACT.Sqrt).then_inc(act_sq, 1)
            n_view = n_t[:, :, :].rearrange("p k (r i n) -> p k r i n", r=REQ, i=TILES)
            for i in range(TILES):
                act.wait_ge(pe_xt, i + 1)
                for hb in range(2):
                    src = B[2 * (i % 2) + hb][:, :].rearrange("p (k r n) -> p k r n", k=4, r=REQ)
                    copy(n_view[:, 4 * hb:4 * hb + 4, :, i, :], src).then_inc(act_nt, 1)
            split_hi(0, 0, 0, 0, 0, wait_free=False)
            for kc in range(KC):
                act.wait_ge(dve_aff, kc + 1)
                copy(h_hi[:, kc, :], n_t[:, kc, :]).then_inc(act_hhi, 1)

            def run(seg, n, evac, last=False):
                b = 8 * seg + n
                nb = b + 1
                if nb < NBLK:
                    u = nb // 4
                    split_hi(nb, nb % 2, u % 2, u // 2, 128 * (nb % 4), wait_free=nb >= 2)
                if evac:
                    evac(n, n % 2, b)

            def ev_v(n, i, b):
                act.wait_ge(pe_blk, b + 1)
                if b >= 2:
                    act.wait_ge(pe_tr, b - 1)
                act.activation(g32[i][:, :], Z[i][:, :], ACT.Gelu_apprx_tanh, bias=pcol[:, 8 + n:9 + n]).then_inc(act_z, 1)

            for n in range(8):
                run(SEG_V, n, ev_v)

            def d_high(n):
                act.wait_ge(dve_d, n + 1)
                if n >= 2:
                    act.wait_ge(pe_pool, 2 * (n // 2))
                copy(d_hi[:, n % 2, :], d32[n % 2][:, :]).then_inc(act_dhi, 1)

            def pool_w_high(g):
                act.wait_ge(s_wp, 16)
                if g:
                    act.wait_ge(pe_pool, 2 * g)
                copy(wp_hi[:, :, :], wp_raw[:, g, :, :]).then_inc(act_wphi, 1)

            def pool_evac(g):
                for o in range(2):
                    act.wait_ge(pe_pool, 2 * g + o + 1)
                    if g or o:
                        act.wait_ge(dve_plo, 2 * g + o)
                    act.activation(g32[0][:, :], MX[o][:, :], ACT.Copy,
                                   scale=pcol[:, 40 + 2 * g + o:41 + 2 * g + o]).then_inc(act_pt, 1)
                    act.wait_ge(act_pt, 2 * g + o + 1)
                    copy(a_hi[:, 2 * g + o, :], g32[0][:, :]).then_inc(act_phi, 1)

            def ev_p(n, i, b):
                if n:
                    d_high(n - 1)
                if n % 2 == 1:
                    if n >= 3:
                        pool_evac(n // 2 - 1)
                    pool_w_high(n // 2)
                act.wait_ge(pe_blk, b + 1)
                if n >= 2:
                    act.wait_ge(dve_d, n - 1)
                else:
                    act.wait_ge(pool_pad, 2)
                act.activation(zpad[i][:, :, 8:8 + SEQ], Z[i][:, :].rearrange("p (r s) -> p r s", r=REQ),
                               ACT.Identity, bias=pcol[:, 16 + n:17 + n]).then_inc(act_z, 1)

            for n in range(8):
                if n == 1:
                    act.wait_ge(dve_tr, 8)
                run(SEG_P, n, ev_p)

            def sigmoid(dst, col):
                def ev(n, i, b):
                    act.wait_ge(pe_blk, b + 1)
                    act.activation(dst[:, n, :], Z[i][:, :], ACT.Sigmoid, bias=pcol[:, col + n:col + n + 1]).then_inc(act_z, 1)
                return ev

            ev_gb = sigmoid(m_b, 32)
            for n in range(8):
                if n == 0:
                    act.wait_ge(pe_mod, 24)
                run(SEG_GB, n, ev_gb)
                if n == 0:
                    d_high(7)
                    act.wait_ge(dve_st, 2)
                    act.activation(rs[:, 1, :], rs[:, 0, :], ACT.Sqrt).then_inc(act_sq, 1)
            pool_evac(3)
            for n in range(8):
                run(SEG_WB, n, None)

            def a_high(n):
                act.wait_ge(dve_a, n + 1)
                copy(a_hi[:, n, :], d32[n % 2][:, :]).then_inc(act_ahi, 1)

            def ev_u(n, i, b):
                if n:
                    if n == 1:
                        act.wait_ge(pe_blk, 32)
                    a_high(n - 1)
                act.wait_ge(pe_blk, b + 1)
                if n >= 2:
                    act.wait_ge(dve_a, n - 1)
                act.activation(g32[i][:, :], Z[i][:, :], ACT.Gelu_apprx_tanh, bias=pcol[:, n:n + 1]).then_inc(act_z, 1)

            for n in range(8):
                run(SEG_U, n, ev_u)

            ev_ga = sigmoid(g_a, 24)
            for n in range(8):
                run(SEG_GA, n, ev_ga)
                if n == 0:
                    a_high(7)

            for n in range(8):
                run(SEG_WA, n, None)
                act.wait_ge(dve_m, n + 1)
                copy(h_hi[:, n, :], d32[n % 2][:, :]).then_inc(act_mhi, 1)

            def ev_o(n, i, b):
                act.wait_ge(pe_blk, b + 1)
                act.wait_ge(pe_tr, 8 + n - 1)
                for r in range(REQ):
                    x = act.activation(g32[i][:, :].rearrange("p (i r n) -> p i r n", i=TILES, r=REQ)[:, :, r, :],
                                       Z[i][:, SEQ * r:SEQ * r + SEQ].rearrange("p (i n) -> p i n", i=TILES), ACT.Copy,
                                       scale=mod_t[:, 2, n, r:r + 1])
                x.then_inc(act_z, 1)

            act.wait_ge(dve_col, 2)
            for n in range(8):
                run(SEG_WO, n, ev_o)
            for i in range(TILES):
                for k in range(2):
                    act.wait_ge(dve_st, 3 + 2 * i + k)
                    act.activation(rs[:, 1, 0:1], rs[:, 0, 0:1], ACT.Sqrt).then_inc(act_sq, 1)
                act.wait_ge(pe_rt, 2 * i + 1)
                for hb in range(2):
                    copy(h2_t[:, 4 * hb:4 * hb + 4, :], TR[hb][:, :].rearrange("p (k n) -> p k n", k=4)).then_inc(act_rt, 1)
            act.wait_ge(dve_st, 11)
            act.activation(q1[:, 2:6, :].rearrange("p k i -> p (k i)"), q1[:, 6:10, :].rearrange("p k i -> p (k i)"), ACT.Exp).then_inc(act_rt, 1)
            act.wait_ge(dve_st, 12)
            act.activation(q1[:, 12, :], q1[:, 11, :], ACT.Exp).then_inc(act_rt, 1)

            def round_(sm, banks, sgb, ht, y, n, before, yms):
                act.wait_ge(sm["gum"], n + 1)
                act.activation(sgb[:, :], banks[0][0:CAP, :], ACT.Silu).then_inc(sm["silu"], 1)
                act.wait_ge(sm["htr"], n + 1)
                copy(ht[:, :, :].rearrange("p f c -> p (f c)"), banks[2][:, 0:FC * CAP]).then_inc(sm["ht"], 1)
                act.wait_ge(sm["ym"], yms)
                if not (isinstance(before, int) and before == 0):
                    act.wait_ge(e_st, 32 * before)
                copy(y[:, :], banks[1][:, :]).then_inc(sm["yo"], 1)

            act.sem_inc(m_sem["yo"], 1)
            act.sem_inc(x_sem["yo"], 1)
            act.wait_ge(dve_rt, 3)

            def expert(e):
                more = act.value_load(tab[0:1, 1, bass.ds(e, 1)], min_val=0, max_val=7)
                first = 0 if isinstance(e, int) else act.value_load(tab[0:1, 2, bass.ds(e, 1)], min_val=0, max_val=16)
                round_(m_sem, (B[0], B[1], B[3]), sg, hid_t, yout, e, e + first, e + 1)
                with act.If(more > 0):
                    with act.Fori(0, more) as r:
                        turns = act.snap(first + r)
                        round_(x_sem, (B[4], B[5], B[7]), sg_x, hid_t_x, yout_x, turns, e + 1 + turns, turns + 2)

            expert(0)
            with act.Fori(1, NEXP) as e:
                expert(e)
            for i in range(TILES):
                act.wait_ge(f_g[i % 2], 32 * (i // 2 + 1))
                copy(y_second[i % 2][:, :], y_second[i % 2][:, :], scale=route_w[:, 1, i:i + 1]).then_inc(f_t, 1)
                act.wait_ge(dve_st, 13 + i)
                act.activation(rs[:, 1, 0:1], rs[:, 0, 0:1], ACT.Sqrt).then_inc(act_sq, 1)
                act.wait_ge(f_o, i + 1)
                for r, y in enumerate((y_prompt, y_sample)):
                    act.dma_start(y[0, HALF * i:HALF * i + HALF, :], y_first[i % 2][HALF * r:HALF * r + HALF, :]).then_inc(s_out[i % 2], 16)
            for i in range(2):
                act.wait_ge(s_out[i], 32 * TILES // 2)

        @block.vector
        def _(dve):
            ch = Chain(dve, dve_c)

            def link(ins):
                ch.did(ins)
                ch.sync()

            sq = [0]
            sts = [0]

            def rstd(w, eps_var):
                ch.sync()
                dve.tensor_scalar(rs[:, 0, 0:w], eps_var, EPS, None, ALU.add).then_inc(dve_st, 1)
                sts[0] += 1
                sq[0] += 1
                dve.wait_ge(act_sq, sq[0])
                link(dve.reciprocal(rs[:, 2, 0:w], rs[:, 1, 0:w]))
                link(dve.tensor_tensor(rs[:, 3, 0:w], rs[:, 2, 0:w], rs[:, 2, 0:w], ALU.mult))
                link(dve.tensor_tensor(rs[:, 3, 0:w], rs[:, 3, 0:w], rs[:, 0, 0:w], ALU.mult))
                link(dve.tensor_scalar(rs[:, 3, 0:w], rs[:, 3, 0:w], -0.5, 1.5, ALU.mult, ALU.add))
                link(dve.tensor_tensor(rs[:, 2, 0:w], rs[:, 2, 0:w], rs[:, 3, 0:w], ALU.mult))

            def stats(src, i):
                for hb in range(2):
                    ch.did(dve.bn_stats(st[:, i, hb, :], src[:, 512 * hb:512 * hb + 512]))
                ch.sync()
                ch.did(dve.bn_aggr(mv[:, i, :], st[:, i, :, :].rearrange("p a b -> p (a b)")))

            dve.wait_ge(pe_pro, 1)
            dve.tensor_copy(pcol[:, :], COL[:, 0:64]).then_inc(dve_pro, 1)
            dve.wait_ge(s_x, 32)
            for i in range(TILES):
                stats(xin[:, i, :], i)
            rstd(TILES, mv[:, :, 1])
            for i in range(TILES):
                dve.tensor_scalar(xin[:, i, :], xin[:, i, :], mv[:, i, 0:1], rs[:, 2, i:i + 1],
                                  ALU.subtract, ALU.mult).then_inc(dve_n, 1)
            dve.wait_ge(pe_pro, 2)
            for hb in range(2):
                x = dve.tensor_copy(ws_t[:, 4 * hb:4 * hb + 4, :], MX[hb][:, :].rearrange("p (k n) -> p k n", k=4))
            x.then_inc(dve_pro, 1)
            dve.wait_ge(s_bmod, 128)

            def mod_rows(g):
                dve.wait_ge(pe_mod, 8 * (g + 1))
                for j in range(4):
                    rows = modrow[32 * j:32 * j + 2, g, :]
                    x = dve.tensor_tensor(rows, MOD[32 * j:32 * j + 2, :], rows, ALU.add)
                x.then_inc(dve_row, 1)

            def mod_cols(g):
                dve.wait_ge(pe_modcol, 4 * (g + 1))
                dve.tensor_copy(mod_t[:, 2 * g:2 * g + 2, :, :].rearrange("p v k r -> p (v k r)"), COL[:, 0:32]).then_inc(dve_col, 1)

            def split_lo(b):
                u = b // 4
                par = b % 2
                dve.wait_ge(act_whi, b + 1)
                dve.tensor_tensor(w_lo[par][:, :, :], raw[:, u % 2, :, 128 * (b % 4):128 * (b % 4) + 128],
                                  w_hi[par][:, :, :].bitcast(f32), ALU.subtract).then_inc(dve_wlo, 1)

            mod_rows(0)
            mod_cols(0)
            dve.wait_ge(dve_col, 1)
            link(dve.tensor_scalar(scale1p[:, :, :].rearrange("p k r -> p (k r)"),
                                   mod_t[:, 1, :, :].rearrange("p k r -> p (k r)"), 1.0, None, ALU.add))
            split_lo(0)
            dve.wait_ge(act_nt, 8)

            def h_low(kc):
                dve.wait_ge(act_hhi, kc + 1)
                dve.tensor_tensor(h_lo[:, kc, :], n_t[:, kc, :], h_hi[:, kc, :].bitcast(f32), ALU.subtract).then_inc(dve_hlo, 1)

            for kc in range(KC):
                for r in range(REQ):
                    part = n_t[:, kc, SEQ * r:SEQ * r + SEQ]
                    x = dve.tensor_scalar(part, part, scale1p[:, kc, r:r + 1], mod_t[:, 0, kc, r:r + 1], ALU.mult, ALU.add)
                x.then_inc(dve_aff, 1)
                if kc:
                    h_low(kc - 1)
            h_low(KC - 1)
            for n in range(8):
                split_lo(n + 1)
                dve.wait_ge(pe_tr, n + 1)
                dve.tensor_copy(v_nat[:, :, 128 * n:128 * n + 128],
                                TR[n % 2][:, :].rearrange("p (c n) -> p c n", c=TILES)).then_inc(dve_tr, 1)
            mod_rows(1)

            def d_low(n):
                dve.wait_ge(act_dhi, n + 1)
                dve.tensor_tensor(d_lo[:, n % 2, :], d32[n % 2][:, :], d_hi[:, n % 2, :].bitcast(f32), ALU.subtract).then_inc(dve_dlo, 1)

            def pool_w_low(g):
                dve.wait_ge(act_wphi, g + 1)
                dve.tensor_tensor(wp_lo[:, :, :], wp_raw[:, g, :, :], wp_hi[:, :, :].bitcast(f32), ALU.subtract).then_inc(dve_wplo, 1)

            def pool_low(g):
                for o in range(2):
                    dve.wait_ge(act_phi, 2 * g + o + 1)
                    dve.tensor_tensor(a_lo[:, 2 * g + o, :], g32[0][:, :], a_hi[:, 2 * g + o, :].bitcast(f32),
                                      ALU.subtract).then_inc(dve_plo, 1)

            for n in range(8):
                split_lo(9 + n)
                if n:
                    d_low(n - 1)
                if n % 2 == 1:
                    if n >= 3:
                        pool_low(n // 2 - 1)
                    pool_w_low(n // 2)
                g = n // 2
                w = WINDOWS[g]
                dve.wait_ge(pool_win, n + 1)
                dve.wait_ge(act_z, 8 + n + 1)
                if n >= 2:
                    dve.wait_ge(dve_dlo, n - 1)
                dve.scalar_tensor_tensor(out=d32[n % 2][:, :].rearrange("p (r s) -> p r s", r=REQ),
                                         in0=wsum[(g + 1) % 2][:, :, 8 - w // 2:8 - w // 2 + SEQ], scalar=1.0 / w,
                                         in1=zpad[n % 2][:, :, 8:8 + SEQ], op0=ALU.mult, op1=ALU.subtract).then_inc(dve_d, 1)
            split_lo(17)
            d_low(7)
            mod_rows(2)
            mod_cols(1)
            dve.wait_ge(dve_tr, 8)
            for i in range(TILES):
                stats(v_nat[:, i, :], i)
            rstd(TILES, mv[:, :, 1])
            dve.wait_ge(s_sgu, 32)
            for n in range(1, 8):
                split_lo(17 + n)
                if n % 2 == 1:
                    i = n // 2
                    row = v_nat[:, i, :]
                    link(dve.tensor_scalar(row, row, mv[:, i, 0:1], rs[:, 2, i:i + 1], ALU.subtract, ALU.mult))
                    link(dve.tensor_tensor(row, row, sgu_bc[:, 0, :], ALU.mult))
                    dve.tensor_tensor(row, row, sgu_bc[:, 1, :], ALU.add).then_inc(dve_vln, 1)
            pool_low(3)
            for n in range(8):
                b = 24 + n
                split_lo(b + 1)
                dve.wait_ge(pe_blk, b + 1)
                dve.wait_ge(act_z, 16 + n + 1)
                dve.tensor_tensor(m_b[:, n, :], Z[n % 2][:, :], m_b[:, n, :], ALU.mult).then_inc(dve_z, 1)
            dve.wait_ge(s_bs, 16)

            def a_low(n):
                dve.wait_ge(act_ahi, n + 1)
                dve.tensor_tensor(a_lo[:, n, :], d32[n % 2][:, :], a_hi[:, n, :].bitcast(f32), ALU.subtract).then_inc(dve_alo, 1)

            for n in range(8):
                b = 32 + n
                split_lo(b + 1)
                if n:
                    a_low(n - 1)
                dve.wait_ge(pe_mix, n + 1)
                if n >= 2:
                    dve.wait_ge(dve_alo, n - 1)
                bias = bs_bc[:, n:n + 1, :].broadcast_to([128, TILES, 128])
                out = d32[n % 2][:, :].rearrange("p (c n) -> p c n", c=TILES)
                link(dve.tensor_tensor(out, MX[n % 2][:, :].rearrange("p (c n) -> p c n", c=TILES), bias, ALU.add))
                dve.wait_ge(act_z, 24 + n + 1)
                dve.tensor_tensor(d32[n % 2][:, :], d32[n % 2][:, :], g32[n % 2][:, :], ALU.mult).then_inc(dve_a, 1)
            for n in range(8):
                split_lo(41 + n)
                if n == 0:
                    a_low(7)
            dve.wait_ge(dve_alo, 8)
            for n in range(8):
                b = 48 + n
                split_lo(b + 1)
                dve.wait_ge(pe_blk, b + 1)
                dve.wait_ge(act_z, 32 + n + 1)
                if n >= 2:
                    dve.wait_ge(dve_mlo, n - 1)
                dve.tensor_tensor(g_a[:, n, :], Z[n % 2][:, :], g_a[:, n, :], ALU.mult).then_inc(dve_z, 1)
                dve.wait_ge(dve_z, 8 + n + 1)
                dve.tensor_tensor(d32[n % 2][:, :], g_a[:, n, :], m_b[:, n, :], ALU.add).then_inc(dve_m, 1)
                dve.wait_ge(act_mhi, n + 1)
                dve.tensor_tensor(h_lo[:, n, :], d32[n % 2][:, :], h_hi[:, n, :].bitcast(f32), ALU.subtract).then_inc(dve_mlo, 1)
            dve.wait_ge(s_xres, 32)
            for n in range(8):
                if n < 7:
                    split_lo(57 + n)
                dve.wait_ge(pe_tr, 8 + n + 1)
                part = res[:, :, 128 * n:128 * n + 128]
                dve.scalar_tensor_tensor(out=part, in0=part, scalar=ALPHA, in1=TR[n % 2][:, :].rearrange("p (c n) -> p c n", c=TILES),
                                         op0=ALU.mult, op1=ALU.add).then_inc(dve_tr, 1)
            dve.wait_ge(dve_tr, 16)
            dve.wait_ge(s_ln1, 32)
            for i in range(TILES):
                row = res[:, i, :]
                out = h2[:, i, :]
                stats(row, 0)
                rstd(1, mv[:, 0, 1:2])
                link(dve.tensor_scalar(row, row, mv[:, 0, 0:1], rs[:, 2, 0:1], ALU.subtract, ALU.mult))
                link(dve.tensor_tensor(row, row, ln1_bc[:, 0, :], ALU.mult))
                link(dve.tensor_tensor(row, row, ln1_bc[:, 1, :], ALU.add))
                stats(row, 0)
                rstd(1, mv[:, 0, 1:2])
                link(dve.tensor_scalar(out, row, mv[:, 0, 0:1], rs[:, 2, 0:1], ALU.subtract, ALU.mult))
                dve.wait_ge(pe_bc, 2)
                for c in range(2):
                    part = out[:, 512 * c:512 * c + 512]
                    ch.did(dve.scalar_tensor_tensor(out=part, in0=B[4 + c][:, :], scalar=1.0, in1=part, op0=ALU.add, op1=ALU.mult))
                ch.sync()
                for c in range(2):
                    part = out[:, 512 * c:512 * c + 512]
                    x = dve.tensor_tensor(part, part, B[6 + c][:, :], ALU.add)
                x.then_inc(dve_h2, 1)
            dve.wait_ge(pe_rt, 2 * TILES)
            NL = NGRP + NEXP
            link(dve.tensor_tensor(lg[:, :, :], B[0][:, 0:256].rearrange("p (i n) -> p i n", i=TILES)[:, :, 0:NL],
                                   br_bc[:, :].rearrange("p (a n) -> p a n", a=1).broadcast_to([128, TILES, NL]), ALU.add))

            def iota(w):
                return cst[:, C_IOTA:C_IOTA + w].rearrange("p (a n) -> p a n", a=1).broadcast_to([128, TILES, w])

            def col(k, w):
                return q1[:, k, :].rearrange("p (i a) -> p i a", a=1).broadcast_to([128, TILES, w])

            def first_max(src, w, kmax, kidx, tmp, out):
                link(dve.tensor_reduce(q1[:, kmax, :], src, AX.X, ALU.max))
                link(dve.tensor_tensor(tmp, src, col(kmax, w), ALU.is_equal))
                link(dve.scalar_tensor_tensor(out=tmp, in0=tmp, scalar=-64.0, in1=iota(w), op0=ALU.mult, op1=ALU.add))
                link(dve.tensor_reduce(q1[:, kidx, :], tmp, AX.X, ALU.min))
                link(dve.tensor_tensor(out, tmp, col(kidx, w), ALU.is_equal))

            lgg = lg[:, :, 0:NGRP]
            oh_g = q[1][:, :, 0:NGRP]
            first_max(lgg, NGRP, 0, 1, q[0][:, :, 0:NGRP], oh_g)
            dve.tensor_tensor(q1[:, 6:10, :].rearrange("p g i -> p i g"), lgg, col(0, NGRP), ALU.subtract).then_inc(dve_st, 1)
            link(dve.tensor_tensor(seltmp[:, :, :, :], lg[:, :, NGRP:].rearrange("p i (g e) -> p i g e", g=NGRP),
                                   oh_g.rearrange("p i (g a) -> p i g a", a=1).broadcast_to([128, TILES, NGRP, EPG]), ALU.mult))
            link(dve.tensor_reduce(q[2][:, :, :], seltmp[:, :, :, :].rearrange("p i g e -> p i e g"), AX.X, ALU.add))
            first_max(q[2][:, :, :], EPG, 10, 1, q[3][:, :, :], q[4][:, :, :])
            link(dve.scalar_tensor_tensor(out=q[5][:, :, :], in0=q[4][:, :, :], scalar=BIG, in1=q[2][:, :, :], op0=ALU.mult, op1=ALU.add))
            first_max(q[5][:, :, :], EPG, 13, 1, q[3][:, :, :], q[6][:, :, :])
            dve.tensor_tensor(q1[:, 11, :], q1[:, 13, :], q1[:, 10, :], ALU.subtract).then_inc(dve_st, 1)
            for j, oh in enumerate((q[4], q[6])):
                for i in range(TILES):
                    ch.did(dve.tensor_tensor(
                        onehot[:, j, i, :].rearrange("p (g e) -> p g e", g=NGRP),
                        q[1][:, i, 0:NGRP].rearrange("p (g a) -> p g a", a=1).broadcast_to([128, NGRP, EPG]),
                        oh[:, i, :].rearrange("p (a e) -> p a e", a=1).broadcast_to([128, NGRP, EPG]), ALU.mult))
            ch.sync()
            dve.tensor_tensor(both[:, :, :], onehot[:, 0, :, :], onehot[:, 1, :, :], ALU.add).then_inc(dve_rt, 1)
            dve.wait_ge(act_rt, 2 * TILES + 1)
            link(dve.tensor_reduce(q1[:, 14, :], q1[:, 2:6, :].rearrange("p g i -> p i g"), AX.X, ALU.add))
            dve.wait_ge(act_rt, 2 * TILES + 2)
            link(dve.tensor_scalar(q1[:, 15, :], q1[:, 12, :], 1.0, None, ALU.add))
            link(dve.tensor_tensor(q1[:, 14, :], q1[:, 14, :], q1[:, 15, :], ALU.mult))
            link(dve.reciprocal(route_w[:, 0, :], q1[:, 14, :]))
            link(dve.tensor_tensor(route_w[:, 1, :], route_w[:, 0, :], q1[:, 12, :], ALU.mult))
            dve.wait_ge(pe_rt, 2 * TILES + 1)
            totals = B[1][:, NEXP * TILES:NEXP * TILES + NEXP]
            cum, start = seltmp[:, 0, :, :].rearrange("p a b -> p (a b)"), seltmp[:, 1, :, :].rearrange("p a b -> p (a b)")
            cnt = seltmp[:, 2, :, :].rearrange("p a b -> p (a b)")
            link(dve.tensor_copy(cnt, totals))
            link(dve.tensor_tensor_scan(cum, ones[:, 0:NEXP], cnt, 0.0, ALU.mult, ALU.add))
            link(dve.tensor_tensor(start, cum, cnt, ALU.subtract))
            link(dve.tensor_tensor(both[:, :, :], B[1][:, 0:NEXP * TILES].rearrange("p (i n) -> p i n", i=TILES),
                                   start.rearrange("p (a n) -> p a n", a=1).broadcast_to([128, TILES, NEXP]), ALU.add))
            for j in range(2):
                link(dve.tensor_tensor(onehot[:, j, :, :], onehot[:, j, :, :], both[:, :, :], ALU.mult))
                link(dve.tensor_reduce(q1[:, j, :], onehot[:, j, :, :], AX.X, ALU.add))
                place = dve.tensor_copy(pos[:, j, :], q1[:, j, :])
                if j == 0:
                    link(place)
            place.then_inc(dve_rt, 1)
            link(dve.memset(tab[0:1, :, :], 0))
            link(dve.tensor_copy(tab[0:1, 0, 0:NEXP], start[0:1, :]))
            link(dve.tensor_scalar(trow[:, 0, :], cnt[0:1, :], float(CAP), None, ALU.is_gt))
            for k in range(2, 8):
                link(dve.scalar_tensor_tensor(out=trow[:, 0, :], in0=cnt[0:1, :], scalar=float(CAP * k), in1=trow[:, 0, :],
                                              op0=ALU.is_gt, op1=ALU.add))
            link(dve.tensor_tensor_scan(trow[:, 1, :], ones[0:1, 0:NEXP], trow[:, 0, :], 0.0, ALU.mult, ALU.add))
            link(dve.tensor_tensor(trow[:, 2, :], trow[:, 1, :], trow[:, 0, :], ALU.subtract))
            link(dve.tensor_copy(tab[0:1, 1, 0:NEXP], trow[:, 0, :]))
            link(dve.tensor_copy(tab[0:1, 2, 0:NEXP], trow[:, 2, :]))
            dve.tensor_copy(tab[0:1, 2, NEXP:NEXP + 1], trow[:, 1, NEXP - 1:NEXP]).then_inc(dve_rt, 1)
            dve.wait_ge(dve_rt, 3)
            dve.wait_ge(s_scat, 16 * 8)
            dve.wait_ge(m_sem["xtr"], 1)
            dve.tensor_copy(x_t[0][:, :, :].rearrange("p k c -> p (k c)"), B[2][:, :]).then_inc(m_sem["xt"], 1)

            def expert(e, s, last=False):
                dve.wait_ge(m_sem["silu"], e + 1)
                dve.tensor_tensor(hid[:, :], B[0][CAP:128, :], sg[:, :], ALU.mult).then_inc(m_sem["hid"], 1)
                if not last:
                    dve.wait_ge(m_sem["xtr"], e + 2)
                    dve.tensor_copy(x_t[(s + 1) % 3][:, :, :].rearrange("p k c -> p (k c)"), B[2][:, :]).then_inc(m_sem["xt"], 1)
                more = dve.value_load(tab[0:1, 1, bass.ds(e, 1)], min_val=0, max_val=7)
                first = dve.value_load(tab[0:1, 2, bass.ds(e, 1)], min_val=0, max_val=16)
                with dve.If(more > 0):
                    with dve.Fori(0, more) as r:
                        turns = dve.snap(first + r)
                        dve.wait_ge(x_sem["xtr"], turns + 2)
                        dve.tensor_copy(x_t_x[:, :, :].rearrange("p k c -> p (k c)"), B[6][:, :]).then_inc(x_sem["xt"], 1)
                        dve.wait_ge(x_sem["silu"], turns + 1)
                        dve.tensor_tensor(hid_x[:, :], B[4][CAP:128, :], sg_x[:, :], ALU.mult).then_inc(x_sem["hid"], 1)

            with dve.Fori(0, 10) as t:
                for k in range(3):
                    expert(3 * t + k, k)
            expert(30, 0)
            expert(31, 1, last=True)
            dve.wait_ge(pe_bc, 3)
            dve.wait_ge(s_ln2, 32)
            for i in range(TILES):
                y = y_first[i % 2]
                dve.wait_ge(f_t, i + 1)
                link(dve.scalar_tensor_tensor(out=y[:, :], in0=y[:, :], scalar=route_w[:, 0, i:i + 1], in1=y_second[i % 2][:, :],
                                              op0=ALU.mult, op1=ALU.add))
                for c, bank in enumerate((B[0], B[2])):
                    part = y[:, 512 * c:512 * c + 512]
                    ch.did(dve.tensor_tensor(part, bank[:, :], part, ALU.mult))
                ch.sync()
                link(dve.scalar_tensor_tensor(out=y[:, :], in0=res[:, i, :], scalar=ALPHA, in1=y[:, :], op0=ALU.mult, op1=ALU.add))
                stats(y, 0)
                rstd(1, mv[:, 0, 1:2])
                link(dve.tensor_scalar(y[:, :], y[:, :], mv[:, 0, 0:1], rs[:, 2, 0:1], ALU.subtract, ALU.mult))
                link(dve.tensor_tensor(y[:, :], y[:, :], ln2_bc[:, 0, :], ALU.mult))
                dve.tensor_tensor(y[:, :], y[:, :], ln2_bc[:, 1, :], ALU.add).then_inc(f_o, 1)


_INS = ["x_prompt", "x_sample", "c_prompt", "c_sample", "w_mod", "b_mod", "w_in", "b_in", "w_spatial",
        "b_spatial", "sgu_g", "sgu_b", "w_pool", "pool_scale", "w_branch_a", "w_branch_b", "w_out",
        "ln1_g", "ln1_b", "w_router_group", "b_router_group", "w_router_expert", "b_router_expert",
        "w_exp_gate", "w_exp_up", "w_exp_down", "ln2_g", "ln2_b"]


def constants():
    import numpy as np

    c = np.zeros((128, C_END), np.float32)
    c[:, C_ID:C_ID + 128] = np.eye(128)
    c[:, C_LT:C_LT + 128] = np.triu(np.ones((128, 128)), 1)
    c[:, C_ONE:C_ONE + 128] = 1.0
    for j in range(4):
        for r in range(REQ):
            c[32 * j + r, C_SEL + 64 * r:C_SEL + 64 * r + 64] = 1.0
    for g, w in enumerate(WINDOWS):
        h = w // 2
        for k in range(h):
            c[:, C_EDGE + 16 * g + k] = w / (k + h)
        for k in range(h - 1):
            c[:, C_EDGE + 16 * g + 8 + k] = w / (SEQ - (SEQ - h + 1 + k) + h)
    c[:, C_IOTA:C_IOTA + 8] = np.arange(8)
    return c


def kernel(**inputs):
    import numpy as _np
    import concourse.bacc as _bacc
    from concourse import mybir as _mybir
    from concourse.bass_utils import run_bass_kernel_spmd as _run

    nc = _bacc.Bacc("TRN2", target_bir_lowering=False, num_devices=1)
    arrays, args = {}, []
    for name in _INS:
        a = _np.ascontiguousarray(inputs[name])
        arrays[f"in_{name}"] = a
        args.append(nc.dram_tensor(f"in_{name}", a.shape, _mybir.dt.from_np(a.dtype), kind="ExternalInput").ap())
    arrays["in_consts"] = constants()
    args.append(nc.dram_tensor("in_consts", (128, C_END), _mybir.dt.float32, kind="ExternalInput").ap())
    for i in range(REQ):
        args.append(nc.dram_tensor(f"out_{i}", (1, SEQ, D), _mybir.dt.float32, kind="ExternalOutput").ap())
    hybrid_encoder(nc, *args)
    r = _run(nc, [arrays], core_ids=[0])
    return tuple(r.results[0][f"out_{i}"] for i in range(REQ))
```

```python
import concourse.bass as bass
from concourse import mybir
from contextlib import ExitStack, contextmanager

D = 1024
REQ = 2
SEQ = 256
TOK = REQ * SEQ
KC = D // 128
TILES = TOK // 128
HALF = 64
D_IN = 5 * D
NEXP = 32
NGRP = 4
EPG = NEXP // NGRP
DE = D // 2
FC = DE // 128
CAP = 64
ASSIGN = 2 * TOK
WINDOWS = (2, 4, 8, 16)
ALPHA = 2.0 ** 0.25
EPS = 1e-5
BIG = -3.0e38

C_ID, C_LT, C_ONE, C_SEL, C_EDGE, C_IOTA, C_END = 0, 128, 256, 384, 512, 576, 584

SEG_V, SEG_P, SEG_GB, SEG_WB, SEG_U, SEG_GA, SEG_WA, SEG_WO = range(8)
NBLK = 64


def hybrid_encoder(nc, x_prompt, x_sample, c_prompt, c_sample, w_mod, b_mod, w_in, b_in, w_spatial,
                   b_spatial, sgu_g, sgu_b, w_pool, pool_scale, w_branch_a, w_branch_b, w_out,
                   ln1_g, ln1_b, w_router_group, b_router_group, w_router_expert, b_router_expert,
                   w_exp_gate, w_exp_up, w_exp_down, ln2_g, ln2_b, consts, y_prompt, y_sample):
    bf16, f32, f32r, i32, u32 = mybir.dt.bfloat16, mybir.dt.float32, mybir.dt.float32r, mybir.dt.int32, mybir.dt.uint32
    ALU, ACT, AX = mybir.AluOpType, mybir.ActivationFunctionType, mybir.AxisListType

    packed_x = nc.dram_tensor("packed_x", (ASSIGN + 8 * CAP, D), f32).ap()
    packed_y = nc.dram_tensor("packed_y", (ASSIGN + 8 * CAP, D), f32).ap()

    ctx = ExitStack()
    with ctx:
        base = (nc.sbuf_base + 63) // 64 * 64

        def at(name, shape, dt, off):
            return nc.alloc_sbuf_tensor_at(name, shape, dt, offset=base + off)

        def sem(name):
            return ctx.enter_context(nc.semaphore(name))

        K = 1024
        SLOT = 48 * K
        R0 = 3 * SLOT
        S0 = R0 + 16 * K
        gate_w = [at(f"gate_w{s}", [128, KC, DE], f32, s * SLOT) for s in range(3)]
        up_w = [at(f"up_w{s}", [128, KC, DE], f32, s * SLOT + 16 * K) for s in range(3)]
        down_w = [at(f"down_w{s}", [128, FC, D], f32, s * SLOT + 32 * K) for s in range(3)]
        a_hi = at("a_hi", [128, KC, TOK], f32r, 0)
        a_lo = at("a_lo", [128, KC, TOK], f32r, 16 * K)
        xin = at("xin", [128, TILES, D], f32, 0)
        ws_raw = at("ws_raw", [128, 8, 128], f32, 16 * K)
        v_nat = at("v_nat", [128, TILES, D], f32, 32 * K)
        g_a = at("g_a", [128, KC, TOK], f32, 32 * K)
        raw = at("raw", [128, 2, KC, 512], f32, SLOT)
        modraw0 = at("modraw0", [128, 4, 4, 512], f32, SLOT)
        m_b = at("m_b", [128, KC, TOK], f32, SLOT + 32 * K)
        modraw = at("modraw", [128, 2, 4, 512], f32, SLOT + 32 * K)
        h_hi = at("h_hi", [128, KC, TOK], f32r, 2 * SLOT)
        h_lo = at("h_lo", [128, KC, TOK], f32r, 2 * SLOT + 16 * K)
        w_hi = [at(f"w_hi{i}", [128, KC, 128], f32r, 2 * SLOT + 32 * K + i * 8 * K) for i in range(2)]
        w_lo = [at(f"w_lo{i}", [128, KC, 128], f32r, 2 * SLOT + 36 * K + i * 8 * K) for i in range(2)]
        ln2_bc = at("ln2_bc", [128, 2, D], f32, 2 * SLOT)
        y_first = [at(f"y_first{i}", [128, D], f32, 2 * SLOT + (8 + 4 * i) * K) for i in range(TILES)]
        y_second = [at(f"y_second{i}", [128, D], f32, 2 * SLOT + (24 + 4 * i) * K) for i in range(TILES)]
        n_t = at("n_t", [128, KC, TOK], f32, R0)
        wp_raw = at("wp_raw", [128, 4, 2, 256], f32, R0)
        bs_bc = at("bs_bc", [128, 8, 128], f32, R0 + 8 * K)
        res = at("res", [128, TILES, D], f32, R0)
        cst = at("cst", [128, C_END], f32, S0)
        pcol = at("pcol", [128, 64], f32, S0 + 2432)
        mod_t = at("mod_t", [128, 6, KC, REQ], f32, S0 + 2688)
        scale1p = at("scale1p", [128, KC, REQ], f32, S0 + 3072)
        silu_c = at("silu_c", [128, REQ, KC], f32, S0 + 3136)
        st = at("st", [128, TILES, 2, 6], f32, S0 + 3200)
        mv = at("mv", [128, TILES, 2], f32, S0 + 3392)
        rs = at("rs", [128, 8, TILES], f32, S0 + 3424)
        modrow = at("modrow", [128, 3, 512], f32, S0 + 3584)
        prow = at("prow", [64, 128], f32, S0 + 9728 + 31232)
        route_w = at("route_w", [128, 2, TILES], f32, S0 + 2432)
        pos = at("pos", [128, 2, TILES], u32, S0 + 2464)
        tab = at("tab", [1, 3, NEXP + 1], i32, S0 + 2688)
        T0 = S0 + 9728
        ws_t = at("ws_t", [128, 8, 128], f32, T0)
        wp_hi = at("wp_hi", [128, 2, 256], f32r, T0 + 4096)
        wp_lo = at("wp_lo", [128, 2, 256], f32r, T0 + 6144)
        PADW = SEQ + 16
        zpad = [at(f"zpad{i}", [128, REQ, PADW], f32, T0 + 8192 + 2176 * i) for i in range(2)]
        wsum = [at(f"wsum{i}", [128, REQ, PADW], f32, T0 + 12544 + 2176 * i) for i in range(2)]
        sgu_bc = at("sgu_bc", [128, 2, D], f32, T0 + 8192)
        d32 = [at(f"d32_{i}", [128, TOK], f32, T0 + 16896 + 2048 * i) for i in range(2)]
        d_hi = at("d_hi", [128, 2, TOK], f32r, T0 + 20992)
        d_lo = at("d_lo", [128, 2, TOK], f32r, T0 + 25088)
        g32 = [at(f"g32_{i}", [128, TOK], f32, T0 + 29184 + 2048 * i) for i in range(2)]
        ln1_bc = at("ln1_bc", [128, 2, D], f32, T0)
        h2 = at("h2", [128, TILES, D], f32, T0 + 8192)
        h2_t = [at(f"h2_t{i}", [128, KC, 128], f32, T0 + 24576 + 4096 * i) for i in range(2)]
        wr = at("wr", [128, KC, NGRP + NEXP], f32, T0 + 33280)
        Q0 = T0 + 34432
        br_bc = at("br_bc", [128, NGRP + NEXP], f32, Q0)
        lg = at("lg", [128, TILES, NGRP + NEXP], f32, Q0 + 160)
        onehot = at("onehot", [128, 2, TILES, NEXP], f32, Q0 + 736)
        st8 = at("st8", [128, TILES, KC, 6], f32, Q0 + 736)
        both = at("both", [128, TILES + 1, NEXP], bf16, Q0 + 1760)
        place = at("place", [128, TILES, NEXP], f32, T0)
        seltmp = at("seltmp", [128, TILES, NGRP, EPG], f32, Q0 + 2272)
        q = [at(f"q{i}", [128, TILES, EPG], f32, Q0 + 2784 + 128 * i) for i in range(7)]
        q1 = at("q1", [128, 16, TILES], f32, Q0 + 3680)
        trow = at("trow", [1, 4, NEXP], f32, Q0 + 3936)
        before_m = at("before_m", [128, 2, 128], bf16, T0 + 512)
        assert Q0 + 3936 + 512 + base <= nc.sbuf_usable_end
        xrows = [at(f"xrows{i}", [CAP, D], f32, T0 + 4096 * i) for i in range(3)]
        x_t = [at(f"x_t{i}", [128, KC, CAP], f32, T0 + 12288 + 2048 * i) for i in range(3)]
        sg = at("sg", [CAP, DE], f32, T0 + 18432)
        hid = at("hid", [CAP, DE], f32, T0 + 20480)
        hid_t = at("hid_t", [128, FC, CAP], f32, T0 + 22528)
        yout = at("yout", [128, 512], f32, T0 + 23552)
        xrows_x = at("xrows_x", [CAP, D], f32, T0 + 25600)
        x_t_x = at("x_t_x", [128, KC, CAP], f32, T0 + 29696)
        sg_x = at("sg_x", [CAP, DE], f32, T0 + 31744)
        hid_x = at("hid_x", [CAP, DE], f32, T0 + 33792)
        hid_t_x = at("hid_t_x", [128, FC, CAP], f32, T0 + 35840)
        yout_x = at("yout_x", [128, 512], f32, T0 + 36864)

        B = [ctx.enter_context(nc.psum_tensor(f"bank{i}", [128, 512], f32)) for i in range(8)]
        Z = B[0:2]
        TR = B[2:4]
        MX = B[4:6]
        MOD = B[6]
        COL = B[7]

        ident = cst[:, C_ID:C_ID + 128]
        ones = cst[:, C_ONE:C_ONE + 128]

        s_param = sem("s_param")
        s_x = sem("s_x")
        s_ws = sem("s_ws")
        s_bmod = sem("s_bmod")
        s_m0 = [sem(f"s_m0_{i}") for i in range(4)]
        s_m = [sem(f"s_m{i}") for i in range(2)]
        s_w = [sem(f"s_w{i}") for i in range(2)]
        s_bs = sem("s_bs")
        s_wp = sem("s_wp")
        s_sgu = sem("s_sgu")
        s_xres = sem("s_xres")
        s_ln1 = sem("s_ln1")
        s_wr = sem("s_wr")
        s_ln2 = sem("s_ln2")
        s_pad = sem("s_pad")
        s_scat = sem("s_scat")
        s_out = sem("s_out")

        pe_pro = sem("pe_pro")
        pe_xt = sem("pe_xt")
        pe_mod = sem("pe_mod")
        pe_modcol = sem("pe_modcol")
        pe_blk = sem("pe_blk")
        pe_tr = sem("pe_tr")
        pe_pool = sem("pe_pool")
        pe_mix = sem("pe_mix")
        pe_rt = sem("pe_rt")
        pe_lg = sem("pe_lg")
        pe_bc = sem("pe_bc")
        act_pro = sem("act_pro")
        act_nt = sem("act_nt")
        act_hhi = sem("act_hhi")
        act_whi = sem("act_whi")
        act_z = sem("act_z")
        act_dhi = sem("act_dhi")
        act_wphi = sem("act_wphi")
        act_pt = sem("act_pt")
        act_phi = sem("act_phi")
        act_ahi = sem("act_ahi")
        act_mhi = sem("act_mhi")
        act_sq = sem("act_sq")
        act_rt = sem("act_rt")
        act_res = sem("act_res")
        act_f = sem("act_f")
        dve_c = sem("dve_c")
        dve_pro = sem("dve_pro")
        dve_st = sem("dve_st")
        dve_n = sem("dve_n")
        dve_row = sem("dve_row")
        dve_row0 = sem("dve_row0")
        dve_col = sem("dve_col")
        dve_aff = sem("dve_aff")
        dve_hlo = sem("dve_hlo")
        dve_wlo = sem("dve_wlo")
        dve_z = sem("dve_z")
        dve_tr = sem("dve_tr")
        dve_d = sem("dve_d")
        dve_dlo = sem("dve_dlo")
        dve_wplo = sem("dve_wplo")
        dve_plo = sem("dve_plo")
        dve_vln = sem("dve_vln")
        dve_a = sem("dve_a")
        dve_alo = sem("dve_alo")
        dve_m = sem("dve_m")
        dve_mlo = sem("dve_mlo")
        dve_h2 = sem("dve_h2")
        dve_rt = sem("dve_rt")
        pool_pad = sem("pool_pad")
        pool_c = sem("pool_c")
        pool_win = sem("pool_win")
        e_gu = [sem(f"e_gu{s}") for s in range(3)]
        e_dn = [sem(f"e_dn{s}") for s in range(3)]
        e_x = [sem(f"e_x{s}") for s in range(3)]
        e_st = sem("e_st")
        x_x = sem("x_x")
        m_sem = {n: sem("e_" + n) for n in ("xtr", "xt", "gum", "silu", "hid", "htr", "ht", "ym", "yo")}
        x_sem = {n: sem("x_" + n) for n in ("xtr", "xt", "gum", "silu", "hid", "htr", "ht", "ym", "yo")}
        f_g = [sem(f"f_g{i}") for i in range(TILES)]
        sp_go = sem("sp_go")
        pe_go = sem("pe_go")
        pool_go = sem("pool_go")
        f_t = sem("f_t")
        f_o = sem("f_o")
        f_m = sem("f_m")
        pool_f = sem("pool_f")
        dve_nb = sem("dve_nb")

        block = ctx.enter_context(nc.Block())

        class Chain:

            def __init__(self, e, s):
                self.e, self.s, self.base, self.n = e, s, 0, 0

            def did(self, ins):
                ins.then_inc(self.s, 1)
                self.n += 1

            def sync(self):
                self.e.wait_ge(self.s, self.base + self.n)

            @contextmanager
            def loop(self, trips, per):
                start = self.base + self.n
                with self.e.Fori(0, trips) as t:
                    self.base, self.n = start + t * per, 0
                    yield t
                    assert self.n == per, (self.n, per)
                self.base, self.n = start + trips * per, 0

        def win_cols(seg, unit):
            first = {SEG_U: 0, SEG_V: D, SEG_P: 2 * D, SEG_GA: 3 * D, SEG_GB: 4 * D}[seg] + 512 * unit
            return w_in[0, :, first:first + 512]

        def unit_source(u):
            seg, half = u // 2, u % 2
            if seg in (SEG_WB, SEG_WA, SEG_WO):
                w = {SEG_WB: w_branch_b, SEG_WA: w_branch_a, SEG_WO: w_out}[seg]
                src = w[0, :, 512 * half:512 * half + 512]
            else:
                src = win_cols(seg, half)
            return src.rearrange("(k p) n -> p k n", p=128)

        def mod_source(m):
            r, kc = m // KC, m % KC
            return w_mod[0, kc * 128:kc * 128 + 128, r * 2048:r * 2048 + 2048].rearrange("p (j n) -> p j n", j=4)

        def gate_src(w, e):
            return w[0, bass.ds(e, 1), :, :].rearrange("a (p k) n -> p (a k) n", p=128)

        @block.sync
        def _(sp):
            def load_unit(u):
                if u >= 2:
                    sp.wait_ge(dve_wlo, 4 * (u - 1))
                sp.dma_start(raw[:, u % 2, :, :], unit_source(u)).then_inc(s_w[u % 2], 16)

            def load_mod(m):
                if m - 10 >= 0:
                    sp.wait_ge(pe_mod, m - 1)
                sp.dma_start(modraw[:, m % 2, :, :], mod_source(m)).then_inc(s_m[m % 2], 16)

            sp.dma_start(cst[:, :], consts).then_inc(s_param, 16)
            sp.dma_start(prow[0:40, :], b_in[0, :].rearrange("(a n) -> a n", n=128)).then_inc(s_param, 16)
            sp.dma_start(prow[40:48, :], pool_scale[0, :].rearrange("(a n) -> a n", n=128)).then_inc(s_param, 16)
            sp.dma_start(prow[48:56, :], c_prompt[0, :].rearrange("(a n) -> a n", n=128)).then_inc(s_param, 16)
            sp.dma_start(prow[56:64, :], c_sample[0, :].rearrange("(a n) -> a n", n=128)).then_inc(s_param, 16)
            for r, x in enumerate((x_prompt, x_sample)):
                sp.dma_start(xin[HALF * r:HALF * r + HALF, :, :],
                             x[0, :, :].rearrange("(i p) d -> p i d", p=HALF)).then_inc(s_x, 16)
            for m in range(KC):
                if m >= 4:
                    sp.wait_ge(pe_mod, m - 3)
                sp.dma_start(modraw0[:, m % 4, :, :], mod_source(m)).then_inc(s_m0[m % 4], 16)
            sp.wait_ge(pe_mod, 6)
            load_unit(0)
            sp.wait_ge(pe_mod, 8)
            load_unit(1)
            for k in range(16):
                if k in (5, 9, 13):
                    load_unit((k - 1) // 4 + 1)
                load_mod(8 + k)
            for u in range(5, 16):
                load_unit(u)

            def load_gate_up(e, s):
                sp.dma_start(gate_w[s][:, :, :], gate_src(w_exp_gate, e)).then_inc(e_gu[s], 16)
                sp.dma_start(up_w[s][:, :, :], gate_src(w_exp_up, e)).then_inc(e_gu[s], 16)

            def load_down(e, s):
                sp.dma_start(down_w[s][:, :, :], gate_src(w_exp_down, e)).then_inc(e_dn[s], 16)

            def load_expert(e, s):
                load_gate_up(e, s)
                load_down(e, s)

            sp.wait_ge(pe_blk, 56)
            sp.wait_ge(dve_m, 8)
            load_expert(0, 0)
            sp.wait_ge(dve_wlo, NBLK)
            load_expert(1, 1)
            sp.wait_ge(pe_blk, NBLK)
            load_expert(2, 2)

            def load_rows(e, s, off):
                sp.dma_start(xrows[s][:, :], packed_x[bass.ds(off, CAP), :]).then_inc(e_x[s], 16)

            def offset(e):
                return sp.value_load(tab[0:1, 0, bass.ds(e, 1)], min_val=0, max_val=ASSIGN)

            def next_expert(e, s):
                done = sp.value_load(tab[0:1, 2, bass.ds(e - 2, 1)], min_val=0, max_val=16)
                sp.wait_ge(m_sem["gum"], e - 2)
                sp.sem_inc(sp_go, 1)
                sp.wait_ge(x_sem["gum"], done + 1)
                sp.sem_inc(sp_go, 1)
                load_gate_up(e, s)
                sp.wait_ge(m_sem["ym"], e - 2)
                sp.sem_inc(sp_go, 1)
                sp.wait_ge(x_sem["ym"], done + 1)
                sp.sem_inc(sp_go, 1)
                load_down(e, s)
                load_rows(e, s, offset(e))

            sp.wait_ge(s_scat, 16 * 8)
            sp.wait_ge(s_pad, 16)
            sp.wait_ge(dve_rt, 3)
            for e in range(3):
                load_rows(e, e, offset(e))
            with sp.Fori(0, 9) as t:
                for k in range(3):
                    next_expert(3 + 3 * t + k, k)
            next_expert(30, 0)
            next_expert(31, 1)

        @block.gpsimd
        def _(pool):
            ch = Chain(pool, pool_c)
            pool.dma_start(ws_raw[:, :, :], w_spatial[0, :, :, :].rearrange("h p q -> p h q")).then_inc(s_ws, 16)
            for j in range(4):
                for r in range(REQ):
                    pool.dma_start(modrow[32 * j + r:32 * j + r + 1, :, :],
                                   b_mod[0:1, :].rearrange("a (g j n) -> a g j n", g=3, j=4)[:, :, j, :]).then_inc(s_bmod, 16)
            pool.dma_start(wr[:, :, 0:NGRP], w_router_group[0, :, :].rearrange("(k p) n -> p k n", p=128)).then_inc(s_wr, 16)
            pool.dma_start(wr[:, :, NGRP:], w_router_expert[0, :, :].rearrange("(k p) n -> p k n", p=128)).then_inc(s_wr, 16)
            pool.dma_start(br_bc[:, 0:NGRP], b_router_group[0, :].partition_broadcast(128)).then_inc(s_wr, 16)
            pool.dma_start(br_bc[:, NGRP:], b_router_expert[0, :].partition_broadcast(128)).then_inc(s_wr, 16)
            for i in range(2):
                pool.memset(zpad[i][:, :, :], 0.0).then_inc(pool_pad, 1)
            pool.wait_ge(pool_pad, 1)
            pool.dma_start(packed_x[ASSIGN:ASSIGN + CAP, :].rearrange("r (h n) -> (r h) n", h=2),
                           zpad[0][:, :, :].rearrange("p r n -> p (r n)")[:, 0:512]).then_inc(s_pad, 16)
            pool.wait_ge(dve_hlo, KC)
            pool.dma_start(wp_raw[:, :, :, :], w_pool[0, :, :, :].rearrange("g (k p) n -> p g k n", p=128)).then_inc(s_wp, 16)
            pool.dma_start(bs_bc[:, :, :].rearrange("p h q -> p (h q)"),
                           b_spatial[0, :, :].rearrange("h q -> (h q)").partition_broadcast(128)).then_inc(s_bs, 16)
            pool.wait_ge(s_param, 80)
            for n in range(8):
                g = n // 2
                w = WINDOWS[g]
                pool.wait_ge(act_z, 8 + n + 1)
                if n:
                    pool.wait_ge(dve_d, n)
                src = zpad[n % 2]
                for k in range(1, g + 2):
                    length = PADW - 2 ** k + 1
                    dst = wsum[k % 2]
                    if k > 1:
                        ch.sync()
                    ch.did(pool.tensor_tensor(dst[:, :, 0:length], src[:, :, 0:length],
                                              src[:, :, 2 ** (k - 1):2 ** (k - 1) + length], ALU.add))
                    src = dst
                ch.sync()
                edges = []
                for r in range(REQ):
                    edges.append((src[:, r, 8 - w // 2:8], C_EDGE + 16 * g, w // 2))
                    if w > 2:
                        first = 8 - w // 2 + SEQ - w // 2 + 1
                        edges.append((src[:, r, first:first + w // 2 - 1], C_EDGE + 16 * g + 8, w // 2 - 1))
                for part, c, width in edges[:-1]:
                    ch.did(pool.tensor_tensor(part, part, cst[:, c:c + width], ALU.mult))
                ch.sync()
                part, c, width = edges[-1]
                pool.tensor_tensor(part, part, cst[:, c:c + width], ALU.mult).then_inc(pool_win, 1)
            pool.wait_ge(dve_d, 8)
            pool.dma_start(sgu_bc[:, 0, :], sgu_g[0, :].partition_broadcast(128)).then_inc(s_sgu, 16)
            pool.dma_start(sgu_bc[:, 1, :], sgu_b[0, :].partition_broadcast(128)).then_inc(s_sgu, 16)
            pool.wait_ge(dve_a, 8)
            for r, x in enumerate((x_prompt, x_sample)):
                pool.dma_start(res[HALF * r:HALF * r + HALF, :, :],
                               x[0, :, :].rearrange("(i p) d -> p i d", p=HALF)).then_inc(s_xres, 16)
            pool.dma_start(ln1_bc[:, 0, :], ln1_g[0, :].partition_broadcast(128)).then_inc(s_ln1, 16)
            pool.dma_start(ln1_bc[:, 1, :], ln1_b[0, :].partition_broadcast(128)).then_inc(s_ln1, 16)
            pool.wait_ge(dve_rt, 2)
            pool.wait_ge(dve_h2, TILES)
            for j in range(2):
                for i in range(TILES):
                    pool.indirect_dma_start(packed_x[0:ASSIGN, :], bass.IndirectOffsetOnAxis(pos[:, j, i:i + 1], 0),
                                            h2[:, i, :], None, bounds_check=ASSIGN - 1, oob_is_err=False).then_inc(s_scat, 16)
            pool.wait_ge(dve_rt, 3)

            def store(y, off, before):
                if not (isinstance(before, int) and before == 0):
                    pool.wait_ge(e_st, 32 * before)
                pool.sem_inc(pool_go, 1)
                pool.dma_start(packed_y[bass.ds(off, CAP), 0:512], y[0:64, :]).then_inc(e_st, 16)
                pool.dma_start(packed_y[bass.ds(off, CAP), 512:1024], y[64:128, :]).then_inc(e_st, 16)

            def expert(e):
                off = pool.value_load(tab[0:1, 0, bass.ds(e, 1)], min_val=0, max_val=ASSIGN)
                more = pool.value_load(tab[0:1, 1, bass.ds(e, 1)], min_val=0, max_val=7)
                first = 0 if isinstance(e, int) else pool.value_load(tab[0:1, 2, bass.ds(e, 1)], min_val=0, max_val=16)

                def load_further(r):
                    pool.wait_ge(x_sem["xtr"], first + r + 1)
                    pool.sem_inc(pool_go, 1)
                    pool.dma_start(xrows_x[:, :], packed_x[bass.ds(pool.snap(off + (r + 1) * CAP), CAP), :]).then_inc(x_x, 16)

                def store_further(r):
                    pool.wait_ge(x_sem["yo"], first + r + 2)
                    store(yout_x, pool.snap(off + (r + 1) * CAP), e + 1 + first + r)

                with pool.If(more > 0):
                    load_further(0)
                pool.wait_ge(m_sem["yo"], e + 2)
                store(yout, off, e + first)
                with pool.If(more > 1):
                    with pool.Fori(0, more - 1) as r:
                        load_further(r + 1)
                        store_further(r)
                with pool.If(more > 0):
                    store_further(more - 1)

            expert(0)
            with pool.Fori(1, NEXP) as e:
                expert(e)
            pool.wait_ge(m_sem["ym"], 30)
            allx = pool.value_load(tab[0:1, 2, NEXP:NEXP + 1], min_val=0, max_val=16)
            pool.wait_ge(x_sem["ym"], allx + 1)
            pool.sem_inc(pool_go, 1)
            pool.dma_start(ln2_bc[:, 0, :], ln2_g[0, :].partition_broadcast(128)).then_inc(s_ln2, 16)
            pool.dma_start(ln2_bc[:, 1, :], ln2_b[0, :].partition_broadcast(128)).then_inc(s_ln2, 16)
            pool.wait_ge(e_st, 32 * (allx + NEXP))
            pool.sem_inc(pool_go, 1)
            for i in range(TILES):
                for j, y in enumerate((y_second, y_first)):
                    pool.indirect_dma_start(y[i][:, :], None, packed_y[0:ASSIGN, :],
                                            bass.IndirectOffsetOnAxis(pos[:, 1 - j, i:i + 1], 0),
                                            bounds_check=ASSIGN - 1, oob_is_err=False).then_inc(f_g[i], 16)
            pool.wait_ge(s_ln2, 32)
            for i in range(2):
                pool.wait_ge(f_m, i + 1)
                pool.tensor_tensor(y_first[i][:, :], y_first[i][:, :], ln2_bc[:, 1, :], ALU.add).then_inc(pool_f, 1)

        @block.tensor
        def _(pe):
            def mm(out, lhsT, rhs, start=True, stop=True):
                return pe.matmul(out, lhsT, rhs, start=start, stop=stop, skip_group_check=True)

            pe.wait_ge(s_param, 80)
            pe.transpose(COL[:, 0:64], prow[0:64, :], ident[0:64, 0:64]).then_inc(pe_pro, 1)
            pe.wait_ge(s_ws, 16)
            for hb in range(8):
                x = pe.transpose(MX[hb // 4][:, 128 * (hb % 4):128 * (hb % 4) + 128], ws_raw[:, hb, :], ident)
            x.then_inc(pe_pro, 1)
            def mod_unit(src, kc):
                for j in range(4):
                    x = mm(MOD[32 * j:32 * j + 2, :], silu_c[:, :, kc], src[:, j, :], start=(kc == 0), stop=(kc == KC - 1))
                x.then_inc(pe_mod, 1)

            def mod_cols(g, j):
                if j:
                    pe.wait_ge(pe_modcol, 4 * g + j)
                for k in range(4):
                    c = 4 * j + k
                    x = mm(COL[:, 2 * c:2 * c + 2], modrow[32 * j:32 * j + 2, g, 128 * k:128 * k + 128],
                           ident[32 * j:32 * j + 2, 32 * j:32 * j + 2])
                x.then_inc(pe_modcol, 1)

            def mod_units0(first, last):
                for m in range(first, last):
                    pe.wait_ge(s_m0[m % 4], 16 * (m // 4 + 1))
                    mod_unit(modraw0[:, m % 4, :, :], m)

            pe.wait_ge(act_pro, 1)
            mod_units0(0, 4)
            for i in range(TILES):
                pe.wait_ge(dve_n, i + 1)
                if i >= 2:
                    pe.wait_ge(act_nt, 2 * (i - 1))
                for kc in range(KC):
                    bank = B[2 * (i % 2) + kc // 4]
                    x = pe.transpose(bank[:, 128 * (kc % 4):128 * (kc % 4) + 128], xin[:, i, 128 * kc:128 * kc + 128], ident)
                x.then_inc(pe_xt, 1)
            mod_units0(4, KC)
            for j in range(4):
                pe.wait_ge(dve_row0, j + 1)
                mod_cols(0, j)

            def block_at(b, i, mov_hi, mov_lo, freed, count, fresh=None):
                pe.wait_ge(act_whi, b + 1)
                pe.wait_ge(dve_wlo, b + 1)
                if freed is not None:
                    pe.wait_ge(freed, count)
                for kc in range(KC):
                    if fresh is not None and kc == KC - 1:
                        pe.wait_ge(fresh[0], KC)
                        pe.wait_ge(fresh[1], KC)
                    mm(Z[i][:, :], w_hi[i][:, kc, :], mov_lo[:, kc, :], start=(kc == 0), stop=False)
                    mm(Z[i][:, :], w_hi[i][:, kc, :], mov_hi[:, kc, :], start=False, stop=False)
                    x = mm(Z[i][:, :], w_lo[i][:, kc, :], mov_hi[:, kc, :], start=False, stop=(kc == KC - 1))
                x.then_inc(pe_blk, 1)

            def transposes(k, zs, trs):
                pe.wait_ge(act_z, zs)
                if trs is not None:
                    pe.wait_ge(dve_tr, trs)
                for c in range(TILES):
                    x = pe.transpose(TR[k][:, 128 * c:128 * c + 128], g32[k][:, 128 * c:128 * c + 128], ident)
                x.then_inc(pe_tr, 1)

            pe.wait_ge(dve_pro, 2)
            pe.wait_ge(act_whi, 1)
            pe.wait_ge(dve_wlo, 1)
            for kc in range(KC):
                pe.wait_ge(act_hhi, kc + 1)
                mm(Z[0][:, :], w_hi[0][:, kc, :], h_hi[:, kc, :], start=(kc == 0), stop=False)
                mm(Z[0][:, :], w_lo[0][:, kc, :], h_hi[:, kc, :], start=False, stop=False)
            for kc in range(KC):
                pe.wait_ge(dve_hlo, kc + 1)
                x = mm(Z[0][:, :], w_hi[0][:, kc, :], h_lo[:, kc, :], start=False, stop=(kc == KC - 1))
            x.then_inc(pe_blk, 1)
            for n in range(8):
                if n:
                    block_at(n, n % 2, h_hi, h_lo, act_z if n >= 2 else None, n - 1)
                    transposes((n - 1) % 2, n, n - 2 if n >= 3 else None)
                pe.wait_ge(s_m[n % 2], 16 * (n // 2 + 1))
                mod_unit(modraw[:, n % 2, :, :], n)
            def pooled(g):
                pe.wait_ge(act_dhi, 2 * g + 2)
                pe.wait_ge(dve_dlo, 2 * g + 2)
                pe.wait_ge(act_wphi, g + 1)
                pe.wait_ge(dve_wplo, g + 1)
                if g:
                    pe.wait_ge(act_pt, 2 * g)
                for o in range(2):
                    cols = slice(128 * o, 128 * o + 128)
                    for kc in range(2):
                        mm(MX[o][:, :], wp_hi[:, kc, cols], d_lo[:, kc, :], start=(kc == 0), stop=False)
                        mm(MX[o][:, :], wp_hi[:, kc, cols], d_hi[:, kc, :], start=False, stop=False)
                        x = mm(MX[o][:, :], wp_lo[:, kc, cols], d_hi[:, kc, :], start=False, stop=(kc == 1))
                    x.then_inc(pe_pool, 1)

            for n in range(8):
                b = 8 + n
                block_at(b, n % 2, h_hi, h_lo, act_z, b - 1)
                if n == 0:
                    transposes(1, 8, 6)
                if n >= 3 and n % 2 == 1:
                    pooled(n // 2 - 1)
                pe.wait_ge(s_m[n % 2], 16 * (5 + n // 2))
                if n == 0:
                    pe.wait_ge(dve_row, 1)
                mod_unit(modraw[:, n % 2, :, :], n)
            for k in range(2):
                block_at(16 + k, k, h_hi, h_lo, act_z, 15 + k)
                mod_cols(1, k)
            pooled(3)
            with pe.Fori(1, 4) as t:
                for k in range(2):
                    block_at(16 + 2 * t + k, k, h_hi, h_lo, act_z, 16 + 2 * t + k - 1)
            pe.wait_ge(act_phi, 8)
            pe.wait_ge(dve_plo, 8)
            for k in range(2):
                block_at(24 + k, k, a_hi, a_lo, act_z, 23 + k)
            with pe.Fori(0, 3) as t:
                for k in range(2):
                    block_at(26 + 2 * t + k, k, a_hi, a_lo, dve_z, 2 * t + k + 1)
            pe.wait_ge(dve_vln, TILES)
            for n in range(8):
                b = 32 + n
                block_at(b, n % 2, h_hi, h_lo, dve_z if n < 2 else act_z, 7 + n if n < 2 else 24 + n - 1)
                if n >= 2:
                    pe.wait_ge(dve_a, n - 1)
                for c in range(TILES):
                    x = mm(MX[n % 2][:, 128 * c:128 * c + 128], v_nat[:, c, 128 * n:128 * n + 128], ws_t[:, n, :])
                x.then_inc(pe_mix, 1)
            with pe.Fori(0, 4) as t:
                for k in range(2):
                    block_at(40 + 2 * t + k, k, h_hi, h_lo, act_z, 31 + 2 * t + k)
            pe.wait_ge(act_ahi, 8)
            pe.wait_ge(dve_alo, 8)
            for k in range(2):
                block_at(48 + k, k, a_hi, a_lo, act_z, 39 + k)
            with pe.Fori(0, 3) as t:
                for k in range(2):
                    block_at(50 + 2 * t + k, k, a_hi, a_lo, dve_z, 8 + 2 * t + k + 1)
            pe.wait_ge(act_mhi, KC - 1)
            pe.wait_ge(dve_mlo, KC - 1)
            block_at(56, 0, h_hi, h_lo, dve_z, 15, fresh=(act_mhi, dve_mlo))
            block_at(57, 1, h_hi, h_lo, dve_z, 16)
            transposes(0, 41, 7)
            with pe.Fori(1, 4) as t:
                for k in range(2):
                    block_at(56 + 2 * t + k, k, h_hi, h_lo, act_z, 39 + 2 * t + k)
                    transposes(1 - k, 40 + 2 * t + k, 6 + 2 * t + k)
            transposes(1, 48, 14)

            def broadcast(vec, banks):
                for c in range(2):
                    ch_id = 2 * vec + c
                    g, j = ch_id // 4, ch_id % 4
                    x = mm(banks[c][:, :], cst[32 * j:32 * j + 2, C_SEL:C_SEL + 128], modrow[32 * j:32 * j + 2, g, :])
                x.then_inc(pe_bc, 1)

            pe.wait_ge(dve_row, 3)
            pe.wait_ge(dve_col, 2)
            broadcast(4, (B[4], B[5]))
            broadcast(3, (B[6], B[7]))
            pe.wait_ge(s_wr, 64)
            def h2_transposes(i):
                pe.wait_ge(dve_h2, i + 1)
                for hb in range(2):
                    if i:
                        pe.wait_ge(act_rt, 2 * i - 1 + hb)
                    for k in range(4):
                        kc = 4 * hb + k
                        x = pe.transpose(TR[hb][:, 128 * k:128 * k + 128], h2[:, i, 128 * kc:128 * kc + 128], ident)
                    x.then_inc(pe_rt, 1)

            pe.wait_ge(dve_tr, 16)
            h2_transposes(0)
            for i in range(TILES):
                if i < TILES - 1:
                    h2_transposes(i + 1)
                pe.wait_ge(act_rt, 2 * (i + 1))
                for kc in range(KC):
                    x = mm(B[0][:, 64 * i:64 * i + NGRP + NEXP], h2_t[i % 2][:, kc, :], wr[:, kc, :], start=(kc == 0), stop=(kc == KC - 1))
                x.then_inc(pe_lg, 1)
            pe.wait_ge(dve_rt, 1)
            before, every = before_m[:, 0, :], before_m[:, 1, :]

            def count(first, last, lhsT, src, start=False, stop=False):
                w = last - first + 1
                return mm(B[1][:, NEXP * first:NEXP * (last + 1)], lhsT,
                          both[:, src:src + w, :].rearrange("p i n -> p (i n)"), start=start, stop=stop)

            count(0, 4, every, 0, start=True)
            count(0, 3, before, 1)
            for back in range(1, TILES):
                x = count(1 + back, 4, every, 1, stop=(back == TILES - 1))
            x.then_inc(pe_lg, 1)

            def x_transposes(rows, bank, s):
                pe.sem_inc(pe_go, 1)
                view = rows[:, :].rearrange("c (p k) -> c k p", k=KC)
                for kc in range(KC):
                    x = pe.transpose(bank[:, CAP * kc:CAP * kc + CAP], view[:, kc, :], ident[0:CAP, 0:CAP])
                x.then_inc(s["xtr"], 1)

            def gate_up(xt, s, bank, sm):
                for kc in range(KC):
                    mm(bank[0:CAP, :], xt[:, kc, :], gate_w[s][:, kc, :], start=(kc == 0), stop=(kc == KC - 1))
                    x = mm(bank[CAP:128, :], xt[:, kc, :], up_w[s][:, kc, :], start=(kc == 0), stop=(kc == KC - 1))
                x.then_inc(sm["gum"], 1)

            def h_transposes(hd, bank, sm):
                pe.sem_inc(pe_go, 1)
                view = hd[:, :].rearrange("c (p f) -> c f p", f=FC)
                for fc in range(FC):
                    x = pe.transpose(bank[:, CAP * fc:CAP * fc + CAP], view[:, fc, :], ident[0:CAP, 0:CAP])
                x.then_inc(sm["htr"], 1)

            def down(ht, s, bank, sm):
                for fc in range(FC):
                    mm(bank[0:CAP, :], ht[:, fc, :], down_w[s][:, fc, 0:512], start=(fc == 0), stop=(fc == FC - 1))
                    x = mm(bank[CAP:128, :], ht[:, fc, :], down_w[s][:, fc, 512:1024], start=(fc == 0), stop=(fc == FC - 1))
                x.then_inc(sm["ym"], 1)

            def expert(e, s, turn, last=False):
                pe.wait_ge(e_gu[s], 32 * (turn + 1))
                pe.wait_ge(m_sem["xt"], e + 1)
                gate_up(x_t[s], s, B[0], m_sem)
                if not last:
                    n = (s + 1) % 3
                    pe.wait_ge(e_x[n], 16 * (turn + 1 + (1 if n == 0 else 0)))
                    x_transposes(xrows[n], B[2], m_sem)
                pe.wait_ge(m_sem["hid"], e + 1)
                h_transposes(hid, B[3], m_sem)
                pe.wait_ge(m_sem["ht"], e + 1)
                pe.wait_ge(e_dn[s], 16 * (turn + 1))
                pe.wait_ge(m_sem["yo"], e + 1)
                down(hid_t, s, B[1], m_sem)
                more = pe.value_load(tab[0:1, 1, bass.ds(e, 1)], min_val=0, max_val=7)
                first = pe.value_load(tab[0:1, 2, bass.ds(e, 1)], min_val=0, max_val=16)
                with pe.If(more > 0):
                    with pe.Fori(0, more) as r:
                        turns = pe.snap(first + r)
                        pe.wait_ge(x_x, 16 * (turns + 1))
                        pe.wait_ge(x_sem["yo"], turns + 1)
                        x_transposes(xrows_x, B[6], x_sem)
                        pe.wait_ge(x_sem["xt"], turns + 1)
                        gate_up(x_t_x, s, B[4], x_sem)
                        pe.wait_ge(x_sem["hid"], turns + 1)
                        h_transposes(hid_x, B[7], x_sem)
                        pe.wait_ge(x_sem["ht"], turns + 1)
                        down(hid_t_x, s, B[5], x_sem)

            pe.sem_inc(x_sem["xtr"], 1)
            pe.sem_inc(x_sem["ym"], 1)
            pe.sem_inc(x_sem["gum"], 1)
            pe.wait_ge(dve_rt, 3)
            pe.wait_ge(e_x[0], 16)
            x_transposes(xrows[0], B[2], m_sem)
            with pe.Fori(0, 10) as t:
                for k in range(3):
                    expert(3 * t + k, k, t)
            expert(30, 0, 10)
            expert(31, 1, 10, last=True)
            broadcast(5, (B[0], B[2]))

        @block.scalar
        def _(act):
            def copy(out, in_, scale=1.0):
                return act.activation(out, in_, ACT.Copy, scale=scale)

            def split_hi(b):
                u = b // 4
                act.wait_ge(s_w[u % 2], 16 * (u // 2 + 1))
                if b >= 2:
                    act.wait_ge(pe_blk, b - 1)
                copy(w_hi[b % 2][:, :, :], raw[:, u % 2, :, 128 * (b % 4):128 * (b % 4) + 128]).then_inc(act_whi, 1)

            act.wait_ge(dve_pro, 1)
            act.activation(silu_c[:, :, :].rearrange("p r k -> p (r k)"), COL[:, 48:64], ACT.Silu).then_inc(act_pro, 1)
            act.wait_ge(dve_st, 1)
            act.activation(rs[:, 1, :], rs[:, 0, :], ACT.Sqrt).then_inc(act_sq, 1)
            n_view = n_t[:, :, :].rearrange("p k (r i n) -> p k r i n", r=REQ, i=TILES)
            for i in range(TILES):
                act.wait_ge(pe_xt, i + 1)
                for hb in range(2):
                    src = B[2 * (i % 2) + hb][:, :].rearrange("p (k r n) -> p k r n", k=4, r=REQ)
                    copy(n_view[:, 4 * hb:4 * hb + 4, :, i, :], src).then_inc(act_nt, 1)
            split_hi(0)
            act.wait_ge(dve_aff, 1)
            for kc in range(KC):
                for r in range(REQ):
                    x = act.activation(h_hi[:, kc, SEQ * r:SEQ * r + SEQ], n_t[:, kc, SEQ * r:SEQ * r + SEQ], ACT.Identity,
                                       scale=scale1p[:, kc, r:r + 1], bias=mod_t[:, 0, kc, r:r + 1])
                x.then_inc(act_hhi, 1)
            split_hi(1)

            def run(seg, n, evac=None):
                b = 8 * seg + n
                if evac:
                    act.wait_ge(pe_blk, b + 1)
                    evac(n, n % 2, b)
                if b + 2 < NBLK:
                    split_hi(b + 2)

            def ev_v(n, i, b):
                if b >= 2:
                    act.wait_ge(pe_tr, b - 1)
                act.activation(g32[i][:, :], Z[i][:, :], ACT.Gelu_apprx_tanh, bias=pcol[:, 8 + n:9 + n]).then_inc(act_z, 1)

            for n in range(8):
                run(SEG_V, n, ev_v)

            def d_high(n):
                act.wait_ge(dve_d, n + 1)
                if n >= 2:
                    act.wait_ge(pe_pool, 2 * (n // 2))
                copy(d_hi[:, n % 2, :], d32[n % 2][:, :]).then_inc(act_dhi, 1)

            def pool_w_high(g):
                act.wait_ge(s_wp, 16)
                if g:
                    act.wait_ge(pe_pool, 2 * g)
                copy(wp_hi[:, :, :], wp_raw[:, g, :, :]).then_inc(act_wphi, 1)

            def pool_evac(g):
                for o in range(2):
                    act.wait_ge(pe_pool, 2 * g + o + 1)
                    if g:
                        act.wait_ge(dve_plo, 2 * g + o - 1)
                    act.activation(g32[o][:, :], MX[o][:, :], ACT.Copy,
                                   scale=pcol[:, 40 + 2 * g + o:41 + 2 * g + o]).then_inc(act_pt, 1)
                    act.wait_ge(act_pt, 2 * g + o + 1)
                    copy(a_hi[:, 2 * g + o, :], g32[o][:, :]).then_inc(act_phi, 1)

            def ev_p(n, i, b):
                if n >= 2:
                    act.wait_ge(dve_d, n - 1)
                else:
                    act.wait_ge(pool_pad, 2)
                    act.wait_ge(s_pad, 16)
                act.activation(zpad[i][:, :, 8:8 + SEQ], Z[i][:, :].rearrange("p (r s) -> p r s", r=REQ),
                               ACT.Identity, bias=pcol[:, 16 + n:17 + n]).then_inc(act_z, 1)

            def pool_steps(n):
                if n:
                    d_high(n - 1)
                if n == 1:
                    pool_w_high(0)
                if n >= 4 and n % 2 == 0:
                    if n == 4:
                        act.wait_ge(dve_tr, 8)
                    pool_evac(n // 2 - 2)
                    if n < 10:
                        pool_w_high(n // 2 - 1)

            for n in range(8):
                run(SEG_P, n, ev_p)
                pool_steps(n)

            def sigmoid(dst, col):
                def ev(n, i, b):
                    act.activation(dst[:, n, :], Z[i][:, :], ACT.Sigmoid, bias=pcol[:, col + n:col + n + 1]).then_inc(act_z, 1)
                return ev

            ev_gb = sigmoid(m_b, 32)
            act.wait_ge(pe_mod, 24)
            for n in range(8):
                run(SEG_GB, n, ev_gb)
                if n == 0:
                    pool_steps(8)
                if n == 2:
                    pool_evac(3)
                if n == 6:
                    act.wait_ge(dve_st, 2)
                    act.activation(rs[:, 1, :], rs[:, 0, :], ACT.Sqrt).then_inc(act_sq, 1)
            for n in range(8):
                run(SEG_WB, n)

            def a_high(n):
                act.wait_ge(dve_a, n + 1)
                copy(a_hi[:, n, :], d32[n % 2][:, :]).then_inc(act_ahi, 1)

            def ev_u(n, i, b):
                if n >= 2:
                    act.wait_ge(dve_a, n - 1)
                act.activation(g32[i][:, :], Z[i][:, :], ACT.Gelu_apprx_tanh, bias=pcol[:, n:n + 1]).then_inc(act_z, 1)

            for n in range(8):
                run(SEG_U, n, ev_u)
                if n:
                    a_high(n - 1)

            ev_ga = sigmoid(g_a, 24)
            for n in range(8):
                run(SEG_GA, n, ev_ga)
                if n == 0:
                    a_high(7)

            for n in range(8):
                run(SEG_WA, n)
                act.wait_ge(dve_m, n + 1)
                copy(h_hi[:, n, :], d32[n % 2][:, :]).then_inc(act_mhi, 1)

            def ev_o(n, i, b):
                act.wait_ge(pe_tr, 8 + n - 1)
                for r in range(REQ):
                    x = act.activation(g32[i][:, :].rearrange("p (i r n) -> p i r n", i=TILES, r=REQ)[:, :, r, :],
                                       Z[i][:, SEQ * r:SEQ * r + SEQ].rearrange("p (i n) -> p i n", i=TILES), ACT.Copy,
                                       scale=mod_t[:, 2, n, r:r + 1])
                x.then_inc(act_z, 1)

            act.wait_ge(dve_col, 2)
            for n in range(8):
                run(SEG_WO, n, ev_o)
            for k in range(2):
                act.wait_ge(dve_st, 3 + k)
                act.activation(rs[:, 1, :], rs[:, 0, :], ACT.Sqrt).then_inc(act_sq, 1)
            for i in range(TILES):
                for hb in range(2):
                    act.wait_ge(pe_rt, 2 * i + hb + 1)
                    if i >= 2:
                        act.wait_ge(pe_lg, i - 1)
                    copy(h2_t[i % 2][:, 4 * hb:4 * hb + 4, :], TR[hb][:, :].rearrange("p (k n) -> p k n", k=4)).then_inc(act_rt, 1)
            act.wait_ge(dve_st, 5)
            act.activation(q1[:, 2:6, :].rearrange("p k i -> p (k i)"), q1[:, 6:10, :].rearrange("p k i -> p (k i)"), ACT.Exp).then_inc(act_rt, 1)
            act.wait_ge(dve_st, 6)
            act.activation(q1[:, 12, :], q1[:, 11, :], ACT.Exp).then_inc(act_rt, 1)
            act.wait_ge(dve_h2, TILES)
            copy(res[:, :, :], res[:, :, :], scale=ALPHA).then_inc(act_res, 1)

            def round_(sm, banks, sgb, ht, y, n, gums, before, yms):
                act.wait_ge(sm["gum"], gums)
                act.activation(sgb[:, :], banks[0][0:CAP, :], ACT.Silu).then_inc(sm["silu"], 1)
                act.wait_ge(sm["htr"], n + 1)
                copy(ht[:, :, :].rearrange("p f c -> p (f c)"), banks[2][:, 0:FC * CAP]).then_inc(sm["ht"], 1)
                act.wait_ge(sm["ym"], yms)
                if not (isinstance(before, int) and before == 0):
                    act.wait_ge(e_st, 32 * before)
                copy(y[:, :], banks[1][:, :]).then_inc(sm["yo"], 1)

            act.sem_inc(m_sem["yo"], 1)
            act.sem_inc(x_sem["yo"], 1)
            act.wait_ge(dve_rt, 3)

            def expert(e):
                more = act.value_load(tab[0:1, 1, bass.ds(e, 1)], min_val=0, max_val=7)
                first = 0 if isinstance(e, int) else act.value_load(tab[0:1, 2, bass.ds(e, 1)], min_val=0, max_val=16)
                round_(m_sem, (B[0], B[1], B[3]), sg, hid_t, yout, e, e + 1, e + first, e + 1)
                with act.If(more > 0):
                    with act.Fori(0, more) as r:
                        turns = act.snap(first + r)
                        round_(x_sem, (B[4], B[5], B[7]), sg_x, hid_t_x, yout_x, turns, turns + 2, e + 1 + turns, turns + 2)

            expert(0)
            with act.Fori(1, NEXP) as e:
                expert(e)
            def second(i):
                act.wait_ge(f_g[i], 32)
                copy(y_second[i][:, :], y_second[i][:, :], scale=route_w[:, 1, i:i + 1]).then_inc(f_t, 1)

            def root(k):
                act.wait_ge(dve_st, 7 + k)
                act.activation(rs[:, 1, 2 * k:2 * k + 2], rs[:, 0, 2 * k:2 * k + 2], ACT.Sqrt).then_inc(act_sq, 1)

            second(0)
            second(1)
            root(0)
            second(2)
            second(3)
            for i in range(2):
                act.wait_ge(dve_nb, 1)
                act.activation(y_first[i][:, :], y_first[i][:, :], ACT.Identity, scale=rs[:, 2, i:i + 1],
                               bias=rs[:, 4, i:i + 1]).then_inc(act_f, 1)
            root(1)
            for i in range(TILES):
                act.wait_ge(pool_f if i < 2 else f_o, i % 2 + 1)
                for r, y in enumerate((y_prompt, y_sample)):
                    act.dma_start(y[0, HALF * i:HALF * i + HALF, :], y_first[i][HALF * r:HALF * r + HALF, :]).then_inc(s_out, 16)
            act.wait_ge(s_out, 32 * TILES)

        @block.vector
        def _(dve):
            ch = Chain(dve, dve_c)

            def link(ins):
                ch.did(ins)
                ch.sync()

            sq = [0]

            def rstd(first, w):
                c = slice(first, first + w)
                ch.sync()
                dve.tensor_scalar(rs[:, 0, c], mv[:, c, 1], EPS, None, ALU.add).then_inc(dve_st, 1)
                sq[0] += 1
                dve.wait_ge(act_sq, sq[0])
                link(dve.reciprocal(rs[:, 2, c], rs[:, 1, c]))
                link(dve.tensor_tensor(rs[:, 3, c], rs[:, 2, c], rs[:, 2, c], ALU.mult))
                link(dve.tensor_tensor(rs[:, 3, c], rs[:, 3, c], rs[:, 0, c], ALU.mult))
                link(dve.tensor_scalar(rs[:, 3, c], rs[:, 3, c], -0.5, 1.5, ALU.mult, ALU.add))
                link(dve.tensor_tensor(rs[:, 2, c], rs[:, 2, c], rs[:, 3, c], ALU.mult))

            def stats(src, i):
                for hb in range(2):
                    ch.did(dve.bn_stats(st[:, i, hb, :], src[:, 512 * hb:512 * hb + 512]))
                ch.sync()
                ch.did(dve.bn_aggr(mv[:, i, :], st[:, i, :, :].rearrange("p a b -> p (a b)")))

            dve.wait_ge(pe_pro, 1)
            dve.tensor_copy(pcol[:, :], COL[:, 0:64]).then_inc(dve_pro, 1)
            dve.wait_ge(s_x, 32)
            for i in range(TILES):
                stats(xin[:, i, :], i)
            rstd(0, TILES)
            for i in range(TILES):
                dve.tensor_scalar(xin[:, i, :], xin[:, i, :], mv[:, i, 0:1], rs[:, 2, i:i + 1],
                                  ALU.subtract, ALU.mult).then_inc(dve_n, 1)
            dve.wait_ge(pe_pro, 2)
            for hb in range(2):
                x = dve.tensor_copy(ws_t[:, 4 * hb:4 * hb + 4, :], MX[hb][:, :].rearrange("p (k n) -> p k n", k=4))
            x.then_inc(dve_pro, 1)
            dve.wait_ge(s_bmod, 128)

            def mod_rows(g, done):
                dve.wait_ge(pe_mod, 8 * (g + 1))
                for j in range(4):
                    rows = modrow[32 * j:32 * j + 2, g, :]
                    x = dve.tensor_tensor(rows, MOD[32 * j:32 * j + 2, :], rows, ALU.add)
                    if g == 0 or j == 3:
                        x.then_inc(done, 1)

            def mod_cols(g, tiles):
                n = 8 * tiles
                dve.wait_ge(pe_modcol, 4 * g + tiles)
                dve.tensor_copy(mod_t[:, 2 * g:2 * g + tiles // 2, :, :].rearrange("p v k r -> p (v k r)"), COL[:, 0:n]).then_inc(dve_col, 1)

            def split_lo(b):
                u = b // 4
                par = b % 2
                dve.wait_ge(act_whi, b + 1)
                dve.tensor_tensor(w_lo[par][:, :, :], raw[:, u % 2, :, 128 * (b % 4):128 * (b % 4) + 128],
                                  w_hi[par][:, :, :].bitcast(f32), ALU.subtract).then_inc(dve_wlo, 1)

            mod_rows(0, dve_row0)
            dve.wait_ge(act_nt, 8)
            mod_cols(0, 4)
            dve.wait_ge(dve_col, 1)
            dve.tensor_scalar(scale1p[:, :, :].rearrange("p k r -> p (k r)"),
                              mod_t[:, 1, :, :].rearrange("p k r -> p (k r)"), 1.0, None, ALU.add).then_inc(dve_aff, 1)
            dve.wait_ge(dve_aff, 1)
            split_lo(0)

            def h_low(kc):
                dve.tensor_tensor(h_lo[:, kc, :], n_t[:, kc, :], h_hi[:, kc, :].bitcast(f32), ALU.subtract).then_inc(dve_hlo, 1)

            for kc in range(KC):
                dve.wait_ge(act_hhi, kc + 1)
                if kc:
                    dve.wait_ge(dve_aff, kc + 1)
                for r in range(REQ):
                    part = n_t[:, kc, SEQ * r:SEQ * r + SEQ]
                    x = dve.tensor_scalar(part, part, scale1p[:, kc, r:r + 1], mod_t[:, 0, kc, r:r + 1], ALU.mult, ALU.add)
                x.then_inc(dve_aff, 1)
                if kc:
                    h_low(kc - 1)
            dve.wait_ge(dve_aff, KC + 1)
            h_low(KC - 1)

            def v_rows(n):
                dve.wait_ge(pe_tr, n + 1)
                dve.tensor_copy(v_nat[:, :, 128 * n:128 * n + 128],
                                TR[n % 2][:, :].rearrange("p (c n) -> p c n", c=TILES)).then_inc(dve_tr, 1)

            for n in range(8):
                split_lo(n + 1)
                if n:
                    v_rows(n - 1)
            mod_rows(1, dve_row)

            def centred(n):
                g = n // 2
                w = WINDOWS[g]
                dve.wait_ge(pool_win, n + 1)
                dve.wait_ge(act_z, 8 + n + 1)
                if n >= 2:
                    dve.wait_ge(dve_dlo, n - 1)
                dve.scalar_tensor_tensor(out=d32[n % 2][:, :].rearrange("p (r s) -> p r s", r=REQ),
                                         in0=wsum[(g + 1) % 2][:, :, 8 - w // 2:8 - w // 2 + SEQ], scalar=1.0 / w,
                                         in1=zpad[n % 2][:, :, 8:8 + SEQ], op0=ALU.mult, op1=ALU.subtract).then_inc(dve_d, 1)

            def d_low(n):
                dve.wait_ge(act_dhi, n + 1)
                dve.tensor_tensor(d_lo[:, n % 2, :], d32[n % 2][:, :], d_hi[:, n % 2, :].bitcast(f32), ALU.subtract).then_inc(dve_dlo, 1)

            def pool_w_low(g):
                dve.wait_ge(act_wphi, g + 1)
                dve.tensor_tensor(wp_lo[:, :, :], wp_raw[:, g, :, :], wp_hi[:, :, :].bitcast(f32), ALU.subtract).then_inc(dve_wplo, 1)

            def pool_low(g):
                for o in range(2):
                    dve.wait_ge(act_phi, 2 * g + o + 1)
                    dve.tensor_tensor(a_lo[:, 2 * g + o, :], g32[o][:, :], a_hi[:, 2 * g + o, :].bitcast(f32),
                                      ALU.subtract).then_inc(dve_plo, 1)

            def pool_steps(n):
                if n >= 2:
                    d_low(n - 2)
                if n >= 5 and n % 2 == 1:
                    pool_low((n - 5) // 2)
                if 1 <= n <= 8:
                    centred(n - 1)

            for n in range(8):
                split_lo(9 + n)
                if n == 0:
                    v_rows(7)
                if n == 2:
                    pool_w_low(0)
                if n >= 5 and n % 2 == 1:
                    pool_w_low(n // 2 - 1)
                pool_steps(n)
            def v_norm(i):
                row = v_nat[:, i, :]
                link(dve.scalar_tensor_tensor(out=row, in0=row, scalar=mv[:, i, 0:1], in1=sgu_bc[:, 0, :], op0=ALU.subtract, op1=ALU.mult))
                dve.scalar_tensor_tensor(out=row, in0=row, scalar=rs[:, 2, i:i + 1], in1=sgu_bc[:, 1, :],
                                         op0=ALU.mult, op1=ALU.add).then_inc(dve_vln, 1)

            for n in range(8):
                split_lo(17 + n)
                if n == 0:
                    pool_steps(8)
                if n == 1:
                    pool_w_low(3)
                    pool_steps(9)
                if n == 2:
                    mod_rows(2, dve_row)
                if n == 3:
                    pool_low(3)
                    dve.wait_ge(dve_row, 2)
                    for j in range(2):
                        rows = modrow[32 * j:32 * j + 2, 2, :]
                        x = dve.tensor_scalar(rows, rows, 1.0, None, ALU.add)
                    x.then_inc(dve_row, 1)
                if n in (4, 5):
                    if n == 4:
                        dve.wait_ge(dve_tr, 8)
                    stats(v_nat[:, 2 * n - 8, :], 2 * n - 8)
                    stats(v_nat[:, 2 * n - 7, :], 2 * n - 7)
                if n == 5:
                    mod_cols(1, 2)
                if n == 6:
                    rstd(0, TILES)
                    dve.wait_ge(s_sgu, 32)
                if n == 7:
                    v_norm(0)
            for n in range(8):
                b = 24 + n
                split_lo(b + 1)
                dve.wait_ge(pe_blk, b + 1)
                dve.wait_ge(act_z, 16 + n + 1)
                dve.tensor_tensor(m_b[:, n, :], Z[n % 2][:, :], m_b[:, n, :], ALU.mult).then_inc(dve_z, 1)
                if n < TILES - 1:
                    v_norm(n + 1)
            dve.wait_ge(s_bs, 16)

            def a_low(n):
                dve.wait_ge(act_ahi, n + 1)
                dve.tensor_tensor(a_lo[:, n, :], d32[n % 2][:, :], a_hi[:, n, :].bitcast(f32), ALU.subtract).then_inc(dve_alo, 1)

            for n in range(8):
                b = 32 + n
                split_lo(b + 1)
                if n:
                    a_low(n - 1)
                dve.wait_ge(pe_mix, n + 1)
                if n >= 2:
                    dve.wait_ge(dve_alo, n - 1)
                bias = bs_bc[:, n:n + 1, :].broadcast_to([128, TILES, 128])
                out = d32[n % 2][:, :].rearrange("p (c n) -> p c n", c=TILES)
                link(dve.tensor_tensor(out, MX[n % 2][:, :].rearrange("p (c n) -> p c n", c=TILES), bias, ALU.add))
                dve.wait_ge(act_z, 24 + n + 1)
                dve.tensor_tensor(d32[n % 2][:, :], d32[n % 2][:, :], g32[n % 2][:, :], ALU.mult).then_inc(dve_a, 1)
            for n in range(8):
                split_lo(41 + n)
                if n == 0:
                    a_low(7)
            dve.wait_ge(dve_alo, 8)
            for n in range(8):
                b = 48 + n
                split_lo(b + 1)
                dve.wait_ge(pe_blk, b + 1)
                dve.wait_ge(act_z, 32 + n + 1)
                if n >= 2:
                    dve.wait_ge(dve_mlo, n - 1)
                dve.tensor_tensor(g_a[:, n, :], Z[n % 2][:, :], g_a[:, n, :], ALU.mult).then_inc(dve_z, 1)
                dve.wait_ge(dve_z, 8 + n + 1)
                dve.tensor_tensor(d32[n % 2][:, :], g_a[:, n, :], m_b[:, n, :], ALU.add).then_inc(dve_m, 1)
                dve.wait_ge(act_mhi, n + 1)
                dve.tensor_tensor(h_lo[:, n, :], d32[n % 2][:, :], h_hi[:, n, :].bitcast(f32), ALU.subtract).then_inc(dve_mlo, 1)
            def block_stats(n):
                dve.wait_ge(dve_tr, 8 + n + 1)
                for i in range(TILES):
                    ch.did(dve.bn_stats(st8[:, i, n, :], res[:, i, 128 * n:128 * n + 128]))

            dve.wait_ge(s_xres, 32)
            def residual(n):
                dve.wait_ge(pe_tr, 8 + n + 1)
                part = res[:, :, 128 * n:128 * n + 128]
                dve.scalar_tensor_tensor(out=part, in0=part, scalar=ALPHA, in1=TR[n % 2][:, :].rearrange("p (c n) -> p c n", c=TILES),
                                         op0=ALU.mult, op1=ALU.add).then_inc(dve_tr, 1)

            for n in range(8):
                if n < 7:
                    split_lo(57 + n)
                if n >= 2:
                    block_stats(n - 2)
                if n:
                    residual(n - 1)
            residual(7)
            block_stats(6)
            block_stats(KC - 1)
            ch.sync()
            for i in range(TILES):
                ch.did(dve.bn_aggr(mv[:, i, :], st8[:, i, :, :].rearrange("p a b -> p (a b)")))
            rstd(0, TILES)
            dve.wait_ge(s_ln1, 32)
            for i in range(TILES):
                row = res[:, i, :]
                link(dve.scalar_tensor_tensor(out=row, in0=row, scalar=mv[:, i, 0:1], in1=ln1_bc[:, 0, :], op0=ALU.subtract, op1=ALU.mult))
                link(dve.scalar_tensor_tensor(out=row, in0=row, scalar=rs[:, 2, i:i + 1], in1=ln1_bc[:, 1, :], op0=ALU.mult, op1=ALU.add))
                stats(row, i)
            rstd(0, TILES)
            dve.wait_ge(pe_bc, 2)
            for i in range(TILES):
                for c in range(2):
                    part = slice(512 * c, 512 * c + 512)
                    ch.did(dve.scalar_tensor_tensor(out=h2[:, i, part], in0=res[:, i, part], scalar=mv[:, i, 0:1], in1=B[4 + c][:, :],
                                                    op0=ALU.subtract, op1=ALU.mult))
                ch.sync()
                for c in range(2):
                    part = h2[:, i, 512 * c:512 * c + 512]
                    x = dve.scalar_tensor_tensor(out=part, in0=part, scalar=rs[:, 2, i:i + 1], in1=B[6 + c][:, :], op0=ALU.mult, op1=ALU.add)
                x.then_inc(dve_h2, 1)
            dve.wait_ge(pe_lg, TILES)
            NL = NGRP + NEXP
            link(dve.tensor_tensor(lg[:, :, :], B[0][:, 0:256].rearrange("p (i n) -> p i n", i=TILES)[:, :, 0:NL],
                                   br_bc[:, :].rearrange("p (a n) -> p a n", a=1).broadcast_to([128, TILES, NL]), ALU.add))

            def iota(w):
                return cst[:, C_IOTA:C_IOTA + w].rearrange("p (a n) -> p a n", a=1).broadcast_to([128, TILES, w])

            def col(k, w):
                return q1[:, k, :].rearrange("p (i a) -> p i a", a=1).broadcast_to([128, TILES, w])

            def first_max(src, w, kmax, kidx, tmp, out):
                link(dve.tensor_reduce(q1[:, kmax, :], src, AX.X, ALU.max))
                link(dve.tensor_tensor(tmp, src, col(kmax, w), ALU.is_equal))
                link(dve.scalar_tensor_tensor(out=tmp, in0=tmp, scalar=-64.0, in1=iota(w), op0=ALU.mult, op1=ALU.add))
                link(dve.tensor_reduce(q1[:, kidx, :], tmp, AX.X, ALU.min))
                link(dve.tensor_tensor(out, tmp, col(kidx, w), ALU.is_equal))

            link(dve.memset(both[:, 0, :], 0.0))
            link(dve.tensor_copy(before_m[:, :, :].rearrange("p a n -> p (a n)"), cst[:, C_LT:C_LT + 256]))
            lgg = lg[:, :, 0:NGRP]
            oh_g = q[1][:, :, 0:NGRP]
            first_max(lgg, NGRP, 0, 1, q[0][:, :, 0:NGRP], oh_g)
            dve.tensor_tensor(q1[:, 6:10, :].rearrange("p g i -> p i g"), lgg, col(0, NGRP), ALU.subtract).then_inc(dve_st, 1)
            link(dve.tensor_tensor(seltmp[:, :, :, :], lg[:, :, NGRP:].rearrange("p i (g e) -> p i g e", g=NGRP),
                                   oh_g.rearrange("p i (g a) -> p i g a", a=1).broadcast_to([128, TILES, NGRP, EPG]), ALU.mult))
            link(dve.tensor_reduce(q[2][:, :, :], seltmp[:, :, :, :].rearrange("p i g e -> p i e g"), AX.X, ALU.add))
            first_max(q[2][:, :, :], EPG, 10, 1, q[3][:, :, :], q[4][:, :, :])
            link(dve.scalar_tensor_tensor(out=q[5][:, :, :], in0=q[4][:, :, :], scalar=BIG, in1=q[2][:, :, :], op0=ALU.mult, op1=ALU.add))
            first_max(q[5][:, :, :], EPG, 13, 1, q[3][:, :, :], q[6][:, :, :])
            dve.tensor_tensor(q1[:, 11, :], q1[:, 13, :], q1[:, 10, :], ALU.subtract).then_inc(dve_st, 1)
            for j, oh in enumerate((q[4], q[6])):
                for i in range(TILES):
                    ch.did(dve.tensor_tensor(
                        onehot[:, j, i, :].rearrange("p (g e) -> p g e", g=NGRP),
                        q[1][:, i, 0:NGRP].rearrange("p (g a) -> p g a", a=1).broadcast_to([128, NGRP, EPG]),
                        oh[:, i, :].rearrange("p (a e) -> p a e", a=1).broadcast_to([128, NGRP, EPG]), ALU.mult))
            ch.sync()
            dve.tensor_tensor(both[:, 1:, :], onehot[:, 0, :, :], onehot[:, 1, :, :], ALU.add).then_inc(dve_rt, 1)
            dve.wait_ge(act_rt, 2 * TILES + 1)
            link(dve.tensor_reduce(q1[:, 14, :], q1[:, 2:6, :].rearrange("p g i -> p i g"), AX.X, ALU.add))
            dve.wait_ge(act_rt, 2 * TILES + 2)
            link(dve.tensor_scalar(q1[:, 15, :], q1[:, 12, :], 1.0, None, ALU.add))
            link(dve.tensor_tensor(q1[:, 14, :], q1[:, 14, :], q1[:, 15, :], ALU.mult))
            link(dve.reciprocal(route_w[:, 0, :], q1[:, 14, :]))
            link(dve.tensor_tensor(route_w[:, 1, :], route_w[:, 0, :], q1[:, 12, :], ALU.mult))
            dve.wait_ge(pe_lg, TILES + 1)
            totals = B[1][:, NEXP * TILES:NEXP * TILES + NEXP]
            cum, start = seltmp[:, 0, :, :].rearrange("p a b -> p (a b)"), seltmp[:, 1, :, :].rearrange("p a b -> p (a b)")
            cnt = seltmp[:, 2, :, :].rearrange("p a b -> p (a b)")
            link(dve.tensor_copy(cnt, totals))
            link(dve.tensor_tensor_scan(cum, ones[:, 0:NEXP], cnt, 0.0, ALU.mult, ALU.add))
            link(dve.tensor_tensor(start, cum, cnt, ALU.subtract))
            link(dve.tensor_tensor(place[:, :, :], B[1][:, 0:NEXP * TILES].rearrange("p (i n) -> p i n", i=TILES),
                                   start.rearrange("p (a n) -> p a n", a=1).broadcast_to([128, TILES, NEXP]), ALU.add))
            for j in range(2):
                link(dve.tensor_tensor(onehot[:, j, :, :], onehot[:, j, :, :], place[:, :, :], ALU.mult))
                link(dve.tensor_reduce(q1[:, j, :], onehot[:, j, :, :], AX.X, ALU.add))
                x = dve.tensor_copy(pos[:, j, :], q1[:, j, :])
                if j == 0:
                    link(x)
            x.then_inc(dve_rt, 1)
            link(dve.memset(tab[0:1, :, :], 0))
            link(dve.tensor_copy(tab[0:1, 0, 0:NEXP], start[0:1, :]))
            link(dve.tensor_scalar(trow[:, 0, :], cnt[0:1, :], float(CAP), None, ALU.is_gt))
            for k in range(2, 8):
                link(dve.scalar_tensor_tensor(out=trow[:, 0, :], in0=cnt[0:1, :], scalar=float(CAP * k), in1=trow[:, 0, :],
                                              op0=ALU.is_gt, op1=ALU.add))
            link(dve.tensor_tensor_scan(trow[:, 1, :], ones[0:1, 0:NEXP], trow[:, 0, :], 0.0, ALU.mult, ALU.add))
            link(dve.tensor_tensor(trow[:, 2, :], trow[:, 1, :], trow[:, 0, :], ALU.subtract))
            link(dve.tensor_copy(tab[0:1, 1, 0:NEXP], trow[:, 0, :]))
            link(dve.tensor_copy(tab[0:1, 2, 0:NEXP], trow[:, 2, :]))
            dve.tensor_copy(tab[0:1, 2, NEXP:NEXP + 1], trow[:, 1, NEXP - 1:NEXP]).then_inc(dve_rt, 1)
            dve.wait_ge(dve_rt, 3)
            dve.wait_ge(s_scat, 16 * 8)
            dve.wait_ge(m_sem["xtr"], 1)
            dve.tensor_copy(x_t[0][:, :, :].rearrange("p k c -> p (k c)"), B[2][:, :]).then_inc(m_sem["xt"], 1)

            def expert(e, s, last=False):
                dve.wait_ge(m_sem["silu"], e + 1)
                dve.tensor_tensor(hid[:, :], B[0][CAP:128, :], sg[:, :], ALU.mult).then_inc(m_sem["hid"], 1)
                if not last:
                    dve.wait_ge(m_sem["xtr"], e + 2)
                    dve.tensor_copy(x_t[(s + 1) % 3][:, :, :].rearrange("p k c -> p (k c)"), B[2][:, :]).then_inc(m_sem["xt"], 1)
                more = dve.value_load(tab[0:1, 1, bass.ds(e, 1)], min_val=0, max_val=7)
                first = dve.value_load(tab[0:1, 2, bass.ds(e, 1)], min_val=0, max_val=16)
                with dve.If(more > 0):
                    with dve.Fori(0, more) as r:
                        turns = dve.snap(first + r)
                        dve.wait_ge(x_sem["xtr"], turns + 2)
                        dve.tensor_copy(x_t_x[:, :, :].rearrange("p k c -> p (k c)"), B[6][:, :]).then_inc(x_sem["xt"], 1)
                        dve.wait_ge(x_sem["silu"], turns + 1)
                        dve.tensor_tensor(hid_x[:, :], B[4][CAP:128, :], sg_x[:, :], ALU.mult).then_inc(x_sem["hid"], 1)

            with dve.Fori(0, 10) as t:
                for k in range(3):
                    expert(3 * t + k, k)
            expert(30, 0)
            expert(31, 1, last=True)
            dve.wait_ge(pe_bc, 3)
            dve.wait_ge(s_ln2, 32)
            dve.wait_ge(act_res, 1)

            def combine(i):
                y = y_first[i]
                dve.wait_ge(f_t, i + 1)
                link(dve.scalar_tensor_tensor(out=y[:, :], in0=y[:, :], scalar=route_w[:, 0, i:i + 1], in1=y_second[i][:, :],
                                              op0=ALU.mult, op1=ALU.add))
                for c, bank in enumerate((B[0], B[2])):
                    part = y[:, 512 * c:512 * c + 512]
                    ch.did(dve.tensor_tensor(part, bank[:, :], part, ALU.mult))
                ch.sync()
                link(dve.tensor_tensor(y[:, :], res[:, i, :], y[:, :], ALU.add))
                stats(y, i)

            combine(0)
            combine(1)
            rstd(0, 2)
            for i in range(2):
                x = dve.scalar_tensor_tensor(out=rs[:, 4, i:i + 1], in0=mv[:, i, 0:1], scalar=-1.0, in1=rs[:, 2, i:i + 1],
                                             op0=ALU.mult, op1=ALU.mult)
            x.then_inc(dve_nb, 1)
            for i in range(2):
                combine(2 + i)
                dve.wait_ge(act_f, i + 1)
                dve.tensor_tensor(y_first[i][:, :], y_first[i][:, :], ln2_bc[:, 0, :], ALU.mult).then_inc(f_m, 1)
            rstd(2, 2)
            for i in range(2, TILES):
                y = y_first[i]
                link(dve.scalar_tensor_tensor(out=y[:, :], in0=y[:, :], scalar=mv[:, i, 0:1], in1=ln2_bc[:, 0, :], op0=ALU.subtract, op1=ALU.mult))
                dve.scalar_tensor_tensor(out=y[:, :], in0=y[:, :], scalar=rs[:, 2, i:i + 1], in1=ln2_bc[:, 1, :],
                                         op0=ALU.mult, op1=ALU.add).then_inc(f_o, 1)


_INS = ["x_prompt", "x_sample", "c_prompt", "c_sample", "w_mod", "b_mod", "w_in", "b_in", "w_spatial",
        "b_spatial", "sgu_g", "sgu_b", "w_pool", "pool_scale", "w_branch_a", "w_branch_b", "w_out",
        "ln1_g", "ln1_b", "w_router_group", "b_router_group", "w_router_expert", "b_router_expert",
        "w_exp_gate", "w_exp_up", "w_exp_down", "ln2_g", "ln2_b"]


def constants():
    import numpy as np

    c = np.zeros((128, C_END), np.float32)
    c[:, C_ID:C_ID + 128] = np.eye(128)
    c[:, C_LT:C_LT + 128] = np.triu(np.ones((128, 128)), 1)
    c[:, C_ONE:C_ONE + 128] = 1.0
    for j in range(4):
        for r in range(REQ):
            c[32 * j + r, C_SEL + 64 * r:C_SEL + 64 * r + 64] = 1.0
    for g, w in enumerate(WINDOWS):
        h = w // 2
        for k in range(h):
            c[:, C_EDGE + 16 * g + k] = w / (k + h)
        for k in range(h - 1):
            c[:, C_EDGE + 16 * g + 8 + k] = w / (SEQ - (SEQ - h + 1 + k) + h)
    c[:, C_IOTA:C_IOTA + 8] = np.arange(8)
    return c


def kernel(**inputs):
    import numpy as _np
    import concourse.bacc as _bacc
    from concourse import mybir as _mybir
    from concourse.bass_utils import run_bass_kernel_spmd as _run

    nc = _bacc.Bacc("TRN2", target_bir_lowering=False, num_devices=1)
    arrays, args = {}, []
    for name in _INS:
        a = _np.ascontiguousarray(inputs[name])
        arrays[f"in_{name}"] = a
        args.append(nc.dram_tensor(f"in_{name}", a.shape, _mybir.dt.from_np(a.dtype), kind="ExternalInput").ap())
    arrays["in_consts"] = constants()
    args.append(nc.dram_tensor("in_consts", (128, C_END), _mybir.dt.float32, kind="ExternalInput").ap())
    for i in range(REQ):
        args.append(nc.dram_tensor(f"out_{i}", (1, SEQ, D), _mybir.dt.float32, kind="ExternalOutput").ap())
    hybrid_encoder(nc, *args)
    r = _run(nc, [arrays], core_ids=[0])
    return tuple(r.results[0][f"out_{i}"] for i in range(REQ))
```

```python
import concourse.bass as bass
from concourse import mybir
from contextlib import ExitStack

D = 1024
REQ = 2
SEQ = 256
TOK = REQ * SEQ
KC = D // 128
TILES = TOK // 128
HALF = 64
D_IN = 5 * D
NEXP = 32
NGRP = 4
EPG = NEXP // NGRP
DE = D // 2
FC = DE // 128
CAP = 64
ASSIGN = 2 * TOK
FURTHER = ASSIGN // CAP
LAST_ROW = (NEXP + FURTHER) * CAP
ROUNDS = NEXP + FURTHER + 8
WINDOWS = (2, 4, 8, 16)
ALPHA = 2.0 ** 0.25
EPS = 1e-5
BIG = -3.0e38

C_ID, C_LT, C_ONE, C_SEL, C_EDGE, C_IOTA, C_END = 0, 128, 256, 384, 512, 576, 608

SEG_V, SEG_P, SEG_GB, SEG_WB, SEG_U, SEG_GA, SEG_WA, SEG_WO = range(8)
NBLK = 64


def hybrid_encoder(nc, x_prompt, x_sample, c_prompt, c_sample, w_mod, b_mod, w_in, b_in, w_spatial,
                   b_spatial, sgu_g, sgu_b, w_pool, pool_scale, w_branch_a, w_branch_b, w_out,
                   ln1_g, ln1_b, w_router_group, b_router_group, w_router_expert, b_router_expert,
                   w_exp_gate, w_exp_up, w_exp_down, ln2_g, ln2_b, consts, y_prompt, y_sample):
    bf16, f32, f32r, i32, u32 = mybir.dt.bfloat16, mybir.dt.float32, mybir.dt.float32r, mybir.dt.int32, mybir.dt.uint32
    ALU, ACT, AX = mybir.AluOpType, mybir.ActivationFunctionType, mybir.AxisListType

    packed_x = nc.dram_tensor("packed_x", (ASSIGN + 8 * CAP, D), f32).ap()
    round_y = nc.dram_tensor("round_y", (ROUNDS * CAP, D), f32).ap()

    ctx = ExitStack()
    with ctx:
        base = (nc.sbuf_base + 63) // 64 * 64

        def at(name, shape, dt, off):
            return nc.alloc_sbuf_tensor_at(name, shape, dt, offset=base + off)

        def sem(name):
            return ctx.enter_context(nc.semaphore(name))

        K = 1024
        SLOT = 48 * K
        R0 = 3 * SLOT
        S0 = R0 + 16 * K
        gate_w = [at(f"gate_w{s}", [128, KC, DE], f32, s * SLOT) for s in range(3)]
        up_w = [at(f"up_w{s}", [128, KC, DE], f32, s * SLOT + 16 * K) for s in range(3)]
        down_w = [at(f"down_w{s}", [128, FC, D], f32, s * SLOT + 32 * K) for s in range(3)]
        a_hi = at("a_hi", [128, KC, TOK], f32r, 0)
        a_lo = at("a_lo", [128, KC, TOK], f32r, 16 * K)
        xin = at("xin", [128, TILES, D], f32, 0)
        ws_raw = at("ws_raw", [128, 8, 128], f32, 16 * K)
        v_nat = at("v_nat", [128, TILES, D], f32, 32 * K)
        g_a = at("g_a", [128, KC, TOK], f32, 32 * K)
        raw = at("raw", [128, 2, KC, 512], f32, SLOT)
        modraw0 = at("modraw0", [128, 4, 4, 512], f32, SLOT)
        m_b = at("m_b", [128, KC, TOK], f32, SLOT + 32 * K)
        modraw = at("modraw", [128, 2, 4, 512], f32, SLOT + 32 * K)
        h_hi = at("h_hi", [128, KC, TOK], f32r, 2 * SLOT)
        h_lo = at("h_lo", [128, KC, TOK], f32r, 2 * SLOT + 16 * K)
        w_hi = [at(f"w_hi{i}", [128, KC, 128], f32r, 2 * SLOT + 32 * K + i * 8 * K) for i in range(2)]
        w_lo = [at(f"w_lo{i}", [128, KC, 128], f32r, 2 * SLOT + 36 * K + i * 8 * K) for i in range(2)]
        ln2_bc = at("ln2_bc", [128, 2, D], f32, 2 * SLOT)
        y_first = [at(f"y_first{i}", [128, D], f32, 2 * SLOT + (8 + 4 * i) * K) for i in range(TILES)]
        y_second = [at(f"y_second{i}", [128, D], f32, 2 * SLOT + (24 + 4 * i) * K) for i in range(TILES)]
        n_t = at("n_t", [128, KC, TOK], f32, R0)
        wp_raw = at("wp_raw", [128, 4, 2, 256], f32, R0)
        bs_bc = at("bs_bc", [128, 8, 128], f32, R0 + 8 * K)
        res = at("res", [128, TILES, D], f32, R0)
        cst = at("cst", [128, C_END], f32, S0)
        pcol = at("pcol", [128, 64], f32, S0 + 2432)
        mod_t = at("mod_t", [128, 6, KC, REQ], f32, S0 + 2688)
        scale1p = at("scale1p", [128, KC, REQ], f32, S0 + 3072)
        silu_c = at("silu_c", [128, REQ, KC], f32, S0 + 3136)
        st = at("st", [128, TILES, 2, 6], f32, S0 + 3200)
        mv = at("mv", [128, TILES, 2], f32, S0 + 3392)
        mv2 = at("mv2", [128, TILES, 2], f32, S0 + 3552)
        rs = at("rs", [128, 8, TILES], f32, S0 + 3424)
        modrow = at("modrow", [128, 3, 512], f32, S0 + 3584)
        prow = at("prow", [64, 128], f32, S0 + 9728 + 31232)
        route_w = at("route_w", [128, 2, TILES], f32, S0 + 2432)
        pos = at("pos", [128, 2, TILES], u32, S0 + 2464)
        pos_y = at("pos_y", [128, 2, TILES], u32, S0 + 2496)
        tab = at("tab", [1, 5, NEXP + 1], i32, S0 + 2528)
        few = at("few", [1, NEXP], i32, S0 + 7680)
        T0 = S0 + 9728
        ws_t = at("ws_t", [128, 8, 128], f32, T0)
        wp_hi = at("wp_hi", [128, 2, 256], f32r, T0 + 4096)
        wp_lo = at("wp_lo", [128, 2, 256], f32r, T0 + 6144)
        PADW = SEQ + 16
        zrow = at("zrow", [128, 512], f32, T0 + 4096)
        zpad = [at(f"zpad{i}", [128, REQ, PADW], f32, T0 + 8192 + 2176 * i) for i in range(2)]
        wsum = [at(f"wsum{i}", [128, REQ, PADW], f32, T0 + 12544 + 2176 * i) for i in range(2)]
        sgu_bc = at("sgu_bc", [128, 2, D], f32, T0 + 8192)
        d32 = [at(f"d32_{i}", [128, TOK], f32, T0 + 16896 + 2048 * i) for i in range(2)]
        d_hi = at("d_hi", [128, 2, TOK], f32r, T0 + 20992)
        d_lo = at("d_lo", [128, 2, TOK], f32r, T0 + 25088)
        g32 = [at(f"g32_{i}", [128, TOK], f32, T0 + 29184 + 2048 * i) for i in range(2)]
        ln1_bc = at("ln1_bc", [128, 2, D], f32, T0)
        h2 = at("h2", [128, TILES, D], f32, T0 + 8192)
        h2_t = [at(f"h2_t{i}", [128, KC, 128], f32, T0 + 24576 + 4096 * i) for i in range(2)]
        wr = at("wr", [128, KC, NGRP + NEXP], f32, T0 + 33280)
        Q0 = T0 + 34432
        br_bc = at("br_bc", [128, NGRP + NEXP], f32, Q0)
        lg = at("lg", [128, TILES, NGRP + NEXP], f32, Q0 + 160)
        onehot = at("onehot", [128, 2, TILES, NEXP], f32, Q0 + 736)
        st8 = at("st8", [128, TILES, KC, 6], f32, Q0 + 736)
        both = at("both", [128, TILES + 1, NEXP], bf16, Q0 + 1760)
        place = at("place", [128, TILES, NEXP], f32, T0)
        seltmp = at("seltmp", [128, TILES, NGRP, EPG], f32, Q0 + 2272)
        q = [at(f"q{i}", [128, TILES, EPG], f32, Q0 + 2784 + 128 * i) for i in range(7)]
        q1 = at("q1", [128, 16, TILES], f32, Q0 + 3680)
        prod = at("prod", [128, TILES, NEXP], f32, T0 + 1024)
        rounds = at("rounds", [128, 5, NEXP], f32, T0 + 1536)
        slots = at("slots", [128, CAP], f32, T0 + 2176)
        sel = [at(f"sel{j}", [128, TILES, CAP], f32, T0 + 2432 + 1024 * j) for j in range(2)]
        before_m = at("before_m", [128, 2, 128], bf16, T0 + 512)
        assert Q0 + 3936 + base <= nc.sbuf_usable_end
        xrows = [at(f"xrows{i}", [CAP, D], f32, T0 + 4096 * i) for i in range(3)]
        x_t = [at(f"x_t{i}", [128, KC, CAP], f32, T0 + o) for i, o in enumerate((29696, 14336, 16384))]
        sg = at("sg", [CAP, DE], f32, T0 + 18432)
        hid = at("hid", [CAP, DE], f32, T0 + 20480)
        hid_t = at("hid_t", [128, FC, CAP], f32, T0 + 22528)
        yout = [at(f"yout{i}", [128, 512], f32, o) for i, o in enumerate((T0 + 23552, S0 + 3584, S0 + 5632))]
        xrows_x = at("xrows_x", [CAP, D], f32, T0 + 25600)
        x_t_x = at("x_t_x", [128, KC, CAP], f32, T0 + 12288)
        sg_x = at("sg_x", [CAP, DE], f32, T0 + 31744)
        hid_x = at("hid_x", [CAP, DE], f32, T0 + 33792)
        hid_t_x = at("hid_t_x", [128, FC, CAP], f32, T0 + 35840)
        yout_x = at("yout_x", [128, 512], f32, T0 + 36864)

        B = [ctx.enter_context(nc.psum_tensor(f"bank{i}", [128, 512], f32)) for i in range(8)]
        Z = B[0:2]
        TR = B[2:4]
        MX = B[4:6]
        MOD = B[6]
        COL = B[7]
        COLS = (B[7], B[3], B[2], B[1])

        ident = cst[:, C_ID:C_ID + 128]
        ones = cst[:, C_ONE:C_ONE + 128]

        s_param = sem("s_param")
        s_x = sem("s_x")
        s_ws = sem("s_ws")
        s_bmod = sem("s_bmod")
        s_m0 = [sem(f"s_m0_{i}") for i in range(4)]
        s_m = [sem(f"s_m{i}") for i in range(2)]
        s_w = [sem(f"s_w{i}") for i in range(2)]
        s_bs = sem("s_bs")
        s_wp = sem("s_wp")
        s_sgu = sem("s_sgu")
        s_xres = sem("s_xres")
        s_ln1 = sem("s_ln1")
        s_wr = sem("s_wr")
        s_ln2 = sem("s_ln2")
        s_zero = sem("s_zero")
        s_scat = sem("s_scat")
        s_out = sem("s_out")

        pe_pro = sem("pe_pro")
        pe_xt = sem("pe_xt")
        pe_mod = sem("pe_mod")
        pe_modcol = sem("pe_modcol")
        pe_blk = sem("pe_blk")
        pe_tr = sem("pe_tr")
        pe_pool = sem("pe_pool")
        pe_mix = sem("pe_mix")
        pe_rt = sem("pe_rt")
        pe_lg = sem("pe_lg")
        pe_bc = sem("pe_bc")
        act_pro = sem("act_pro")
        act_nt = sem("act_nt")
        act_hhi = sem("act_hhi")
        act_whi = sem("act_whi")
        act_z = sem("act_z")
        act_dhi = sem("act_dhi")
        act_wphi = sem("act_wphi")
        act_pt = sem("act_pt")
        act_phi = sem("act_phi")
        act_ahi = sem("act_ahi")
        act_mhi = sem("act_mhi")
        act_sq = sem("act_sq")
        act_rt = sem("act_rt")
        act_res = sem("act_res")
        act_f = sem("act_f")
        dve_c = sem("dve_c")
        dve_pro = sem("dve_pro")
        dve_st = sem("dve_st")
        dve_n = sem("dve_n")
        dve_row = sem("dve_row")
        dve_row0 = sem("dve_row0")
        dve_col = sem("dve_col")
        dve_aff = sem("dve_aff")
        dve_hlo = sem("dve_hlo")
        dve_wlo = sem("dve_wlo")
        dve_z = sem("dve_z")
        dve_tr = sem("dve_tr")
        dve_d = sem("dve_d")
        dve_dlo = sem("dve_dlo")
        dve_wplo = sem("dve_wplo")
        dve_plo = sem("dve_plo")
        dve_vln = sem("dve_vln")
        dve_a = sem("dve_a")
        dve_alo = sem("dve_alo")
        dve_m = sem("dve_m")
        dve_mlo = sem("dve_mlo")
        dve_h2 = sem("dve_h2")
        dve_rt = sem("dve_rt")
        dve_sel = sem("dve_sel")
        pe_sel = sem("pe_sel")
        act_sel = sem("act_sel")
        pool_pad = sem("pool_pad")
        pool_c = sem("pool_c")
        pool_win = sem("pool_win")
        e_gu = [sem(f"e_gu{s}") for s in range(3)]
        e_half = sem("e_half")
        e_dn = [sem(f"e_dn{s}") for s in range(3)]
        e_x = [sem(f"e_x{s}") for s in range(3)]
        y_st = [sem(f"y_st{s}") for s in range(3)]
        x_st = sem("x_st")
        x_first = sem("x_first")
        x_x = sem("x_x")
        m_sem = {n: sem("e_" + n) for n in ("xtr", "xt", "gum", "silu", "hid", "htr", "ht", "ym", "yo")}
        x_sem = {n: sem("x_" + n) for n in ("xtr", "xt", "gum", "silu", "hid", "htr", "ht", "ym", "yo")}
        f_g = [sem(f"f_g{i}") for i in range(TILES)]
        sp_go = sem("sp_go")
        pe_go = sem("pe_go")
        pool_go = sem("pool_go")
        f_t = sem("f_t")
        f_w = sem("f_w")
        f_c = sem("f_c")
        f_o = sem("f_o")
        f_m = sem("f_m")
        pool_f = sem("pool_f")
        dve_nb = sem("dve_nb")

        block = ctx.enter_context(nc.Block())

        class Chain:

            def __init__(self, e, s):
                self.e, self.s, self.n = e, s, 0

            def did(self, ins):
                ins.then_inc(self.s, 1)
                self.n += 1
                return self.n

            def sync(self):
                self.e.wait_ge(self.s, self.n)

        def win_cols(seg, unit):
            first = {SEG_U: 0, SEG_V: D, SEG_P: 2 * D, SEG_GA: 3 * D, SEG_GB: 4 * D}[seg] + 512 * unit
            return w_in[0, :, first:first + 512]

        def unit_source(u):
            seg, half = u // 2, u % 2
            if seg in (SEG_WB, SEG_WA, SEG_WO):
                w = {SEG_WB: w_branch_b, SEG_WA: w_branch_a, SEG_WO: w_out}[seg]
                src = w[0, :, 512 * half:512 * half + 512]
            else:
                src = win_cols(seg, half)
            return src.rearrange("(k p) n -> p k n", p=128)

        def mod_source(m):
            r, kc = m // KC, m % KC
            return w_mod[0, kc * 128:kc * 128 + 128, r * 2048:r * 2048 + 2048].rearrange("p (j n) -> p j n", j=4)

        def gate_src(w, e):
            return w[0, bass.ds(e, 1), :, :].rearrange("a (p k) n -> p (a k) n", p=128)

        @block.sync
        def _(sp):
            def load_unit(u):
                if u >= 2:
                    sp.wait_ge(dve_wlo, 4 * (u - 1))
                sp.dma_start(raw[:, u % 2, :, :], unit_source(u)).then_inc(s_w[u % 2], 16)

            def load_mod(m):
                if m - 10 >= 0:
                    sp.wait_ge(pe_mod, m - 1)
                sp.dma_start(modraw[:, m % 2, :, :], mod_source(m)).then_inc(s_m[m % 2], 16)

            sp.dma_start(cst[:, :], consts).then_inc(s_param, 16)
            sp.dma_start(prow[0:40, :], b_in[0, :].rearrange("(a n) -> a n", n=128)).then_inc(s_param, 16)
            sp.dma_start(prow[40:48, :], pool_scale[0, :].rearrange("(a n) -> a n", n=128)).then_inc(s_param, 16)
            sp.dma_start(prow[48:56, :], c_prompt[0, :].rearrange("(a n) -> a n", n=128)).then_inc(s_param, 16)
            sp.dma_start(prow[56:64, :], c_sample[0, :].rearrange("(a n) -> a n", n=128)).then_inc(s_param, 16)
            for r, x in enumerate((x_prompt, x_sample)):
                sp.dma_start(xin[HALF * r:HALF * r + HALF, :, :],
                             x[0, :, :].rearrange("(i p) d -> p i d", p=HALF)).then_inc(s_x, 16)
            for m in range(KC):
                if m >= 4:
                    sp.wait_ge(pe_mod, m - 3)
                sp.dma_start(modraw0[:, m % 4, :, :], mod_source(m)).then_inc(s_m0[m % 4], 16)
            sp.wait_ge(pe_mod, 6)
            load_unit(0)
            sp.wait_ge(pe_mod, 8)
            load_unit(1)
            for k in range(16):
                if k in (5, 9, 13):
                    load_unit((k - 1) // 4 + 1)
                load_mod(8 + k)
            for u in range(5, 16):
                load_unit(u)

            def load_gate_up(e, s):
                if isinstance(e, int) and e == NEXP - 1:
                    for chunks, loaded in ((slice(0, KC // 2), e_half), (slice(KC // 2, KC), e_gu[s])):
                        sp.dma_start(gate_w[s][:, chunks, :], gate_src(w_exp_gate, e)[:, chunks, :]).then_inc(loaded, 16)
                        sp.dma_start(up_w[s][:, chunks, :], gate_src(w_exp_up, e)[:, chunks, :]).then_inc(loaded, 16)
                    return
                sp.dma_start(gate_w[s][:, :, :], gate_src(w_exp_gate, e)).then_inc(e_gu[s], 16)
                sp.dma_start(up_w[s][:, :, :], gate_src(w_exp_up, e)).then_inc(e_gu[s], 16)

            def load_down(e, s):
                sp.dma_start(down_w[s][:, :, :], gate_src(w_exp_down, e)).then_inc(e_dn[s], 16)

            def load_expert(e, s):
                load_gate_up(e, s)
                load_down(e, s)

            sp.wait_ge(pe_blk, 56)
            sp.wait_ge(dve_m, 8)
            load_expert(0, 0)
            sp.wait_ge(dve_wlo, NBLK)
            load_expert(1, 1)
            sp.wait_ge(pe_blk, NBLK)
            load_expert(2, 2)

            def load_rows(e, s, off):
                half = CAP // 2
                if isinstance(e, int) and e < 3:
                    sp.dma_start(xrows[s][:, :], packed_x[bass.ds(off, CAP), :]).then_inc(e_x[s], 16)
                    return
                is_few = sp.value_load(few[0:1, bass.ds(e, 1)], min_val=0, max_val=1)
                with sp.If(is_few > 0):
                    sp.dma_start(xrows[s][0:half, :], packed_x[bass.ds(off, half), :]).then_inc(e_x[s], 16)
                with sp.If(is_few < 1):
                    sp.dma_start(xrows[s][:, :], packed_x[bass.ds(off, CAP), :]).then_inc(e_x[s], 16)

            def offset(e):
                return sp.value_load(tab[0:1, 0, bass.ds(e, 1)], min_val=0, max_val=ASSIGN)

            def next_expert(e, s):
                done = sp.value_load(tab[0:1, 2, bass.ds(e - 2, 1)], min_val=0, max_val=16)
                sp.wait_ge(m_sem["gum"], e - 2)
                sp.sem_inc(sp_go, 1)
                sp.wait_ge(x_sem["gum"], done + 1)
                sp.sem_inc(sp_go, 1)
                load_rows(e, s, offset(e))
                load_gate_up(e, s)
                sp.wait_ge(m_sem["ym"], e - 2)
                sp.sem_inc(sp_go, 1)
                sp.wait_ge(x_sem["ym"], done + 1)
                sp.sem_inc(sp_go, 1)
                load_down(e, s)

            def load_further_rows(e):
                more = sp.value_load(tab[0:1, 1, bass.ds(e, 1)], min_val=0, max_val=7)
                first = sp.value_load(tab[0:1, 2, bass.ds(e, 1)], min_val=0, max_val=FURTHER)
                with sp.If(more > 0):
                    sp.wait_ge(x_sem["xtr"], first + 1)
                    sp.sem_inc(sp_go, 1)
                    sp.dma_start(xrows_x[:, :], packed_x[bass.ds(sp.snap(offset(e) + CAP), CAP), :]).then_inc(x_first, 16)

            sp.wait_ge(s_scat, 16 * 8)
            sp.wait_ge(x_st, 16)
            sp.wait_ge(dve_rt, 3)
            sp.wait_ge(m_sem["xtr"], 1)
            for e in range(3):
                load_rows(e, e, offset(e))
            load_further_rows(0)
            sp.wait_ge(e_x[0], 16)
            next_expert(3, 0)
            for e in range(1, 4):
                load_further_rows(e)
            for k in range(1, 3):
                next_expert(3 + k, k)
                load_further_rows(3 + k)
            with sp.Fori(1, 9) as t:
                for k in range(3):
                    next_expert(3 + 3 * t + k, k)
                    load_further_rows(3 + 3 * t + k)
            for e in (30, 31):
                next_expert(e, e % 3)
                load_further_rows(e)

        @block.gpsimd
        def _(pool):
            ch = Chain(pool, pool_c)
            pool.dma_start(ws_raw[:, :, :], w_spatial[0, :, :, :].rearrange("h p q -> p h q")).then_inc(s_ws, 16)
            for j in range(4):
                for r in range(REQ):
                    pool.dma_start(modrow[32 * j + r:32 * j + r + 1, :, :],
                                   b_mod[0:1, :].rearrange("a (g j n) -> a g j n", g=3, j=4)[:, :, j, :]).then_inc(s_bmod, 16)
            pool.dma_start(wr[:, :, 0:NGRP], w_router_group[0, :, :].rearrange("(k p) n -> p k n", p=128)).then_inc(s_wr, 16)
            pool.dma_start(wr[:, :, NGRP:], w_router_expert[0, :, :].rearrange("(k p) n -> p k n", p=128)).then_inc(s_wr, 16)
            pool.dma_start(br_bc[:, 0:NGRP], b_router_group[0, :].partition_broadcast(128)).then_inc(s_wr, 16)
            pool.dma_start(br_bc[:, NGRP:], b_router_expert[0, :].partition_broadcast(128)).then_inc(s_wr, 16)
            for i in range(2):
                pool.memset(zpad[i][:, :, :], 0.0).then_inc(pool_pad, 1)
            pool.wait_ge(pool_pad, 1)
            pool.dma_start(packed_x[ASSIGN:ASSIGN + CAP, :].rearrange("r (h n) -> (r h) n", h=2),
                           zpad[0][:, :, :].rearrange("p r n -> p (r n)")[:, 0:512]).then_inc(x_st, 16)
            pool.wait_ge(dve_hlo, KC)
            pool.dma_start(wp_raw[:, :, :, :], w_pool[0, :, :, :].rearrange("g (k p) n -> p g k n", p=128)).then_inc(s_wp, 16)
            pool.dma_start(bs_bc[:, :, :].rearrange("p h q -> p (h q)"),
                           b_spatial[0, :, :].rearrange("h q -> (h q)").partition_broadcast(128)).then_inc(s_bs, 16)
            pool.wait_ge(s_param, 80)
            for n in range(8):
                g = n // 2
                w = WINDOWS[g]
                pool.wait_ge(act_z, 8 + n + 1)
                if n:
                    pool.wait_ge(dve_d, n)
                src = zpad[n % 2]
                for k in range(1, g + 2):
                    length = PADW - 2 ** k + 1
                    dst = wsum[k % 2]
                    if k > 1:
                        ch.sync()
                    ch.did(pool.tensor_tensor(dst[:, :, 0:length], src[:, :, 0:length],
                                              src[:, :, 2 ** (k - 1):2 ** (k - 1) + length], ALU.add))
                    src = dst
                ch.sync()
                edges = []
                for r in range(REQ):
                    edges.append((src[:, r, 8 - w // 2:8], C_EDGE + 16 * g, w // 2))
                    if w > 2:
                        first = 8 - w // 2 + SEQ - w // 2 + 1
                        edges.append((src[:, r, first:first + w // 2 - 1], C_EDGE + 16 * g + 8, w // 2 - 1))
                for part, c, width in edges[:-1]:
                    ch.did(pool.tensor_tensor(part, part, cst[:, c:c + width], ALU.mult))
                ch.sync()
                part, c, width = edges[-1]
                pool.tensor_tensor(part, part, cst[:, c:c + width], ALU.mult).then_inc(pool_win, 1)
            pool.wait_ge(dve_d, 8)
            pool.dma_start(sgu_bc[:, 0, :], sgu_g[0, :].partition_broadcast(128)).then_inc(s_sgu, 16)
            pool.dma_start(sgu_bc[:, 1, :], sgu_b[0, :].partition_broadcast(128)).then_inc(s_sgu, 16)
            pool.wait_ge(pe_pool, 8)
            pool.memset(zrow[:, :], 0.0).then_inc(pool_pad, 1)
            pool.wait_ge(pool_pad, 3)
            zeroes = zrow[:, :].rearrange("p (a n) -> p a n", a=1).broadcast_to([128, 8, 512])
            for k in range(LAST_ROW // 512):
                pool.wait_ge(pe_blk, 22 + 3 * k)
                pool.dma_start(round_y[512 * k:512 * k + 512, :].rearrange("(p r) (h n) -> p (r h) n", p=128, h=2), zeroes).then_inc(s_zero, 16)
            pool.wait_ge(s_zero, 16 * (LAST_ROW // 512))
            pool.wait_ge(dve_a, 8)
            for r, x in enumerate((x_prompt, x_sample)):
                pool.dma_start(res[HALF * r:HALF * r + HALF, :, :],
                               x[0, :, :].rearrange("(i p) d -> p i d", p=HALF)).then_inc(s_xres, 16)
            pool.dma_start(ln1_bc[:, 0, :], ln1_g[0, :].partition_broadcast(128)).then_inc(s_ln1, 16)
            pool.dma_start(ln1_bc[:, 1, :], ln1_b[0, :].partition_broadcast(128)).then_inc(s_ln1, 16)
            pool.wait_ge(dve_rt, 2)
            pool.wait_ge(dve_h2, TILES)
            for j in range(2):
                for i in range(TILES):
                    pool.indirect_dma_start(packed_x[0:ASSIGN, :], bass.IndirectOffsetOnAxis(pos[:, j, i:i + 1], 0),
                                            h2[:, i, :], None, bounds_check=ASSIGN - 1, oob_is_err=False).then_inc(s_scat, 16)
            pool.wait_ge(dve_rt, 3)

            def store(y, turn, done, rows):
                row = turn * CAP
                pool.dma_start(round_y[bass.ds(row, rows), 0:512], y[0:rows, :]).then_inc(done, 16)
                pool.dma_start(round_y[bass.ds(row, rows), 512:1024], y[64:64 + rows, :]).then_inc(done, 16)

            def expert(e, s):
                off = pool.value_load(tab[0:1, 0, bass.ds(e, 1)], min_val=0, max_val=ASSIGN)
                more = pool.value_load(tab[0:1, 1, bass.ds(e, 1)], min_val=0, max_val=7)
                first = pool.value_load(tab[0:1, 2, bass.ds(e, 1)], min_val=0, max_val=FURTHER)

                def load_further(r):
                    pool.wait_ge(x_sem["xtr"], first + r + 1)
                    pool.sem_inc(pool_go, 1)
                    pool.dma_start(xrows_x[:, :], packed_x[bass.ds(pool.snap(off + (r + 1) * CAP), CAP), :]).then_inc(x_x, 16)

                def store_further(r):
                    turn = pool.snap(e + 1 + first + r)
                    pool.wait_ge(x_sem["yo"], first + r + 2)
                    pool.sem_inc(pool_go, 1)
                    store(yout_x, turn, x_st, CAP)

                turn = pool.snap(first + e)
                pool.wait_ge(m_sem["yo"], e + 1)
                pool.sem_inc(pool_go, 1)
                is_few = pool.value_load(few[0:1, bass.ds(e, 1)], min_val=0, max_val=1)
                with pool.If(is_few > 0):
                    store(yout[s], turn, y_st[s], CAP // 2)
                with pool.If(is_few < 1):
                    store(yout[s], turn, y_st[s], CAP)
                with pool.If(more > 1):
                    with pool.Fori(0, more - 1) as r:
                        load_further(r + 1)
                        store_further(r)
                with pool.If(more > 0):
                    store_further(more - 1)

            with pool.Fori(0, 10) as t:
                for k in range(3):
                    expert(3 * t + k, k)
            expert(30, 0)
            allx = pool.value_load(tab[0:1, 2, NEXP - 2:NEXP - 1], min_val=0, max_val=FURTHER)
            pool.wait_ge(m_sem["ym"], 30)
            pool.wait_ge(x_sem["ym"], allx + 1)
            pool.sem_inc(pool_go, 1)
            pool.dma_start(ln2_bc[:, 0, :], ln2_g[0, :].partition_broadcast(128)).then_inc(s_ln2, 16)
            pool.dma_start(ln2_bc[:, 1, :], ln2_b[0, :].partition_broadcast(128)).then_inc(s_ln2, 16)
            expert(31, 1)
            allx = pool.value_load(tab[0:1, 2, NEXP:NEXP + 1], min_val=0, max_val=FURTHER)
            for k, uses in enumerate((11, 11, 10)):
                pool.wait_ge(y_st[k], 32 * uses)
            pool.wait_ge(x_st, 32 * allx + 16)
            pool.sem_inc(pool_go, 1)
            for i in range(TILES):
                for j, y in enumerate((y_second, y_first)):
                    pool.indirect_dma_start(y[i][:, :], None, round_y[0:LAST_ROW, :],
                                            bass.IndirectOffsetOnAxis(pos_y[:, 1 - j, i:i + 1], 0),
                                            bounds_check=LAST_ROW - 1, oob_is_err=False).then_inc(f_g[i], 16)
            for i in range(1, TILES):
                pool.wait_ge(f_w, i)
                pool.tensor_tensor(y_first[i][:, :], y_first[i][:, :], y_second[i][:, :], ALU.add).then_inc(f_c, 1)
            pool.wait_ge(s_ln2, 32)
            for i in range(2):
                pool.wait_ge(f_m, i + 1)
                pool.tensor_tensor(y_first[i][:, :], y_first[i][:, :], ln2_bc[:, 1, :], ALU.add).then_inc(pool_f, 1)

        @block.tensor
        def _(pe):
            def mm(out, lhsT, rhs, start=True, stop=True):
                return pe.matmul(out, lhsT, rhs, start=start, stop=stop, skip_group_check=True)

            pe.wait_ge(s_param, 80)
            pe.transpose(COL[:, 0:64], prow[0:64, :], ident[0:64, 0:64]).then_inc(pe_pro, 1)
            pe.wait_ge(s_ws, 16)
            for hb in range(8):
                x = pe.transpose(MX[hb // 4][:, 128 * (hb % 4):128 * (hb % 4) + 128], ws_raw[:, hb, :], ident)
            x.then_inc(pe_pro, 1)
            def mod_unit(src, kc):
                for j in range(4):
                    x = mm(MOD[32 * j:32 * j + 2, :], silu_c[:, :, kc], src[:, j, :], start=(kc == 0), stop=(kc == KC - 1))
                x.then_inc(pe_mod, 1)

            def mod_cols(g, j):
                for k in range(4):
                    c = 4 * j + k
                    x = mm(COLS[j][:, 2 * c:2 * c + 2], modrow[32 * j:32 * j + 2, g, 128 * k:128 * k + 128],
                           ident[32 * j:32 * j + 2, 32 * j:32 * j + 2])
                x.then_inc(pe_modcol, 1)

            def mod_units0(first, last):
                for m in range(first, last):
                    pe.wait_ge(s_m0[m % 4], 16 * (m // 4 + 1))
                    mod_unit(modraw0[:, m % 4, :, :], m)

            pe.wait_ge(act_pro, 1)
            mod_units0(0, 4)
            for i in range(TILES):
                pe.wait_ge(dve_n, i + 1)
                if i >= 2:
                    pe.wait_ge(act_nt, 2 * (i - 1))
                for kc in range(KC):
                    bank = B[2 * (i % 2) + kc // 4]
                    x = pe.transpose(bank[:, 128 * (kc % 4):128 * (kc % 4) + 128], xin[:, i, 128 * kc:128 * kc + 128], ident)
                x.then_inc(pe_xt, 1)
            mod_units0(4, KC)
            pe.wait_ge(act_nt, 2 * TILES)
            for j in range(4):
                pe.wait_ge(dve_row0, j + 1)
                mod_cols(0, j)

            def block_at(b, i, mov_hi, mov_lo, freed, count, fresh=None):
                pe.wait_ge(act_whi, b + 1)
                pe.wait_ge(dve_wlo, b + 1)
                if freed is not None:
                    pe.wait_ge(freed, count)
                for kc in range(KC):
                    if fresh is not None and kc == KC - 1:
                        pe.wait_ge(fresh[0], KC)
                        pe.wait_ge(fresh[1], KC)
                    mm(Z[i][:, :], w_hi[i][:, kc, :], mov_lo[:, kc, :], start=(kc == 0), stop=False)
                    mm(Z[i][:, :], w_hi[i][:, kc, :], mov_hi[:, kc, :], start=False, stop=False)
                    x = mm(Z[i][:, :], w_lo[i][:, kc, :], mov_hi[:, kc, :], start=False, stop=(kc == KC - 1))
                x.then_inc(pe_blk, 1)

            def transposes(k, zs, trs):
                pe.wait_ge(act_z, zs)
                if trs is not None:
                    pe.wait_ge(dve_tr, trs)
                for c in range(TILES):
                    x = pe.transpose(TR[k][:, 128 * c:128 * c + 128], g32[k][:, 128 * c:128 * c + 128], ident)
                x.then_inc(pe_tr, 1)

            pe.wait_ge(dve_pro, 2)
            pe.wait_ge(act_whi, 1)
            pe.wait_ge(dve_wlo, 1)
            for kc in range(KC):
                pe.wait_ge(act_hhi, kc + 1)
                mm(Z[0][:, :], w_hi[0][:, kc, :], h_hi[:, kc, :], start=(kc == 0), stop=False)
                mm(Z[0][:, :], w_lo[0][:, kc, :], h_hi[:, kc, :], start=False, stop=False)
            for kc in range(KC):
                pe.wait_ge(dve_hlo, kc + 1)
                x = mm(Z[0][:, :], w_hi[0][:, kc, :], h_lo[:, kc, :], start=False, stop=(kc == KC - 1))
            x.then_inc(pe_blk, 1)
            for n in range(8):
                if n:
                    block_at(n, n % 2, h_hi, h_lo, act_z if n >= 2 else None, n - 1)
                    transposes((n - 1) % 2, n, n - 2 if n >= 3 else None)
                pe.wait_ge(s_m[n % 2], 16 * (n // 2 + 1))
                mod_unit(modraw[:, n % 2, :, :], n)
            def pooled(g):
                pe.wait_ge(act_dhi, 2 * g + 2)
                pe.wait_ge(dve_dlo, 2 * g + 2)
                pe.wait_ge(act_wphi, g + 1)
                pe.wait_ge(dve_wplo, g + 1)
                if g:
                    pe.wait_ge(act_pt, 2 * g)
                for o in range(2):
                    cols = slice(128 * o, 128 * o + 128)
                    for kc in range(2):
                        mm(MX[o][:, :], wp_hi[:, kc, cols], d_lo[:, kc, :], start=(kc == 0), stop=False)
                        mm(MX[o][:, :], wp_hi[:, kc, cols], d_hi[:, kc, :], start=False, stop=False)
                        x = mm(MX[o][:, :], wp_lo[:, kc, cols], d_hi[:, kc, :], start=False, stop=(kc == 1))
                    x.then_inc(pe_pool, 1)

            for n in range(8):
                b = 8 + n
                block_at(b, n % 2, h_hi, h_lo, act_z, b - 1)
                if n == 0:
                    transposes(1, 8, 6)
                if n >= 3 and n % 2 == 1:
                    pooled(n // 2 - 1)
                pe.wait_ge(s_m[n % 2], 16 * (5 + n // 2))
                if n == 0:
                    pe.wait_ge(dve_row, 1)
                mod_unit(modraw[:, n % 2, :, :], n)
            for k in range(2):
                block_at(16 + k, k, h_hi, h_lo, act_z, 15 + k)
                mod_cols(1, k)
            for k in range(2):
                block_at(18 + k, k, h_hi, h_lo, act_z, 17 + k)
            pooled(3)
            with pe.Fori(2, 4) as t:
                for k in range(2):
                    block_at(16 + 2 * t + k, k, h_hi, h_lo, act_z, 16 + 2 * t + k - 1)
            pe.wait_ge(act_phi, 8)
            pe.wait_ge(dve_plo, 8)
            for k in range(2):
                block_at(24 + k, k, a_hi, a_lo, act_z, 23 + k)
            with pe.Fori(0, 3) as t:
                for k in range(2):
                    block_at(26 + 2 * t + k, k, a_hi, a_lo, dve_z, 2 * t + k + 1)
            pe.wait_ge(dve_vln, TILES)
            for n in range(8):
                b = 32 + n
                block_at(b, n % 2, h_hi, h_lo, dve_z if n < 2 else act_z, 7 + n if n < 2 else 24 + n - 1)
                if n >= 2:
                    pe.wait_ge(dve_a, n - 1)
                for c in range(TILES):
                    x = mm(MX[n % 2][:, 128 * c:128 * c + 128], v_nat[:, c, 128 * n:128 * n + 128], ws_t[:, n, :])
                x.then_inc(pe_mix, 1)
            with pe.Fori(0, 4) as t:
                for k in range(2):
                    block_at(40 + 2 * t + k, k, h_hi, h_lo, act_z, 31 + 2 * t + k)
            pe.wait_ge(act_ahi, 8)
            pe.wait_ge(dve_alo, 8)
            for k in range(2):
                block_at(48 + k, k, a_hi, a_lo, act_z, 39 + k)
            with pe.Fori(0, 3) as t:
                for k in range(2):
                    block_at(50 + 2 * t + k, k, a_hi, a_lo, dve_z, 8 + 2 * t + k + 1)
            pe.wait_ge(act_mhi, KC - 1)
            pe.wait_ge(dve_mlo, KC - 1)
            block_at(56, 0, h_hi, h_lo, dve_z, 15, fresh=(act_mhi, dve_mlo))
            block_at(57, 1, h_hi, h_lo, dve_z, 16)
            transposes(0, 41, 7)
            with pe.Fori(1, 4) as t:
                for k in range(2):
                    block_at(56 + 2 * t + k, k, h_hi, h_lo, act_z, 39 + 2 * t + k)
                    transposes(1 - k, 40 + 2 * t + k, 6 + 2 * t + k)
            transposes(1, 48, 14)

            def broadcast(vec, banks):
                for c in range(2):
                    ch_id = 2 * vec + c
                    g, j = ch_id // 4, ch_id % 4
                    x = mm(banks[c][:, :], cst[32 * j:32 * j + 2, C_SEL:C_SEL + 128], modrow[32 * j:32 * j + 2, g, :])
                x.then_inc(pe_bc, 1)

            pe.wait_ge(dve_row, 3)
            pe.wait_ge(dve_col, 2)
            broadcast(4, (B[4], B[5]))
            broadcast(3, (B[6], B[7]))
            pe.wait_ge(s_wr, 64)
            def h2_transposes(i):
                pe.wait_ge(dve_h2, i + 1)
                for hb in range(2):
                    if i:
                        pe.wait_ge(act_rt, 2 * i - 1 + hb)
                    for k in range(4):
                        kc = 4 * hb + k
                        x = pe.transpose(TR[hb][:, 128 * k:128 * k + 128], h2[:, i, 128 * kc:128 * kc + 128], ident)
                    x.then_inc(pe_rt, 1)

            pe.wait_ge(dve_tr, 16)
            for i in range(TILES):
                h2_transposes(i)
                for kc in range(KC):
                    if kc % 4 == 0:
                        pe.wait_ge(act_rt, 2 * i + kc // 4 + 1)
                    x = mm(B[0][:, 64 * i:64 * i + NGRP + NEXP], h2_t[i % 2][:, kc, :], wr[:, kc, :], start=(kc == 0), stop=(kc == KC - 1))
                x.then_inc(pe_lg, 1)
            pe.wait_ge(dve_rt, 1)
            before, every = before_m[:, 0, :], before_m[:, 1, :]

            def count(first, last, lhsT, src, start=False, stop=False):
                w = last - first + 1
                return mm(B[1][:, NEXP * first:NEXP * (last + 1)], lhsT,
                          both[:, src:src + w, :].rearrange("p i n -> p (i n)"), start=start, stop=stop)

            count(0, 4, every, 0, start=True)
            count(0, 3, before, 1)
            for back in range(1, TILES):
                x = count(1 + back, 4, every, 1, stop=(back == TILES - 1))
            x.then_inc(pe_lg, 1)

            def x_transposes(rows, bank, s):
                pe.sem_inc(pe_go, 1)
                view = rows[:, :].rearrange("c (p k) -> c k p", k=KC)
                for kc in range(KC):
                    x = pe.transpose(bank[:, CAP * kc:CAP * kc + CAP], view[:, kc, :], ident[0:CAP, 0:CAP])
                x.then_inc(s["xtr"], 1)

            def gate_up(xt, s, bank, sm, halves=None):
                for kc in range(KC):
                    if halves is not None and kc == KC // 2:
                        pe.wait_ge(*halves)
                    mm(bank[0:CAP, :], xt[:, kc, :], gate_w[s][:, kc, :], start=(kc == 0), stop=(kc == KC - 1))
                    x = mm(bank[CAP:128, :], xt[:, kc, :], up_w[s][:, kc, :], start=(kc == 0), stop=(kc == KC - 1))
                x.then_inc(sm["gum"], 1)

            def h_transposes(hd, bank, sm):
                pe.sem_inc(pe_go, 1)
                view = hd[:, :].rearrange("c (p f) -> c f p", f=FC)
                for fc in range(FC):
                    x = pe.transpose(bank[:, CAP * fc:CAP * fc + CAP], view[:, fc, :], ident[0:CAP, 0:CAP])
                x.then_inc(sm["htr"], 1)

            def down(ht, s, bank, sm):
                for fc in range(FC):
                    mm(bank[0:CAP, :], ht[:, fc, :], down_w[s][:, fc, 0:512], start=(fc == 0), stop=(fc == FC - 1))
                    x = mm(bank[CAP:128, :], ht[:, fc, :], down_w[s][:, fc, 512:1024], start=(fc == 0), stop=(fc == FC - 1))
                x.then_inc(sm["ym"], 1)

            def expert(e, s, turn, last=False):
                if last:
                    pe.wait_ge(e_half, 32)
                else:
                    pe.wait_ge(e_gu[s], 32 * (turn + 1))
                pe.wait_ge(m_sem["xt"], e + 1)
                gate_up(x_t[s], s, B[0], m_sem, halves=(e_gu[s], 32 * (turn + 1)) if last else None)
                if not last:
                    n = (s + 1) % 3
                    pe.wait_ge(e_x[n], 16 * (turn + 1 + (1 if n == 0 else 0)))
                    x_transposes(xrows[n], B[2], m_sem)
                pe.wait_ge(m_sem["hid"], e + 1)
                h_transposes(hid, B[3], m_sem)
                pe.wait_ge(m_sem["ht"], e + 1)
                pe.wait_ge(e_dn[s], 16 * (turn + 1))
                if not (isinstance(e, int) and e == 0):
                    pe.wait_ge(m_sem["yo"], e)
                down(hid_t, s, B[1], m_sem)
                more = pe.value_load(tab[0:1, 1, bass.ds(e, 1)], min_val=0, max_val=7)
                first = pe.value_load(tab[0:1, 2, bass.ds(e, 1)], min_val=0, max_val=16)
                def further_round(turns):
                    pe.wait_ge(x_sem["yo"], turns + 1)
                    x_transposes(xrows_x, B[6], x_sem)
                    pe.wait_ge(x_sem["xt"], turns + 1)
                    gate_up(x_t_x, s, B[4], x_sem)
                    pe.wait_ge(x_sem["hid"], turns + 1)
                    h_transposes(hid_x, B[7], x_sem)
                    pe.wait_ge(x_sem["ht"], turns + 1)
                    down(hid_t_x, s, B[5], x_sem)

                with pe.If(more > 0):
                    having = pe.value_load(tab[0:1, 3, bass.ds(e, 1)], min_val=0, max_val=FURTHER)
                    others = pe.value_load(tab[0:1, 4, bass.ds(e, 1)], min_val=0, max_val=FURTHER)
                    pe.wait_ge(x_first, 16 * (having + 1))
                    pe.sem_inc(pe_go, 1)
                    further_round(first)
                    with pe.If(more > 1):
                        with pe.Fori(1, more) as r:
                            pe.wait_ge(x_x, 16 * (others + r))
                            pe.sem_inc(pe_go, 1)
                            further_round(pe.snap(first + r))

            pe.wait_ge(dve_sel, 1)
            for i in range(TILES):
                for c in range(2):
                    x = mm(B[3][CAP * c:CAP * c + CAP, :], sel[0][:, i, :], h2[:, i, 512 * c:512 * c + 512],
                           start=(i == 0), stop=(i == TILES - 1))
            x.then_inc(pe_sel, 1)
            pe.wait_ge(act_sel, 2)
            x_transposes(xrows_x, B[2], m_sem)
            pe.sem_inc(x_sem["xtr"], 1)
            pe.sem_inc(x_sem["ym"], 1)
            pe.sem_inc(x_sem["gum"], 1)
            pe.wait_ge(dve_rt, 3)
            for k in range(3):
                expert(k, k, 0)
            with pe.Fori(1, 10) as t:
                for k in range(3):
                    expert(3 * t + k, k, t)
            expert(30, 0, 10)
            expert(31, 1, 10, last=True)
            broadcast(5, (B[0], B[2]))

        @block.scalar
        def _(act):
            def copy(out, in_, scale=1.0):
                return act.activation(out, in_, ACT.Copy, scale=scale)

            def split_hi(b):
                u = b // 4
                act.wait_ge(s_w[u % 2], 16 * (u // 2 + 1))
                if b >= 2:
                    act.wait_ge(pe_blk, b - 1)
                copy(w_hi[b % 2][:, :, :], raw[:, u % 2, :, 128 * (b % 4):128 * (b % 4) + 128]).then_inc(act_whi, 1)

            act.wait_ge(dve_pro, 1)
            act.activation(silu_c[:, :, :].rearrange("p r k -> p (r k)"), COL[:, 48:64], ACT.Silu).then_inc(act_pro, 1)
            act.wait_ge(dve_st, 1)
            act.activation(rs[:, 1, :], rs[:, 0, :], ACT.Sqrt).then_inc(act_sq, 1)
            n_view = n_t[:, :, :].rearrange("p k (r i n) -> p k r i n", r=REQ, i=TILES)
            for i in range(TILES):
                act.wait_ge(pe_xt, i + 1)
                for hb in range(2):
                    src = B[2 * (i % 2) + hb][:, :].rearrange("p (k r n) -> p k r n", k=4, r=REQ)
                    copy(n_view[:, 4 * hb:4 * hb + 4, :, i, :], src).then_inc(act_nt, 1)
            split_hi(0)
            act.wait_ge(dve_aff, 1)
            for kc in range(KC):
                for r in range(REQ):
                    x = act.activation(h_hi[:, kc, SEQ * r:SEQ * r + SEQ], n_t[:, kc, SEQ * r:SEQ * r + SEQ], ACT.Identity,
                                       scale=scale1p[:, kc, r:r + 1], bias=mod_t[:, 0, kc, r:r + 1])
                x.then_inc(act_hhi, 1)
            split_hi(1)

            def run(seg, n, evac=None):
                b = 8 * seg + n
                if evac:
                    act.wait_ge(pe_blk, b + 1)
                    evac(n, n % 2, b)
                if b + 2 < NBLK:
                    split_hi(b + 2)

            def ev_v(n, i, b):
                if b >= 2:
                    act.wait_ge(pe_tr, b - 1)
                act.activation(g32[i][:, :], Z[i][:, :], ACT.Gelu_apprx_tanh, bias=pcol[:, 8 + n:9 + n]).then_inc(act_z, 1)

            for n in range(8):
                run(SEG_V, n, ev_v)

            def d_high(n):
                act.wait_ge(dve_d, n + 1)
                if n >= 2:
                    act.wait_ge(pe_pool, 2 * (n // 2))
                copy(d_hi[:, n % 2, :], d32[n % 2][:, :]).then_inc(act_dhi, 1)

            def pool_w_high(g):
                act.wait_ge(s_wp, 16)
                if g:
                    act.wait_ge(pe_pool, 2 * g)
                copy(wp_hi[:, :, :], wp_raw[:, g, :, :]).then_inc(act_wphi, 1)

            def pool_evac(g):
                for o in range(2):
                    act.wait_ge(pe_pool, 2 * g + o + 1)
                    if g:
                        act.wait_ge(dve_plo, 2 * g + o - 1)
                    act.activation(g32[o][:, :], MX[o][:, :], ACT.Copy,
                                   scale=pcol[:, 40 + 2 * g + o:41 + 2 * g + o]).then_inc(act_pt, 1)
                    act.wait_ge(act_pt, 2 * g + o + 1)
                    copy(a_hi[:, 2 * g + o, :], g32[o][:, :]).then_inc(act_phi, 1)

            def ev_p(n, i, b):
                if n >= 2:
                    act.wait_ge(dve_d, n - 1)
                else:
                    act.wait_ge(pool_pad, 2)
                    act.wait_ge(x_st, 16)
                act.activation(zpad[i][:, :, 8:8 + SEQ], Z[i][:, :].rearrange("p (r s) -> p r s", r=REQ),
                               ACT.Identity, bias=pcol[:, 16 + n:17 + n]).then_inc(act_z, 1)

            def pool_steps(n):
                if n:
                    d_high(n - 1)
                if n == 1:
                    pool_w_high(0)
                if n >= 4 and n % 2 == 0:
                    if n == 4:
                        act.wait_ge(dve_tr, 8)
                    pool_evac(n // 2 - 2)
                    if n < 10:
                        pool_w_high(n // 2 - 1)

            for n in range(8):
                run(SEG_P, n, ev_p)
                pool_steps(n)

            def sigmoid(dst, col):
                def ev(n, i, b):
                    act.activation(dst[:, n, :], Z[i][:, :], ACT.Sigmoid, bias=pcol[:, col + n:col + n + 1]).then_inc(act_z, 1)
                return ev

            ev_gb = sigmoid(m_b, 32)
            act.wait_ge(pe_mod, 24)
            for n in range(8):
                run(SEG_GB, n, ev_gb)
                if n == 0:
                    pool_steps(8)
                if n == 4:
                    pool_evac(3)
                if n == 6:
                    act.wait_ge(dve_st, 2)
                    act.activation(rs[:, 1, :], rs[:, 0, :], ACT.Sqrt).then_inc(act_sq, 1)
            for n in range(8):
                run(SEG_WB, n)

            def a_high(n):
                act.wait_ge(dve_a, n + 1)
                copy(a_hi[:, n, :], d32[n % 2][:, :]).then_inc(act_ahi, 1)

            def ev_u(n, i, b):
                if n >= 2:
                    act.wait_ge(dve_a, n - 1)
                act.activation(g32[i][:, :], Z[i][:, :], ACT.Gelu_apprx_tanh, bias=pcol[:, n:n + 1]).then_inc(act_z, 1)

            for n in range(8):
                run(SEG_U, n, ev_u)
                if n:
                    a_high(n - 1)

            ev_ga = sigmoid(g_a, 24)
            for n in range(8):
                run(SEG_GA, n, ev_ga)
                if n == 0:
                    a_high(7)

            for n in range(8):
                run(SEG_WA, n)
                act.wait_ge(dve_m, n + 1)
                copy(h_hi[:, n, :], d32[n % 2][:, :]).then_inc(act_mhi, 1)

            def ev_o(n, i, b):
                act.wait_ge(pe_tr, 8 + n - 1)
                for r in range(REQ):
                    x = act.activation(g32[i][:, :].rearrange("p (i r n) -> p i r n", i=TILES, r=REQ)[:, :, r, :],
                                       Z[i][:, SEQ * r:SEQ * r + SEQ].rearrange("p (i n) -> p i n", i=TILES), ACT.Copy,
                                       scale=mod_t[:, 2, n, r:r + 1])
                x.then_inc(act_z, 1)

            act.wait_ge(dve_col, 2)
            for n in range(8):
                run(SEG_WO, n, ev_o)
            act.wait_ge(dve_st, 3)
            act.activation(rs[:, 1, :], rs[:, 0, :], ACT.Sqrt).then_inc(act_sq, 1)

            def root2(i):
                act.wait_ge(dve_st, 4 + i)
                act.activation(rs[:, 6, i:i + 1], rs[:, 5, i:i + 1], ACT.Sqrt).then_inc(act_sq, 1)

            root2(0)
            for i in range(TILES):
                if i + 1 < TILES:
                    root2(i + 1)
                for hb in range(2):
                    act.wait_ge(pe_rt, 2 * i + hb + 1)
                    if i >= 2:
                        act.wait_ge(pe_lg, i - 1)
                    copy(h2_t[i % 2][:, 4 * hb:4 * hb + 4, :], TR[hb][:, :].rearrange("p (k n) -> p k n", k=4)).then_inc(act_rt, 1)
            act.wait_ge(dve_st, 8)
            act.activation(q1[:, 2:6, :].rearrange("p k i -> p (k i)"), q1[:, 6:10, :].rearrange("p k i -> p (k i)"), ACT.Exp).then_inc(act_rt, 1)
            act.wait_ge(dve_st, 9)
            act.activation(q1[:, 12, :], q1[:, 11, :], ACT.Exp).then_inc(act_rt, 1)
            act.wait_ge(pe_sel, 1)
            for c in range(2):
                copy(xrows_x[:, 512 * c:512 * c + 512], B[3][CAP * c:CAP * c + CAP, :]).then_inc(act_sel, 1)
            act.wait_ge(dve_h2, TILES)
            copy(res[:, :, :], res[:, :, :], scale=ALPHA).then_inc(act_res, 1)

            def round_(sm, banks, sgb, ht, y, n, ones, stored, count):
                act.wait_ge(sm["gum"], n + ones + 1)
                act.activation(sgb[:, :], banks[0][0:CAP, :], ACT.Silu).then_inc(sm["silu"], 1)
                act.wait_ge(sm["htr"], n + 1)
                copy(ht[:, :, :].rearrange("p f c -> p (f c)"), banks[2][:, 0:FC * CAP]).then_inc(sm["ht"], 1)
                act.wait_ge(sm["ym"], n + ones + 1)
                if count is not None:
                    act.wait_ge(stored, count)
                copy(y[:, :], banks[1][:, :]).then_inc(sm["yo"], 1)

            act.sem_inc(x_sem["yo"], 1)
            act.wait_ge(dve_rt, 3)
            act.wait_ge(s_scat, 16 * 8)

            def expert(e, s, turn):
                round_(m_sem, (B[0], B[1], B[3]), sg, hid_t, yout[s], e, 0, y_st[s],
                       None if isinstance(turn, int) and turn == 0 else 32 * turn)
                more = act.value_load(tab[0:1, 1, bass.ds(e, 1)], min_val=0, max_val=7)
                first = act.value_load(tab[0:1, 2, bass.ds(e, 1)], min_val=0, max_val=FURTHER)
                with act.If(more > 0):
                    with act.Fori(0, more) as r:
                        turns = act.snap(first + r)
                        round_(x_sem, (B[4], B[5], B[7]), sg_x, hid_t_x, yout_x, turns, 1, x_st, 32 * turns + 16)

            for k in range(3):
                expert(k, k, 0)
            with act.Fori(1, 10) as t:
                for k in range(3):
                    expert(3 * t + k, k, t)
            expert(30, 0, 10)
            expert(31, 1, 10)
            def root(k):
                act.wait_ge(dve_st, 10 + k)
                act.activation(rs[:, 1, 2 * k:2 * k + 2], rs[:, 0, 2 * k:2 * k + 2], ACT.Sqrt).then_inc(act_sq, 1)

            for i in range(TILES):
                act.wait_ge(f_g[i], 32)
                x = copy(y_second[i][:, :], y_second[i][:, :], scale=route_w[:, 1, i:i + 1])
                if i == 0:
                    x.then_inc(f_t, 1)
                else:
                    copy(y_first[i][:, :], y_first[i][:, :], scale=route_w[:, 0, i:i + 1]).then_inc(f_w, 1)
            root(0)
            for i in range(2):
                act.wait_ge(dve_nb, 1)
                act.activation(y_first[i][:, :], y_first[i][:, :], ACT.Identity, scale=rs[:, 2, i:i + 1],
                               bias=rs[:, 4, i:i + 1]).then_inc(act_f, 1)
            root(1)
            for i in range(TILES):
                act.wait_ge(pool_f if i < 2 else f_o, i % 2 + 1)
                for r, y in enumerate((y_prompt, y_sample)):
                    act.dma_start(y[0, HALF * i:HALF * i + HALF, :], y_first[i][HALF * r:HALF * r + HALF, :]).then_inc(s_out, 16)
            act.wait_ge(s_out, 32 * TILES)

        @block.vector
        def _(dve):
            ch = Chain(dve, dve_c)

            def link(ins):
                ch.did(ins)
                ch.sync()

            sq = [0]

            def rstd(first, w):
                c = slice(first, first + w)
                ch.sync()
                dve.tensor_scalar(rs[:, 0, c], mv[:, c, 1], EPS, None, ALU.add).then_inc(dve_st, 1)
                sq[0] += 1
                dve.wait_ge(act_sq, sq[0])
                link(dve.reciprocal(rs[:, 2, c], rs[:, 1, c]))
                link(dve.tensor_tensor(rs[:, 3, c], rs[:, 2, c], rs[:, 2, c], ALU.mult))
                link(dve.tensor_tensor(rs[:, 3, c], rs[:, 3, c], rs[:, 0, c], ALU.mult))
                link(dve.tensor_scalar(rs[:, 3, c], rs[:, 3, c], -0.5, 1.5, ALU.mult, ALU.add))
                link(dve.tensor_tensor(rs[:, 2, c], rs[:, 2, c], rs[:, 3, c], ALU.mult))

            def stats(src, i):
                for hb in range(2):
                    ch.did(dve.bn_stats(st[:, i, hb, :], src[:, 512 * hb:512 * hb + 512]))
                ch.sync()
                ch.did(dve.bn_aggr(mv[:, i, :], st[:, i, :, :].rearrange("p a b -> p (a b)")))

            dve.wait_ge(pe_pro, 1)
            dve.tensor_copy(pcol[:, :], COL[:, 0:64]).then_inc(dve_pro, 1)
            dve.wait_ge(s_x, 32)
            for i in range(TILES):
                stats(xin[:, i, :], i)
            rstd(0, TILES)
            for i in range(TILES):
                dve.tensor_scalar(xin[:, i, :], xin[:, i, :], mv[:, i, 0:1], rs[:, 2, i:i + 1],
                                  ALU.subtract, ALU.mult).then_inc(dve_n, 1)
            dve.wait_ge(pe_pro, 2)
            for hb in range(2):
                x = dve.tensor_copy(ws_t[:, 4 * hb:4 * hb + 4, :], MX[hb][:, :].rearrange("p (k n) -> p k n", k=4))
            x.then_inc(dve_pro, 1)
            dve.wait_ge(s_bmod, 128)

            def mod_rows(g, done):
                dve.wait_ge(pe_mod, 8 * (g + 1))
                for j in range(4):
                    rows = modrow[32 * j:32 * j + 2, g, :]
                    x = dve.tensor_tensor(rows, MOD[32 * j:32 * j + 2, :], rows, ALU.add)
                    if g == 0 or j == 3:
                        x.then_inc(done, 1)

            def mod_cols(g, tiles):
                cols = mod_t[:, :, :, :].rearrange("p v k r -> p (v k r)")
                for j in range(tiles):
                    dve.wait_ge(pe_modcol, 4 * g + j + 1)
                    x = dve.tensor_copy(cols[:, 32 * g + 8 * j:32 * g + 8 * j + 8], COLS[j][:, 8 * j:8 * j + 8])
                x.then_inc(dve_col, 1)

            def split_lo(b):
                u = b // 4
                par = b % 2
                dve.wait_ge(act_whi, b + 1)
                dve.tensor_tensor(w_lo[par][:, :, :], raw[:, u % 2, :, 128 * (b % 4):128 * (b % 4) + 128],
                                  w_hi[par][:, :, :].bitcast(f32), ALU.subtract).then_inc(dve_wlo, 1)

            mod_rows(0, dve_row0)
            dve.wait_ge(act_nt, 8)
            mod_cols(0, 4)
            dve.wait_ge(dve_col, 1)
            dve.tensor_scalar(scale1p[:, :, :].rearrange("p k r -> p (k r)"),
                              mod_t[:, 1, :, :].rearrange("p k r -> p (k r)"), 1.0, None, ALU.add).then_inc(dve_aff, 1)
            dve.wait_ge(dve_aff, 1)
            split_lo(0)

            def h_low(kc):
                dve.tensor_tensor(h_lo[:, kc, :], n_t[:, kc, :], h_hi[:, kc, :].bitcast(f32), ALU.subtract).then_inc(dve_hlo, 1)

            for kc in range(KC):
                dve.wait_ge(act_hhi, kc + 1)
                if kc:
                    dve.wait_ge(dve_aff, kc + 1)
                for r in range(REQ):
                    part = n_t[:, kc, SEQ * r:SEQ * r + SEQ]
                    x = dve.tensor_scalar(part, part, scale1p[:, kc, r:r + 1], mod_t[:, 0, kc, r:r + 1], ALU.mult, ALU.add)
                x.then_inc(dve_aff, 1)
                if kc:
                    h_low(kc - 1)
            dve.wait_ge(dve_aff, KC + 1)
            h_low(KC - 1)

            def v_rows(n):
                dve.wait_ge(pe_tr, n + 1)
                dve.tensor_copy(v_nat[:, :, 128 * n:128 * n + 128],
                                TR[n % 2][:, :].rearrange("p (c n) -> p c n", c=TILES)).then_inc(dve_tr, 1)

            for n in range(8):
                split_lo(n + 1)
                if n:
                    v_rows(n - 1)
            mod_rows(1, dve_row)

            def centred(n):
                g = n // 2
                w = WINDOWS[g]
                dve.wait_ge(pool_win, n + 1)
                dve.wait_ge(act_z, 8 + n + 1)
                if n >= 2:
                    dve.wait_ge(dve_dlo, n - 1)
                dve.scalar_tensor_tensor(out=d32[n % 2][:, :].rearrange("p (r s) -> p r s", r=REQ),
                                         in0=wsum[(g + 1) % 2][:, :, 8 - w // 2:8 - w // 2 + SEQ], scalar=1.0 / w,
                                         in1=zpad[n % 2][:, :, 8:8 + SEQ], op0=ALU.mult, op1=ALU.subtract).then_inc(dve_d, 1)

            def d_low(n):
                dve.wait_ge(act_dhi, n + 1)
                dve.tensor_tensor(d_lo[:, n % 2, :], d32[n % 2][:, :], d_hi[:, n % 2, :].bitcast(f32), ALU.subtract).then_inc(dve_dlo, 1)

            def pool_w_low(g):
                dve.wait_ge(act_wphi, g + 1)
                dve.tensor_tensor(wp_lo[:, :, :], wp_raw[:, g, :, :], wp_hi[:, :, :].bitcast(f32), ALU.subtract).then_inc(dve_wplo, 1)

            def pool_low(g):
                for o in range(2):
                    dve.wait_ge(act_phi, 2 * g + o + 1)
                    dve.tensor_tensor(a_lo[:, 2 * g + o, :], g32[o][:, :], a_hi[:, 2 * g + o, :].bitcast(f32),
                                      ALU.subtract).then_inc(dve_plo, 1)

            def pool_steps(n):
                if n >= 2:
                    d_low(n - 2)
                if n >= 5 and n % 2 == 1:
                    pool_low((n - 5) // 2)
                if 1 <= n <= 8:
                    centred(n - 1)

            for n in range(8):
                split_lo(9 + n)
                if n == 0:
                    v_rows(7)
                if n == 2:
                    pool_w_low(0)
                if n >= 5 and n % 2 == 1:
                    pool_w_low(n // 2 - 1)
                pool_steps(n)
            def v_norm(i):
                row = v_nat[:, i, :]
                link(dve.scalar_tensor_tensor(out=row, in0=row, scalar=mv[:, i, 0:1], in1=sgu_bc[:, 0, :], op0=ALU.subtract, op1=ALU.mult))
                dve.scalar_tensor_tensor(out=row, in0=row, scalar=rs[:, 2, i:i + 1], in1=sgu_bc[:, 1, :],
                                         op0=ALU.mult, op1=ALU.add).then_inc(dve_vln, 1)

            for n in range(8):
                split_lo(17 + n)
                if n == 0:
                    pool_steps(8)
                if n == 1:
                    pool_w_low(3)
                    pool_steps(9)
                if n == 2:
                    mod_rows(2, dve_row)
                if n == 5:
                    pool_low(3)
                if n == 3:
                    dve.wait_ge(dve_row, 2)
                    for j in range(2):
                        rows = modrow[32 * j:32 * j + 2, 2, :]
                        x = dve.tensor_scalar(rows, rows, 1.0, None, ALU.add)
                    x.then_inc(dve_row, 1)
                if n in (4, 5):
                    if n == 4:
                        dve.wait_ge(dve_tr, 8)
                    stats(v_nat[:, 2 * n - 8, :], 2 * n - 8)
                    stats(v_nat[:, 2 * n - 7, :], 2 * n - 7)
                if n == 5:
                    mod_cols(1, 2)
                if n == 6:
                    rstd(0, TILES)
                    dve.wait_ge(s_sgu, 32)
                if n == 7:
                    v_norm(0)
            for n in range(8):
                b = 24 + n
                split_lo(b + 1)
                dve.wait_ge(pe_blk, b + 1)
                dve.wait_ge(act_z, 16 + n + 1)
                dve.tensor_tensor(m_b[:, n, :], Z[n % 2][:, :], m_b[:, n, :], ALU.mult).then_inc(dve_z, 1)
                if n < TILES - 1:
                    v_norm(n + 1)
            dve.wait_ge(s_bs, 16)

            def a_low(n):
                dve.wait_ge(act_ahi, n + 1)
                dve.tensor_tensor(a_lo[:, n, :], d32[n % 2][:, :], a_hi[:, n, :].bitcast(f32), ALU.subtract).then_inc(dve_alo, 1)

            for n in range(8):
                b = 32 + n
                split_lo(b + 1)
                if n:
                    a_low(n - 1)
                dve.wait_ge(pe_mix, n + 1)
                if n >= 2:
                    dve.wait_ge(dve_alo, n - 1)
                bias = bs_bc[:, n:n + 1, :].broadcast_to([128, TILES, 128])
                out = d32[n % 2][:, :].rearrange("p (c n) -> p c n", c=TILES)
                link(dve.tensor_tensor(out, MX[n % 2][:, :].rearrange("p (c n) -> p c n", c=TILES), bias, ALU.add))
                dve.wait_ge(act_z, 24 + n + 1)
                dve.tensor_tensor(d32[n % 2][:, :], d32[n % 2][:, :], g32[n % 2][:, :], ALU.mult).then_inc(dve_a, 1)
            for n in range(8):
                split_lo(41 + n)
                if n == 0:
                    a_low(7)
            dve.wait_ge(dve_alo, 8)
            for n in range(8):
                b = 48 + n
                split_lo(b + 1)
                dve.wait_ge(pe_blk, b + 1)
                dve.wait_ge(act_z, 32 + n + 1)
                if n >= 2:
                    dve.wait_ge(dve_mlo, n - 1)
                dve.tensor_tensor(g_a[:, n, :], Z[n % 2][:, :], g_a[:, n, :], ALU.mult).then_inc(dve_z, 1)
                dve.wait_ge(dve_z, 8 + n + 1)
                dve.tensor_tensor(d32[n % 2][:, :], g_a[:, n, :], m_b[:, n, :], ALU.add).then_inc(dve_m, 1)
                dve.wait_ge(act_mhi, n + 1)
                dve.tensor_tensor(h_lo[:, n, :], d32[n % 2][:, :], h_hi[:, n, :].bitcast(f32), ALU.subtract).then_inc(dve_mlo, 1)
            def block_stats(n):
                dve.wait_ge(dve_tr, 8 + n + 1)
                for i in range(TILES):
                    ch.did(dve.bn_stats(st8[:, i, n, :], res[:, i, 128 * n:128 * n + 128]))

            dve.wait_ge(s_xres, 32)
            def residual(n):
                dve.wait_ge(pe_tr, 8 + n + 1)
                part = res[:, :, 128 * n:128 * n + 128]
                dve.scalar_tensor_tensor(out=part, in0=part, scalar=ALPHA, in1=TR[n % 2][:, :].rearrange("p (c n) -> p c n", c=TILES),
                                         op0=ALU.mult, op1=ALU.add).then_inc(dve_tr, 1)

            for n in range(8):
                if n < 7:
                    split_lo(57 + n)
                if n >= 2:
                    block_stats(n - 2)
                if n:
                    residual(n - 1)
            residual(7)
            block_stats(6)
            block_stats(KC - 1)
            ch.sync()
            for i in range(TILES):
                ch.did(dve.bn_aggr(mv[:, i, :], st8[:, i, :, :].rearrange("p a b -> p (a b)")))
            rstd(0, TILES)
            ch.sync()
            dve.wait_ge(s_ln1, 32)

            def gain1(i):
                row = res[:, i, :]
                return ch.did(dve.scalar_tensor_tensor(out=row, in0=row, scalar=mv[:, i, 0:1], in1=ln1_bc[:, 0, :],
                                                       op0=ALU.subtract, op1=ALU.mult))

            def bias1(i, gained):
                row = res[:, i, :]
                dve.wait_ge(dve_c, gained)
                return ch.did(dve.scalar_tensor_tensor(out=row, in0=row, scalar=rs[:, 2, i:i + 1], in1=ln1_bc[:, 1, :],
                                                       op0=ALU.mult, op1=ALU.add))

            def variance2(i, biased):
                dve.wait_ge(dve_c, biased)
                for hb in range(2):
                    read = ch.did(dve.bn_stats(st[:, i, hb, :], res[:, i, 512 * hb:512 * hb + 512]))
                dve.wait_ge(dve_c, read)
                aggregated = ch.did(dve.bn_aggr(mv2[:, i, :], st[:, i, :, :].rearrange("p a b -> p (a b)")))
                dve.wait_ge(dve_c, aggregated)
                dve.tensor_scalar(rs[:, 5, i:i + 1], mv2[:, i, 1:2], EPS, None, ALU.add).then_inc(dve_st, 1)

            variance2(0, bias1(0, gain1(0)))
            for i in range(TILES):
                more = i + 1 < TILES
                var, root, tmp, inv = (rs[:, k, i:i + 1] for k in (5, 6, 3, 7))
                if more:
                    gained = gain1(i + 1)
                dve.wait_ge(act_sq, 4 + i)
                inverted = ch.did(dve.reciprocal(inv, root))
                if more:
                    biased = bias1(i + 1, gained)
                dve.wait_ge(dve_c, inverted)
                link(dve.tensor_tensor(tmp, inv, inv, ALU.mult))
                link(dve.tensor_tensor(tmp, tmp, var, ALU.mult))
                corrected = ch.did(dve.tensor_scalar(tmp, tmp, -0.5, 1.5, ALU.mult, ALU.add))
                if more:
                    variance2(i + 1, biased)
                dve.wait_ge(dve_c, corrected)
                inverted = ch.did(dve.tensor_tensor(inv, inv, tmp, ALU.mult))
                if i == 0:
                    dve.wait_ge(pe_bc, 2)
                halves = [slice(512 * c, 512 * c + 512) for c in range(2)]
                scaled = []
                for c, part in enumerate(halves):
                    scaled.append(ch.did(dve.scalar_tensor_tensor(out=h2[:, i, part], in0=res[:, i, part], scalar=mv2[:, i, 0:1],
                                                                  in1=B[4 + c][:, :], op0=ALU.subtract, op1=ALU.mult)))
                dve.wait_ge(dve_c, inverted)
                for c, part in enumerate(halves):
                    dve.wait_ge(dve_c, scaled[c])
                    x = dve.scalar_tensor_tensor(out=h2[:, i, part], in0=h2[:, i, part], scalar=inv, in1=B[6 + c][:, :],
                                                 op0=ALU.mult, op1=ALU.add)
                x.then_inc(dve_h2, 1)
            ch.sync()
            ch.did(dve.tensor_copy(slots[:, 0:NEXP], cst[:, C_IOTA:C_IOTA + NEXP]))
            ch.did(dve.tensor_scalar(slots[:, NEXP:CAP], cst[:, C_IOTA:C_IOTA + NEXP], float(NEXP), None, ALU.add))
            dve.wait_ge(pe_lg, TILES)
            NL = NGRP + NEXP
            link(dve.tensor_tensor(lg[:, :, :], B[0][:, 0:256].rearrange("p (i n) -> p i n", i=TILES)[:, :, 0:NL],
                                   br_bc[:, :].rearrange("p (a n) -> p a n", a=1).broadcast_to([128, TILES, NL]), ALU.add))

            def iota(w):
                return cst[:, C_IOTA:C_IOTA + w].rearrange("p (a n) -> p a n", a=1).broadcast_to([128, TILES, w])

            def col(k, w):
                return q1[:, k, :].rearrange("p (i a) -> p i a", a=1).broadcast_to([128, TILES, w])

            def first_max(src, w, kmax, kidx, tmp, out):
                link(dve.tensor_reduce(q1[:, kmax, :], src, AX.X, ALU.max))
                link(dve.tensor_tensor(tmp, src, col(kmax, w), ALU.is_equal))
                link(dve.scalar_tensor_tensor(out=tmp, in0=tmp, scalar=-64.0, in1=iota(w), op0=ALU.mult, op1=ALU.add))
                link(dve.tensor_reduce(q1[:, kidx, :], tmp, AX.X, ALU.min))
                link(dve.tensor_tensor(out, tmp, col(kidx, w), ALU.is_equal))

            link(dve.memset(both[:, 0, :], 0.0))
            link(dve.tensor_copy(before_m[:, :, :].rearrange("p a n -> p (a n)"), cst[:, C_LT:C_LT + 256]))
            lgg = lg[:, :, 0:NGRP]
            oh_g = q[1][:, :, 0:NGRP]
            first_max(lgg, NGRP, 0, 1, q[0][:, :, 0:NGRP], oh_g)
            dve.tensor_tensor(q1[:, 6:10, :].rearrange("p g i -> p i g"), lgg, col(0, NGRP), ALU.subtract).then_inc(dve_st, 1)
            link(dve.tensor_tensor(seltmp[:, :, :, :], lg[:, :, NGRP:].rearrange("p i (g e) -> p i g e", g=NGRP),
                                   oh_g.rearrange("p i (g a) -> p i g a", a=1).broadcast_to([128, TILES, NGRP, EPG]), ALU.mult))
            link(dve.tensor_reduce(q[2][:, :, :], seltmp[:, :, :, :].rearrange("p i g e -> p i e g"), AX.X, ALU.add))
            first_max(q[2][:, :, :], EPG, 10, 1, q[3][:, :, :], q[4][:, :, :])
            link(dve.scalar_tensor_tensor(out=q[5][:, :, :], in0=q[4][:, :, :], scalar=BIG, in1=q[2][:, :, :], op0=ALU.mult, op1=ALU.add))
            first_max(q[5][:, :, :], EPG, 13, 1, q[3][:, :, :], q[6][:, :, :])
            dve.tensor_tensor(q1[:, 11, :], q1[:, 13, :], q1[:, 10, :], ALU.subtract).then_inc(dve_st, 1)
            for j, oh in enumerate((q[4], q[6])):
                for i in range(TILES):
                    ch.did(dve.tensor_tensor(
                        onehot[:, j, i, :].rearrange("p (g e) -> p g e", g=NGRP),
                        q[1][:, i, 0:NGRP].rearrange("p (g a) -> p g a", a=1).broadcast_to([128, NGRP, EPG]),
                        oh[:, i, :].rearrange("p (a e) -> p a e", a=1).broadcast_to([128, NGRP, EPG]), ALU.mult))
            ch.sync()
            dve.tensor_tensor(both[:, 1:, :], onehot[:, 0, :, :], onehot[:, 1, :, :], ALU.add).then_inc(dve_rt, 1)
            dve.wait_ge(pe_lg, TILES + 1)
            totals = B[1][:, NEXP * TILES:NEXP * TILES + NEXP]
            cum, start = seltmp[:, 0, :, :].rearrange("p a b -> p (a b)"), seltmp[:, 1, :, :].rearrange("p a b -> p (a b)")
            cnt = seltmp[:, 2, :, :].rearrange("p a b -> p (a b)")
            link(dve.tensor_copy(cnt, totals))
            link(dve.tensor_tensor_scan(cum, ones[:, 0:NEXP], cnt, 0.0, ALU.mult, ALU.add))
            link(dve.tensor_tensor(start, cum, cnt, ALU.subtract))
            link(dve.tensor_tensor(place[:, :, :], B[1][:, 0:NEXP * TILES].rearrange("p (i n) -> p i n", i=TILES),
                                   start.rearrange("p (a n) -> p a n", a=1).broadcast_to([128, TILES, NEXP]), ALU.add))
            for j in range(2):
                link(dve.tensor_tensor(prod[:, :, :], onehot[:, j, :, :], place[:, :, :], ALU.mult))
                link(dve.tensor_reduce(q1[:, j, :], prod[:, :, :], AX.X, ALU.add))
                x = dve.tensor_copy(pos[:, j, :], q1[:, j, :])
                if j == 0:
                    link(x)
            x.then_inc(dve_rt, 1)
            for j in range(2):
                ch.did(dve.tensor_tensor(sel[j][:, :, :], slots[:, :].rearrange("p (a n) -> p a n", a=1).broadcast_to([128, TILES, CAP]),
                                         q1[:, j, :].rearrange("p (i a) -> p i a", a=1).broadcast_to([128, TILES, CAP]), ALU.is_equal))
            ch.sync()
            dve.tensor_tensor(sel[0][:, :, :], sel[0][:, :, :], sel[1][:, :, :], ALU.add).then_inc(dve_sel, 1)
            dve.wait_ge(act_rt, 2 * TILES + 1)
            link(dve.tensor_reduce(q1[:, 14, :], q1[:, 2:6, :].rearrange("p g i -> p i g"), AX.X, ALU.add))
            dve.wait_ge(act_rt, 2 * TILES + 2)
            link(dve.tensor_scalar(q1[:, 15, :], q1[:, 12, :], 1.0, None, ALU.add))
            link(dve.tensor_tensor(q1[:, 14, :], q1[:, 14, :], q1[:, 15, :], ALU.mult))
            link(dve.reciprocal(route_w[:, 0, :], q1[:, 14, :]))
            link(dve.tensor_tensor(route_w[:, 1, :], route_w[:, 0, :], q1[:, 12, :], ALU.mult))
            further, upto, earlier = rounds[:, 0, :], rounds[:, 1, :], rounds[:, 2, :]
            link(dve.tensor_copy(tab[0:1, 0, 0:NEXP], start[0:1, :]))
            link(dve.tensor_scalar(further, cnt, float(CAP), None, ALU.is_gt))
            for k in range(2, TOK // CAP):
                link(dve.scalar_tensor_tensor(out=further, in0=cnt, scalar=float(CAP * k), in1=further, op0=ALU.is_gt, op1=ALU.add))
            link(dve.tensor_copy(tab[0:1, 1, 0:NEXP], further[0:1, :]))
            link(dve.tensor_tensor_scan(upto, ones[:, 0:NEXP], further, 0.0, ALU.mult, ALU.add))
            link(dve.tensor_tensor(earlier, upto, further, ALU.subtract))
            link(dve.tensor_copy(tab[0:1, 2, 0:NEXP], earlier[0:1, :]))
            link(dve.tensor_copy(tab[0:1, 2, NEXP:NEXP + 1], upto[0:1, NEXP - 1:NEXP]))
            link(dve.tensor_scalar(rounds[:, 3, :], further, 0.0, None, ALU.is_gt))
            link(dve.tensor_tensor_scan(rounds[:, 4, :], ones[:, 0:NEXP], rounds[:, 3, :], 0.0, ALU.mult, ALU.add))
            link(dve.tensor_tensor(rounds[:, 3, :], rounds[:, 4, :], rounds[:, 3, :], ALU.subtract))
            link(dve.tensor_tensor(rounds[:, 4, :], earlier, rounds[:, 3, :], ALU.subtract))
            link(dve.tensor_copy(tab[0:1, 3:5, 0:NEXP], rounds[0:1, 3:5, :]))
            link(dve.tensor_scalar(few[:, :], cnt[0:1, :], CAP / 2, None, ALU.is_le))
            link(dve.tensor_tensor(earlier, earlier, cst[:, C_IOTA:C_IOTA + NEXP], ALU.add))
            link(dve.tensor_scalar(earlier, earlier, float(CAP), None, ALU.mult))
            link(dve.tensor_tensor(place[:, :, :], B[1][:, 0:NEXP * TILES].rearrange("p (i n) -> p i n", i=TILES),
                                   earlier.rearrange("p (a n) -> p a n", a=1).broadcast_to([128, TILES, NEXP]), ALU.add))
            for j in range(2):
                link(dve.tensor_tensor(prod[:, :, :], onehot[:, j, :, :], place[:, :, :], ALU.mult))
                link(dve.tensor_reduce(q1[:, j, :], prod[:, :, :], AX.X, ALU.add))
                x = dve.tensor_copy(pos_y[:, j, :], q1[:, j, :])
                if j == 0:
                    link(x)
            x.then_inc(dve_rt, 1)
            dve.wait_ge(dve_rt, 3)
            dve.wait_ge(m_sem["xtr"], 1)
            dve.tensor_copy(x_t[0][:, :, :].rearrange("p k c -> p (k c)"), B[2][:, :]).then_inc(m_sem["xt"], 1)
            dve.wait_ge(s_scat, 16 * 8)

            def expert(e, s, last=False):
                dve.wait_ge(m_sem["silu"], e + 1)
                dve.tensor_tensor(hid[:, :], B[0][CAP:128, :], sg[:, :], ALU.mult).then_inc(m_sem["hid"], 1)
                if not last:
                    dve.wait_ge(m_sem["xtr"], e + 2)
                    dve.tensor_copy(x_t[(s + 1) % 3][:, :, :].rearrange("p k c -> p (k c)"), B[2][:, :]).then_inc(m_sem["xt"], 1)
                more = dve.value_load(tab[0:1, 1, bass.ds(e, 1)], min_val=0, max_val=7)
                first = dve.value_load(tab[0:1, 2, bass.ds(e, 1)], min_val=0, max_val=16)
                with dve.If(more > 0):
                    with dve.Fori(0, more) as r:
                        turns = dve.snap(first + r)
                        dve.wait_ge(x_sem["xtr"], turns + 2)
                        dve.tensor_copy(x_t_x[:, :, :].rearrange("p k c -> p (k c)"), B[6][:, :]).then_inc(x_sem["xt"], 1)
                        dve.wait_ge(x_sem["silu"], turns + 1)
                        dve.tensor_tensor(hid_x[:, :], B[4][CAP:128, :], sg_x[:, :], ALU.mult).then_inc(x_sem["hid"], 1)

            with dve.Fori(0, 10) as t:
                for k in range(3):
                    expert(3 * t + k, k)
            expert(30, 0)
            expert(31, 1, last=True)
            dve.wait_ge(pe_bc, 3)
            dve.wait_ge(s_ln2, 32)
            dve.wait_ge(act_res, 1)

            def gated(i):
                y = y_first[i]
                if i == 0:
                    dve.wait_ge(f_t, 1)
                    link(dve.scalar_tensor_tensor(out=y[:, :], in0=y[:, :], scalar=route_w[:, 0, i:i + 1], in1=y_second[i][:, :],
                                                  op0=ALU.mult, op1=ALU.add))
                else:
                    dve.wait_ge(f_c, i)
                for c, bank in enumerate((B[0], B[2])):
                    part = y[:, 512 * c:512 * c + 512]
                    done = ch.did(dve.tensor_tensor(part, bank[:, :], part, ALU.mult))
                return done

            def with_residual(i, behind):
                dve.wait_ge(dve_c, behind)
                return ch.did(dve.tensor_tensor(y_first[i][:, :], res[:, i, :], y_first[i][:, :], ALU.add))

            def statistics(i, behind):
                dve.wait_ge(dve_c, behind)
                for hb in range(2):
                    done = ch.did(dve.bn_stats(st[:, i, hb, :], y_first[i][:, 512 * hb:512 * hb + 512]))
                return done

            def aggregate(i, behind):
                dve.wait_ge(dve_c, behind)
                return ch.did(dve.bn_aggr(mv[:, i, :], st[:, i, :, :].rearrange("p a b -> p (a b)")))

            def variance(c, behind):
                dve.wait_ge(dve_c, behind)
                dve.tensor_scalar(rs[:, 0, c], mv[:, c, 1], EPS, None, ALU.add).then_inc(dve_st, 1)

            def reciprocal_root(c, roots):
                dve.wait_ge(act_sq, roots)
                return ch.did(dve.reciprocal(rs[:, 2, c], rs[:, 1, c]))

            def newton(c, behind):
                dve.wait_ge(dve_c, behind)
                link(dve.tensor_tensor(rs[:, 3, c], rs[:, 2, c], rs[:, 2, c], ALU.mult))
                return ch.did(dve.tensor_tensor(rs[:, 3, c], rs[:, 3, c], rs[:, 0, c], ALU.mult))

            def newton_end(c, behind):
                dve.wait_ge(dve_c, behind)
                link(dve.tensor_scalar(rs[:, 3, c], rs[:, 3, c], -0.5, 1.5, ALU.mult, ALU.add))
                link(dve.tensor_tensor(rs[:, 2, c], rs[:, 2, c], rs[:, 3, c], ALU.mult))

            def gain(i):
                dve.wait_ge(act_f, i + 1)
                dve.tensor_tensor(y_first[i][:, :], y_first[i][:, :], ln2_bc[:, 0, :], ALU.mult).then_inc(f_m, 1)

            roots = sq[0] + TILES
            ch.sync()
            for i in range(2):
                seen = aggregate(i, statistics(i, with_residual(i, gated(i))))
            pair = slice(0, 2)
            variance(pair, seen)
            y2 = gated(2)
            inverted = reciprocal_root(pair, roots + 1)
            y2 = with_residual(2, y2)
            squared = newton(pair, inverted)
            y2 = statistics(2, y2)
            newton_end(pair, squared)
            for i in range(2):
                x = dve.scalar_tensor_tensor(out=rs[:, 4, i:i + 1], in0=mv[:, i, 0:1], scalar=-1.0, in1=rs[:, 2, i:i + 1],
                                             op0=ALU.mult, op1=ALU.mult)
            x.then_inc(dve_nb, 1)
            aggregate(2, y2)
            seen = aggregate(3, statistics(3, with_residual(3, gated(3))))
            pair = slice(2, 4)
            variance(pair, seen)
            gain(0)
            inverted = reciprocal_root(pair, roots + 2)
            gain(1)
            newton_end(pair, newton(pair, inverted))
            gained = [ch.did(dve.scalar_tensor_tensor(out=y_first[i][:, :], in0=y_first[i][:, :], scalar=mv[:, i, 0:1],
                                                      in1=ln2_bc[:, 0, :], op0=ALU.subtract, op1=ALU.mult)) for i in (2, 3)]
            for i in (2, 3):
                dve.wait_ge(dve_c, gained[i - 2])
                dve.scalar_tensor_tensor(out=y_first[i][:, :], in0=y_first[i][:, :], scalar=rs[:, 2, i:i + 1], in1=ln2_bc[:, 1, :],
                                         op0=ALU.mult, op1=ALU.add).then_inc(f_o, 1)


_INS = ["x_prompt", "x_sample", "c_prompt", "c_sample", "w_mod", "b_mod", "w_in", "b_in", "w_spatial",
        "b_spatial", "sgu_g", "sgu_b", "w_pool", "pool_scale", "w_branch_a", "w_branch_b", "w_out",
        "ln1_g", "ln1_b", "w_router_group", "b_router_group", "w_router_expert", "b_router_expert",
        "w_exp_gate", "w_exp_up", "w_exp_down", "ln2_g", "ln2_b"]


def constants():
    import numpy as np

    c = np.zeros((128, C_END), np.float32)
    c[:, C_ID:C_ID + 128] = np.eye(128)
    c[:, C_LT:C_LT + 128] = np.triu(np.ones((128, 128)), 1)
    c[:, C_ONE:C_ONE + 128] = 1.0
    for j in range(4):
        for r in range(REQ):
            c[32 * j + r, C_SEL + 64 * r:C_SEL + 64 * r + 64] = 1.0
    for g, w in enumerate(WINDOWS):
        h = w // 2
        for k in range(h):
            c[:, C_EDGE + 16 * g + k] = w / (k + h)
        for k in range(h - 1):
            c[:, C_EDGE + 16 * g + 8 + k] = w / (SEQ - (SEQ - h + 1 + k) + h)
    c[:, C_IOTA:C_IOTA + NEXP] = np.arange(NEXP)
    return c


def kernel(**inputs):
    import numpy as _np
    import concourse.bacc as _bacc
    from concourse import mybir as _mybir
    from concourse.bass_utils import run_bass_kernel_spmd as _run

    nc = _bacc.Bacc("TRN2", target_bir_lowering=False, num_devices=1)
    arrays, args = {}, []
    for name in _INS:
        a = _np.ascontiguousarray(inputs[name])
        arrays[f"in_{name}"] = a
        args.append(nc.dram_tensor(f"in_{name}", a.shape, _mybir.dt.from_np(a.dtype), kind="ExternalInput").ap())
    arrays["in_consts"] = constants()
    args.append(nc.dram_tensor("in_consts", (128, C_END), _mybir.dt.float32, kind="ExternalInput").ap())
    for i in range(REQ):
        args.append(nc.dram_tensor(f"out_{i}", (1, SEQ, D), _mybir.dt.float32, kind="ExternalOutput").ap())
    hybrid_encoder(nc, *args)
    r = _run(nc, [arrays], core_ids=[0])
    return tuple(r.results[0][f"out_{i}"] for i in range(REQ))
```
